# Optimizing a Trainium2 kernel written in Bass

```python
import math
import jax, jax.numpy as jnp
from jax import lax
import numpy as np

D_MODEL = 1024
BATCH = 1
SEQ = 256
DEPTH = 2

N_MIXERS = 2
N_GLA_LAYERS = (DEPTH + 1) // 2
N_SB_LAYERS = DEPTH // 2
D_FF = 2816
EPS = 1e-6

GLA_HEADS = 4
GLA_DK = D_MODEL // 2
GLA_DV = D_MODEL
GLA_HK = GLA_DK // GLA_HEADS
GLA_HV = GLA_DV // GLA_HEADS
GLA_GATE_RANK = 16
GLA_GATE_TAU = 16.0
GLA_CHUNK = 64
GLA_IN_COLS = GLA_DK + GLA_DK + GLA_DV + GLA_DV + GLA_GATE_RANK

SB_HEADS = 16
SB_HD = D_MODEL // SB_HEADS
SB_QBLOCK = 128
SB_IN_COLS = 3 * D_MODEL


def rmsnorm(x, g):
    xf = x.astype(jnp.float32)
    y = xf * lax.rsqrt(jnp.mean(xf * xf, axis=-1, keepdims=True) + EPS)
    return (y * g.astype(jnp.float32)).astype(x.dtype)

def swiglu(h, w_gate, w_up, w_down):
    return (jax.nn.silu(h @ w_gate) * (h @ w_up)) @ w_down

def gla_mixer(h, w_in, w_gk2, b_gk, o_norm, w_out):
    B, S, _ = h.shape
    nc = S // GLA_CHUNK
    proj = h @ w_in
    q, k, v, g, gk_lr = jnp.split(
        proj, [GLA_DK, 2 * GLA_DK, 2 * GLA_DK + GLA_DV, 2 * GLA_DK + 2 * GLA_DV], axis=-1)
    log_a = jax.nn.log_sigmoid((gk_lr @ w_gk2 + b_gk).astype(jnp.float32)) / GLA_GATE_TAU

    def to_chunks(t, d):
        return t.astype(jnp.float32).reshape(B, nc, GLA_CHUNK, GLA_HEADS, d).transpose(1, 0, 3, 2, 4)

    qc = to_chunks(q, GLA_HK) * (GLA_HK ** -0.5)
    kc = to_chunks(k, GLA_HK)
    vc = to_chunks(v, GLA_HV)
    bc = jnp.cumsum(to_chunks(log_a, GLA_HK), axis=3)
    causal = jnp.tril(jnp.ones((GLA_CHUNK, GLA_CHUNK), dtype=bool))

    def step(state, inp):
        q_t, k_t, v_t, b_t = inp
        o_inter = jnp.einsum('bhtk,bhkv->bhtv', q_t * jnp.exp(b_t), state)
        diff = b_t[:, :, :, None, :] - b_t[:, :, None, :, :]
        decay = jnp.exp(jnp.where(causal[:, :, None], diff, -jnp.inf))
        scores = jnp.einsum('bhtk,bhtsk,bhsk->bhts', q_t, decay, k_t)
        o_intra = jnp.einsum('bhts,bhsv->bhtv', scores, v_t)
        b_last = b_t[:, :, -1, :]
        k_dec = k_t * jnp.exp(b_last[:, :, None, :] - b_t)
        state = jnp.exp(b_last)[..., None] * state + jnp.einsum('bhsk,bhsv->bhkv', k_dec, v_t)
        return state, o_inter + o_intra

    state0 = jnp.zeros((B, GLA_HEADS, GLA_HK, GLA_HV), jnp.float32)
    _, o = lax.scan(step, state0, (qc, kc, vc, bc))
    o = o.transpose(1, 0, 3, 2, 4).reshape(B, S, GLA_HEADS, GLA_HV)
    o = rmsnorm(o, o_norm).reshape(B, S, GLA_DV)
    o = o.astype(h.dtype) * jax.nn.silu(g)
    return o @ w_out

def sb_mixer(h, w_in, w_out):
    B, S, _ = h.shape
    nb = S // SB_QBLOCK
    q, k, v = jnp.split(h @ w_in, 3, axis=-1)

    def heads(t):
        return t.reshape(B, S, SB_HEADS, SB_HD).transpose(0, 2, 1, 3)

    q, k, v = heads(q), heads(k), heads(v)
    q_blocks = q.reshape(B, SB_HEADS, nb, SB_QBLOCK, SB_HD).transpose(2, 0, 1, 3, 4)
    s_pos = jnp.arange(S)
    scale = 1.0 / math.sqrt(SB_HD)

    def block(args):
        idx, q_blk = args
        z = jnp.einsum('bhtd,bhsd->bhts', q_blk, k).astype(jnp.float32) * scale
        t_pos = idx * SB_QBLOCK + jnp.arange(SB_QBLOCK)
        mask = s_pos[None, :] < t_pos[:, None]
        sp = jnp.where(mask, jax.nn.softplus(z), 0.0)
        rem = lax.cumsum(sp, axis=3, reverse=True) - sp
        weights = jnp.where(mask, jnp.exp(jax.nn.log_sigmoid(z) - rem), 0.0)
        return jnp.einsum('bhts,bhsd->bhtd', weights.astype(v.dtype), v)

    o = lax.map(block, (jnp.arange(nb), q_blocks))
    o = o.transpose(1, 0, 3, 2, 4).reshape(B, S, D_MODEL)
    return o @ w_out

def first_inputs(seed: int = 0) -> dict:
    key = jax.random.key(seed)
    ks = jax.random.split(key, 24)
    f32 = jnp.float32

    def nrm(k, shape, fan_in, gain=1.0):
        return jax.random.normal(k, shape, f32) * (gain * fan_in ** -0.5)

    def gain(k, shape):
        return 1.0 + 0.02 * jax.random.normal(k, shape, f32)

    return {
        "x": jax.random.normal(ks[0], (BATCH, SEQ, D_MODEL), f32),
        "ffn1_norm": gain(ks[1], (DEPTH, D_MODEL)),
        "ffn1_w_gate": nrm(ks[2], (DEPTH, D_MODEL, D_FF), D_MODEL),
        "ffn1_w_up": nrm(ks[3], (DEPTH, D_MODEL, D_FF), D_MODEL),
        "ffn1_w_down": nrm(ks[4], (DEPTH, D_FF, D_MODEL), D_FF),
        "mix_norm": gain(ks[5], (DEPTH, D_MODEL)),
        "ffn2_norm": gain(ks[6], (DEPTH, D_MODEL)),
        "ffn2_w_gate": nrm(ks[7], (DEPTH, D_MODEL, D_FF), D_MODEL),
        "ffn2_w_up": nrm(ks[8], (DEPTH, D_MODEL, D_FF), D_MODEL),
        "ffn2_w_down": nrm(ks[9], (DEPTH, D_FF, D_MODEL), D_FF),
        "gla_w_in": nrm(ks[10], (N_GLA_LAYERS, D_MODEL, GLA_IN_COLS), D_MODEL),
        "gla_w_gk2": nrm(ks[11], (N_GLA_LAYERS, GLA_GATE_RANK, GLA_DK), GLA_GATE_RANK),
        "gla_b_gk": 0.1 * jax.random.normal(ks[12], (N_GLA_LAYERS, GLA_DK), f32),
        "gla_o_norm": gain(ks[13], (N_GLA_LAYERS, GLA_HV)),
        "gla_w_out": nrm(ks[14], (N_GLA_LAYERS, GLA_DV, D_MODEL), GLA_DV),
        "sb_w_in": nrm(ks[15], (N_SB_LAYERS, D_MODEL, SB_IN_COLS), D_MODEL),
        "sb_w_out": nrm(ks[16], (N_SB_LAYERS, D_MODEL, D_MODEL), D_MODEL),
        "final_norm": gain(ks[17], (D_MODEL,)),
    }

def first_block(x, ffn1_norm, ffn1_w_gate, ffn1_w_up, ffn1_w_down, mix_norm,
              ffn2_norm, ffn2_w_gate, ffn2_w_up, ffn2_w_down,
              gla_w_in, gla_w_gk2, gla_b_gk, gla_o_norm, gla_w_out,
              sb_w_in, sb_w_out, final_norm):
    for i in range(DEPTH):
        x = x + 0.5 * swiglu(rmsnorm(x, ffn1_norm[i]), ffn1_w_gate[i], ffn1_w_up[i], ffn1_w_down[i])
        h = rmsnorm(x, mix_norm[i])
        j = i // N_MIXERS
        if i % N_MIXERS == 0:
            y = gla_mixer(h, gla_w_in[j], gla_w_gk2[j], gla_b_gk[j], gla_o_norm[j], gla_w_out[j])
        else:
            y = sb_mixer(h, sb_w_in[j], sb_w_out[j])
        x = x + y.astype(x.dtype)
        x = x + 0.5 * swiglu(rmsnorm(x, ffn2_norm[i]), ffn2_w_gate[i], ffn2_w_up[i], ffn2_w_down[i])
    return rmsnorm(x, final_norm)


DEPTH_2 = 1

D_MIX = D_MODEL
D_CONV = D_MIX // 2
D_ATTN = D_MIX - D_CONV
CONV_WIDTH = 3
CONV_GROUPS = 8
HEAD_DIM = 64
V_DIM = 2 * HEAD_DIM
N_HEADS = D_ATTN // V_DIM
Q_WIDTH = N_HEADS * 2 * HEAD_DIM
D_IN = 3 * D_CONV + 2 * Q_WIDTH + N_HEADS * V_DIM
Q_BLOCK = 128
N_EXPERT_GROUPS = 4
EXPERTS_PER_GROUP = 8
TOP_K = 2
D_EXPERT = D_MODEL // 2


def rms_norm(x, g):
    xf = x.astype(jnp.float32)
    y = xf * lax.rsqrt(jnp.mean(xf * xf, axis=-1, keepdims=True) + EPS)
    return (y * g.astype(jnp.float32)).astype(x.dtype)

def lambda_init(layer_idx):
    return 0.8 - 0.6 * math.exp(-0.3 * layer_idx)

def causal_depthwise_conv(u, w):
    K = w.shape[0]
    S = u.shape[1]
    up = jnp.pad(u, ((0, 0), (K - 1, 0), (0, 0)))
    y = up[:, 0:S, :] * w[0]
    for k in range(1, K):
        y = y + up[:, k:k + S, :] * w[k]
    return y

def short_conv_group(xc, b_gate, c_gate, conv_w, conv_out_g):
    y = b_gate * causal_depthwise_conv(c_gate * xc, conv_w)
    Bsz, S, _ = y.shape
    yg = y.reshape(Bsz, S, CONV_GROUPS, D_CONV // CONV_GROUPS)
    yg = rms_norm(yg, jnp.ones((D_CONV // CONV_GROUPS,), y.dtype))
    return yg.reshape(Bsz, S, D_CONV) * conv_out_g.astype(y.dtype)

def diff_attention_group(q, k, v, q_norm_g, k_norm_g, lq1, lk1, lq2, lk2, subln_g, lam_init):
    Bsz, S, _ = q.shape
    q = rms_norm(q.reshape(Bsz, S, N_HEADS, 2, HEAD_DIM), q_norm_g) * (HEAD_DIM ** -0.5)
    k = rms_norm(k.reshape(Bsz, S, N_HEADS, 2, HEAD_DIM), k_norm_g)
    v = v.reshape(Bsz, S, N_HEADS, V_DIM)
    qT = q.transpose(0, 2, 3, 1, 4)
    kT = k.transpose(0, 2, 3, 1, 4)
    vT = v.transpose(0, 2, 1, 3)
    lam = (jnp.exp(jnp.sum(lq1.astype(jnp.float32) * lk1.astype(jnp.float32)))
           - jnp.exp(jnp.sum(lq2.astype(jnp.float32) * lk2.astype(jnp.float32)))
           + lam_init)
    key_pos = jnp.arange(S)
    n_blocks = S // Q_BLOCK

    def one_block(i):
        start = i * Q_BLOCK
        qb = lax.dynamic_slice_in_dim(qT, start, Q_BLOCK, axis=3)
        s = jnp.einsum('bhcqd,bhckd->bhcqk', qb, kT).astype(jnp.float32)
        q_pos = start + jnp.arange(Q_BLOCK)
        mask = key_pos[None, :] <= q_pos[:, None]
        s = jnp.where(mask, s, -jnp.inf)
        p = jax.nn.softmax(s, axis=-1)
        a = (p[:, :, 0] - lam * p[:, :, 1]).astype(vT.dtype)
        return jnp.einsum('bhqk,bhkv->bqhv', a, vT)

    out = lax.map(one_block, jnp.arange(n_blocks))
    out = out.transpose(1, 0, 2, 3, 4).reshape(Bsz, S, N_HEADS, V_DIM)
    out = rms_norm(out, subln_g) * (1.0 - lam_init)
    return out.reshape(Bsz, S, D_ATTN)

def hierarchical_moe(h, w_router_group, w_router_expert, w_gate, w_up, w_down):
    T = h.shape[0]
    G, E = N_EXPERT_GROUPS, EXPERTS_PER_GROUP
    p_group = jax.nn.softmax(jnp.einsum('td,dg->tg', h, w_router_group).astype(jnp.float32), axis=-1)
    g_idx = jnp.argmax(p_group, axis=-1)
    g_gate = jnp.max(p_group, axis=-1)
    logits_e = jnp.einsum('td,de->te', h, w_router_expert).astype(jnp.float32).reshape(T, G, E)
    logits_sel = jnp.take_along_axis(logits_e, g_idx[:, None, None], axis=1)[:, 0]
    top_vals, top_idx = lax.top_k(logits_sel, TOP_K)
    top_w = jax.nn.softmax(top_vals, axis=-1)
    exp_w = jnp.sum(jax.nn.one_hot(top_idx, E, dtype=jnp.float32) * top_w[..., None], axis=1)
    comb = (jax.nn.one_hot(g_idx, G, dtype=jnp.float32)[:, :, None]
            * exp_w[:, None, :] * g_gate[:, None, None]).astype(h.dtype)
    y = jnp.zeros_like(h)
    for g in range(G):
        hg = jnp.einsum('td,edf->tef', h, w_gate[g])
        hu = jnp.einsum('td,edf->tef', h, w_up[g])
        act = jax.nn.silu(hg) * hu * comb[:, g, :, None]
        y = y + jnp.einsum('tef,efd->td', act, w_down[g])
    return y

def second_inputs(seed: int = 0) -> dict:
    key = jax.random.key(seed)
    ks = jax.random.split(key, 20)
    f32 = jnp.float32
    G, E, F = N_EXPERT_GROUPS, EXPERTS_PER_GROUP, D_EXPERT

    def nrm(k, shape, scale):
        return jax.random.normal(k, shape, f32) * scale

    return {
        "x": nrm(ks[0], (BATCH, SEQ, D_MODEL), 1.0),
        "attn_norm_g": 1.0 + nrm(ks[1], (DEPTH_2, D_MODEL), 0.02),
        "w_in": nrm(ks[2], (DEPTH_2, D_MODEL, D_IN), D_MODEL ** -0.5),
        "conv_w": nrm(ks[3], (DEPTH_2, CONV_WIDTH, D_CONV), CONV_WIDTH ** -0.5),
        "conv_out_g": 1.0 + nrm(ks[4], (DEPTH_2, D_CONV), 0.02),
        "q_norm_g": 1.0 + nrm(ks[5], (DEPTH_2, HEAD_DIM), 0.02),
        "k_norm_g": 1.0 + nrm(ks[6], (DEPTH_2, HEAD_DIM), 0.02),
        "lambda_q1": nrm(ks[7], (DEPTH_2, HEAD_DIM), 0.1),
        "lambda_k1": nrm(ks[8], (DEPTH_2, HEAD_DIM), 0.1),
        "lambda_q2": nrm(ks[9], (DEPTH_2, HEAD_DIM), 0.1),
        "lambda_k2": nrm(ks[10], (DEPTH_2, HEAD_DIM), 0.1),
        "attn_subln_g": 1.0 + nrm(ks[11], (DEPTH_2, V_DIM), 0.02),
        "w_out": nrm(ks[12], (DEPTH_2, D_MIX, D_MODEL), D_MIX ** -0.5),
        "ffn_norm_g": 1.0 + nrm(ks[13], (DEPTH_2, D_MODEL), 0.02),
        "w_router_group": nrm(ks[14], (DEPTH_2, D_MODEL, G), D_MODEL ** -0.5),
        "w_router_expert": nrm(ks[15], (DEPTH_2, D_MODEL, G * E), D_MODEL ** -0.5),
        "w_exp_gate": nrm(ks[16], (DEPTH_2, G, E, D_MODEL, F), D_MODEL ** -0.5),
        "w_exp_up": nrm(ks[17], (DEPTH_2, G, E, D_MODEL, F), D_MODEL ** -0.5),
        "w_exp_down": nrm(ks[18], (DEPTH_2, G, E, F, D_MODEL), F ** -0.5),
    }

def second_block(x, attn_norm_g, w_in, conv_w, conv_out_g, q_norm_g, k_norm_g,
              lambda_q1, lambda_k1, lambda_q2, lambda_k2, attn_subln_g, w_out,
              ffn_norm_g, w_router_group, w_router_expert, w_exp_gate, w_exp_up, w_exp_down):
    Bsz, S, D = x.shape
    split_points = [D_CONV, 2 * D_CONV, 3 * D_CONV,
                    3 * D_CONV + Q_WIDTH, 3 * D_CONV + 2 * Q_WIDTH]
    h = x
    for l in range(DEPTH_2):
        lam_init = lambda_init(l)
        hn = rms_norm(h, attn_norm_g[l])
        proj = jnp.einsum('bsd,de->bse', hn, w_in[l])
        xc, b_gate, c_gate, q, k, v = jnp.split(proj, split_points, axis=-1)
        y_conv = short_conv_group(xc, b_gate, c_gate, conv_w[l], conv_out_g[l])
        y_attn = diff_attention_group(q, k, v, q_norm_g[l], k_norm_g[l],
                                      lambda_q1[l], lambda_k1[l], lambda_q2[l], lambda_k2[l],
                                      attn_subln_g[l], lam_init)
        mix = jnp.concatenate([y_conv, y_attn], axis=-1)
        h = h + jnp.einsum('bse,ed->bsd', mix, w_out[l])
        hn2 = rms_norm(h, ffn_norm_g[l]).reshape(Bsz * S, D)
        y_ffn = hierarchical_moe(hn2, w_router_group[l], w_router_expert[l],
                                 w_exp_gate[l], w_exp_up[l], w_exp_down[l])
        h = h + y_ffn.reshape(Bsz, S, D)
    return h


def setup_inputs(seed=0):
    out = dict(first_inputs(seed))
    for name, value in second_inputs(seed + 1).items():
        if name != "x":
            out[name + "_2"] = value
    return out


def reference(
    x, ffn1_norm, ffn1_w_gate, ffn1_w_up, ffn1_w_down, mix_norm, ffn2_norm, ffn2_w_gate,
    ffn2_w_up, ffn2_w_down, gla_w_in, gla_w_gk2, gla_b_gk, gla_o_norm, gla_w_out, sb_w_in,
    sb_w_out, final_norm, attn_norm_g_2, w_in_2, conv_w_2, conv_out_g_2, q_norm_g_2, k_norm_g_2,
    lambda_q1_2, lambda_k1_2, lambda_q2_2, lambda_k2_2, attn_subln_g_2, w_out_2, ffn_norm_g_2,
    w_router_group_2, w_router_expert_2, w_exp_gate_2, w_exp_up_2, w_exp_down_2,
):
    x = first_block(
        x, ffn1_norm, ffn1_w_gate, ffn1_w_up, ffn1_w_down, mix_norm, ffn2_norm, ffn2_w_gate,
        ffn2_w_up, ffn2_w_down, gla_w_in, gla_w_gk2, gla_b_gk, gla_o_norm, gla_w_out, sb_w_in,
        sb_w_out, final_norm,
    )
    return second_block(
        x, attn_norm_g_2, w_in_2, conv_w_2, conv_out_g_2, q_norm_g_2, k_norm_g_2, lambda_q1_2,
        lambda_k1_2, lambda_q2_2, lambda_k2_2, attn_subln_g_2, w_out_2, ffn_norm_g_2,
        w_router_group_2, w_router_expert_2, w_exp_gate_2, w_exp_up_2, w_exp_down_2,
    )


_drawn_inputs = setup_inputs


def setup_inputs(seed=0):
    import zlib

    import numpy as np

    out = dict(_drawn_inputs(seed))
    spreads = {}
    factors = {'conv_out_g_2': 12.511,
     'q_norm_g_2': 4.094,
     'k_norm_g_2': 4.936,
     'lambda_k2_2': 3.907,
     'attn_subln_g_2': 13.408,
     'lambda_q1_2': 2.948,
     'ffn_norm_g_2': 5.352}
    for name, (base, spread) in spreads.items():
        noise = np.random.default_rng([zlib.crc32(name.encode()), seed]).standard_normal(out[name].shape)
        drawn = base * np.exp(spread * noise) if base else spread * noise
        out[name] = __import__('jax').numpy.asarray(drawn.astype(out[name].dtype))
    for name, factor in factors.items():
        out[name] = (out[name] * factor).astype(out[name].dtype)
    return out
```

```python
from contextlib import ExitStack

import numpy as np

import concourse.bass as bass
from concourse import mybir

F32 = mybir.dt.float32
F32R = mybir.dt.float32r
I32 = mybir.dt.int32
U32 = mybir.dt.uint32
ALU = mybir.AluOpType
ACT = mybir.ActivationFunctionType
AX = mybir.AxisListType.X

P = 128
TOKENS = 256
TT = TOKENS // P
D = 1024
KD = D // P
EPS = 1e-6
BANK = 512
SLOT = 2048
RING = 3

D_FF = 2816
CHUNK = 256
N_CHUNKS = D_FF // CHUNK
FFN_PIECES = 3 * N_CHUNKS
IN_CHUNKS = 6
IN_PIECES = 2 * IN_CHUNKS
OUT_PIECES = 4
HALF_D = 512

GLA_HEADS, GLA_K, GLA_V, GLA_RANK = 4, 128, 256, 16
GLA_TAU = 16.0
GLA_COLS = IN_CHUNKS * BANK + GLA_RANK
LEVELS = [64, 32, 16, 8, 4, 2, 1]

SB_HEADS, SB_HD = 16, 64
GROUP = 4
SB_GROUPS = SB_HEADS // GROUP

DA_HEADS, DA_HD, DA_V = 4, 64, 128
D_CONV = 512
CONV_W = 3
LAMBDA_INIT = 0.8 - 0.6 * float(np.exp(-0.3 * 0))
NEG = -1e30

GROUPS, PER_GROUP, EXPERTS = 4, 8, 32
D_EXP = 512
SLOTS = 64
MAX_OVER = 2 * TOKENS // (SLOTS + 1)
MAX_TILES = TOKENS // SLOTS
ITEMS = EXPERTS + MAX_OVER
ITEM_COLS = ITEMS + 1

FIRST_PIECE = {}
_at = 0
for _name, _n in [("ffn0", FFN_PIECES), ("gla_in", IN_PIECES), ("gla_out", OUT_PIECES), ("ffn1", FFN_PIECES),
                  ("ffn2", FFN_PIECES), ("sb_in", IN_PIECES), ("sb_out", OUT_PIECES), ("ffn3", FFN_PIECES),
                  ("mix_in", IN_PIECES), ("mix_out", OUT_PIECES), ("experts", 0)]:
    FIRST_PIECE[_name] = _at
    _at += _n

STOP = None


def build(nc, t, out):
    ctx = ExitStack()
    with ctx:
        def sb(name, shape, dt=F32):
            return ctx.enter_context(nc.sbuf_tensor(name, shape, dt))

        def sem(name):
            return ctx.enter_context(nc.semaphore(name))

        raw = sb("raw", [P, RING, SLOT])
        high = sb("high", [P, RING, SLOT], F32R)
        low = sb("low", [P, RING, SLOT], F32R)
        hT_high = sb("hT_high", [P, KD, TOKENS], F32R)
        hT_low = sb("hT_low", [P, KD, TOKENS], F32R)
        aT_high = sb("aT_high", [P, 2, TOKENS], F32R)
        aT_low = sb("aT_low", [P, 2, TOKENS], F32R)
        zero_r = sb("zero_r", [P, BANK], F32R)
        x = sb("x", [P, TT, D])
        h = sb("h", [P, TT, D])
        gate = sb("gate", [P, TT, CHUNK])
        act_tok = sb("act_tok", [P, TT, CHUNK])
        gain = sb("gain", [P, 2, D])
        square = sb("square", [P, D])
        proj = sb("proj", [P, TT, GLA_COLS])
        stat = sb("stat", [P, 64])
        eps = sb("eps", [P, 1])
        ident = sb("ident", [P, P])
        ones = sb("ones", [P, TOKENS])
        suffix = sb("suffix", [P, P])
        strict = sb("strict", [P, P])
        causal = sb("causal", [P, 3 * P])
        levels = sb("levels", [P, len(LEVELS), P])
        wgk2 = sb("wgk2", [GLA_RANK, GLA_HEADS * GLA_K])
        bgk = sb("bgk", [P, GLA_HEADS])
        gla_gain = sb("gla_gain", [P, GLA_V])
        gkw = sb("gkw", [P, KD, GLA_RANK])
        gkw_high = sb("gkw_high", [P, KD, GLA_RANK], F32R)
        gkw_low = sb("gkw_low", [P, KD, GLA_RANK], F32R)
        router = sb("router", [P, KD, GROUPS + EXPERTS])
        router_high = sb("router_high", [P, KD, GROUPS + EXPERTS], F32R)
        router_low = sb("router_low", [P, KD, GROUPS + EXPERTS], F32R)
        SCRATCH = 10752
        scratch = sb("scratch", [P, SCRATCH])

        class Area:

            def __init__(self):
                self.at = 0

            def take(self, n):
                self.at += n
                assert self.at <= SCRATCH, self.at
                return scratch[:, self.at - n:self.at]

        psum = ctx.enter_context(nc.psum_tensor("psum", [P, 8, BANK], F32))

        def banks(a, n=1):
            return psum[:, a:a + n, :].rearrange("p b n -> p (b n)")

        Y = [banks(0, 2), banks(2, 2)]
        GU = [banks(4), banks(5)]
        TURN_A = banks(6)
        TURN_X = banks(7)

        conv_rows = nc.dram_tensor("conv_rows", (TOKENS + CONV_W - 1, D_CONV), F32, kind="Internal").ap()
        h_rows = nc.dram_tensor("h_rows", (TOKENS, D), F32, kind="Internal").ap()
        y_rows = nc.dram_tensor("y_rows", (ITEMS * SLOTS, D), F32, kind="Internal").ap()

        landed = [sem(f"landed{i}") for i in range(RING)]
        rounded, split, used = sem("rounded"), sem("split"), sem("used")
        consts = sem("consts")
        pool_step, dve_step, act_step = sem("pool_step"), sem("dve_step"), sem("act_step")
        x_loaded, gain_loaded = sem("x_loaded"), [sem("gain_loaded0"), sem("gain_loaded1")]
        small_loaded, mix_loaded = sem("small_loaded"), sem("mix_loaded")
        small_high, small_low = sem("small_high"), sem("small_low")
        x_ready, squares, h_ready = sem("x_ready"), sem("squares"), sem("h_ready")
        roots, eps_set = sem("roots"), sem("eps_set")
        turned, turn_high, turn_low = sem("turned"), sem("turn_high"), sem("turn_low")
        gu_first, gate_ready, act_ready = sem("gu_first"), sem("gate_ready"), sem("act_ready")
        a_turned, a_high, a_low = sem("a_turned"), sem("a_high"), sem("a_low")
        in_first, in_copied = sem("in_first"), [sem("in_copied0"), sem("in_copied1")]
        g = {n: sem("gla_" + n) for n in ("rank", "rank_sb", "rankT", "rankT_sb", "z", "abs", "ln", "qkT", "q_sb",
                                          "k_sb", "diff", "decay", "scaled", "scores", "kept", "out", "sq", "silu", "summed", "roots")}
        s = {n: sem("sb_" + n) for n in ("qkT", "q_sb", "k_sb", "z", "z_sb", "ln", "sp", "sums", "arg", "exp", "w",
                                         "out", "out_sb", "even")}
        m = {n: sem("mix_" + n) for n in ("u", "zeros", "stored", "shifted", "qk", "qkT", "q_sb", "k_sb", "dots",
                                          "bias", "exp", "a", "aT", "aT_sb", "out", "sq", "lam", "lam_exp",
                                          "qk_sq", "qk_sum", "qk_root", "dots_sb", "conv", "sum", "root")}
        e = {n: sem("moe_" + n) for n in ("h_stored", "logits", "gexp_in", "gexp", "picked", "ranks", "maps", "index",
                                          "plan", "x_index", "x_landed", "x_turned", "x_high",
                                          "x_low", "silu", "act", "a_turned", "a_high", "a_low", "y_sb",
                                          "y_stored", "picks", "iota", "cleared", "padded",
                                          "pe_passed", "pool_passed")}
        final, stored_out = sem("final"), sem("stored_out")

        w_in = {"gla_in": t["gla_w_in"][0], "sb_in": t["sb_w_in"][0], "mix_in": t["w_in_2"][0]}
        w_out = {"gla_out": t["gla_w_out"][0], "sb_out": t["sb_w_out"][0], "mix_out": t["w_out_2"][0]}
        ffns = [(t[f"ffn{1 + i % 2}_w_gate"][i // 2], t[f"ffn{1 + i % 2}_w_up"][i // 2],
                 t[f"ffn{1 + i % 2}_w_down"][i // 2]) for i in range(4)]
        gains = [t["ffn1_norm"][0], t["mix_norm"][0], t["ffn2_norm"][0], t["ffn1_norm"][1], t["mix_norm"][1],
                 t["ffn2_norm"][1], t["final_norm"], t["attn_norm_g_2"][0], t["ffn_norm_g_2"][0]]
        TURN_OF_NORM = {0: 0, 1: 1, 2: 3, 3: 4, 4: 5, 5: 7, 7: 8, 8: 10}
        GLA_TURN, SB_TURN, MIX_TURN = 2, 6, 9
        H_ORDER = ["n0", "n1", "gla", "n2", "n3", "n4", "sb", "n5", "n7", "mix", "n8"]

        def scales_with(r, n):
            return 0 if isinstance(r, int) and r == 0 else r * n

        def piece_loads(sp, p, r, parts):
            if p >= RING or not isinstance(r, int):
                sp.wait_ge(split, p - RING + 1 + scales_with(r, 3))
            for dst, src in parts:
                sp.dma_start(dst, src).then_inc(landed[p % RING], 16)

        def round_piece(act, p, r=0):
            act.wait_ge(landed[p % RING], 32 * (p // RING + 1) + scales_with(r, 32))
            if p >= RING or not isinstance(r, int):
                act.wait_ge(used, p - RING + 1 + scales_with(r, 3))
            act.activation(high[:, p % RING, :], raw[:, p % RING, :], ACT.Copy).then_inc(rounded, 1)

        def split_piece(dve, p, r=0):
            dve.wait_ge(rounded, p + 1 + scales_with(r, 3))
            dve.tensor_tensor(low[:, p % RING, :], raw[:, p % RING, :], high[:, p % RING, :].bitcast(F32),
                              ALU.subtract).then_inc(split, 1)

        def product(pe, psum_out, lhs_high, lhs_low, rhs_high, rhs_low, start, stop=False):
            pe.matmul(psum_out, lhs_high, rhs_high, start=start, stop=False, skip_group_check=True)
            pe.matmul(psum_out, lhs_high, rhs_low, start=False, stop=False, skip_group_check=True)
            return pe.matmul(psum_out, lhs_low, rhs_high, start=False, stop=stop, skip_group_check=True)

        def gate_up_parts(p, w_gate, w_up, half, col):
            dst = raw[:, p % RING, :].rearrange("p (k n) -> p k n", k=4)
            rows = slice(half * 4 * P, (half + 1) * 4 * P)
            return [(dst[:, :, i * CHUNK:(i + 1) * CHUNK],
                     w[rows, bass.ds(col, CHUNK)].rearrange("(k p) n -> p k n", p=P)) for i, w in enumerate((w_gate, w_up))]

        def down_parts(p, w_down, row):
            dst = raw[:, p % RING, :].rearrange("p (k n) -> p k n", k=2)
            src = w_down[bass.ds(row, 2 * P), :].rearrange("(k p) n -> p k n", p=P)
            return [(dst[:, i, :], src[:, i, :]) for i in range(2)]

        def in_parts(p, w, half, n):
            dst = raw[:, p % RING, :].rearrange("p (k n) -> p k n", k=4)
            src = w[half * 4 * P:(half + 1) * 4 * P, n * BANK:(n + 1) * BANK].rearrange("(k p) n -> p k n", p=P)
            return [(dst[:, 2 * i:2 * i + 2, :], src[:, 2 * i:2 * i + 2, :]) for i in range(2)]

        def four_k(buf, p):
            return buf[:, p % RING, :].rearrange("p (k n) -> p k n", k=4)

        def two_k(buf, p):
            return buf[:, p % RING, :].rearrange("p (k n) -> p k n", k=2)

        def ffn_loads(sp, i):
            b = FIRST_PIECE[f"ffn{i}"]
            w_gate, w_up, w_down = ffns[i]
            for half in range(2):
                piece_loads(sp, b + half, 0, gate_up_parts(b + half, w_gate, w_up, half, 0))
            with sp.Fori(0, N_CHUNKS - 1) as c:
                for half in range(2):
                    piece_loads(sp, b + 2 + half, c, gate_up_parts(b + 2 + half, w_gate, w_up, half, (c + 1) * CHUNK))
                piece_loads(sp, b + 4, c, down_parts(b + 4, w_down, c * CHUNK))
            last = b + FFN_PIECES - 1
            piece_loads(sp, last, 0, down_parts(last, w_down, (N_CHUNKS - 1) * CHUNK))

        def in_loads(sp, name):
            for n in range(IN_CHUNKS):
                for half in range(2):
                    p = FIRST_PIECE[name] + 2 * n + half
                    piece_loads(sp, p, 0, in_parts(p, w_in[name], half, n))

        def out_loads(sp, name):
            for j in range(OUT_PIECES):
                p = FIRST_PIECE[name] + j
                piece_loads(sp, p, 0, down_parts(p, w_out[name], j * 2 * P))

        def norm_dve(dve, step, k, scale, last_piece):
            for tt in range(TT):
                if k == 0:
                    dve.wait_ge(x_loaded, 16)
                elif k != 7:
                    dve.wait_ge(used, last_piece + 1)
                    dve.scalar_tensor_tensor(x[:, tt, :], Y[tt], scale, x[:, tt, :], ALU.mult,
                                             ALU.add).then_inc(x_ready, 1)
            dve.wait_ge(roots, k + 1)
            step(dve.reciprocal(stat[:, 4:6], stat[:, 2:4]))
            for tt in range(TT):
                dve.wait_ge(gain_loaded[k % 2], 16 * (k // 2 + 1))
                to = x if k == 6 else h
                if k != 0 and k != 7:
                    dve.wait_ge(x_ready, X_COUNT[k] + tt + 1)
                dve.scalar_tensor_tensor(to[:, tt, :], x[:, tt, :], stat[:, 4 + tt:5 + tt], gain[:, k % 2, :], ALU.mult,
                                         ALU.mult).then_inc(x_ready if k == 6 else h_ready, 1)

        X_COUNT = {1: 0, 2: 2, 3: 4, 4: 6, 5: 8, 6: 10, 8: 14}

        def norm_act(act, k):
            for tt in range(TT):
                if k == 0:
                    act.wait_ge(x_loaded, 16)
                elif k == 7:
                    act.wait_ge(x_ready, 12 + tt + 1)
                else:
                    act.wait_ge(x_ready, X_COUNT[k] + tt + 1)
                if 2 * k + tt:
                    act.wait_ge(squares, 2 * k + tt)
                act.activation(square[:, :], x[:, tt, :], ACT.Square,
                               accum_out=stat[:, tt:tt + 1]).then_inc(squares, 1)
            if k == 0:
                act.wait_ge(eps_set, 1)
            act.wait_ge(squares, 2 * k + TT)
            act.activation(stat[:, 2:4], stat[:, 0:2], ACT.Sqrt, scale=1.0 / D, bias=eps[:, :]).then_inc(roots, 1)

        def turn_pe(pe, n, who):
            if n == 0:
                pe.wait_ge(consts, 1)
            for tt in range(TT):
                pe.wait_ge(h_ready, 2 * H_ORDER.index(who) + (TT if who in ("sb", "mix") else tt + 1))
                for k in range(KD):
                    dst = psum[:, 4 + k // 2, (k % 2) * TOKENS + tt * P:(k % 2) * TOKENS + (tt + 1) * P]
                    ins = pe.transpose(dst, h[:, tt, k * P:(k + 1) * P], ident[:, :])
                    if tt == TT - 1 and k % 2:
                        ins.then_inc(turned, 1)

        def turn_bank(buf, j):
            return buf[:, 2 * j:2 * j + 2, :].rearrange("p k n -> p (k n)")

        def turn_act(act, n):
            for j in range(4):
                act.wait_ge(turned, 4 * n + j + 1)
                act.activation(turn_bank(hT_high, j), banks(4 + j), ACT.Copy).then_inc(turn_high, 1)

        def turn_dve(dve, n):
            for j in range(4):
                dve.wait_ge(turn_high, 4 * n + j + 1)
                dve.tensor_tensor(turn_bank(hT_low, j), banks(4 + j), turn_bank(hT_high, j).bitcast(F32),
                                  ALU.subtract).then_inc(turn_low, 1)

        def clear_Y(pe):
            for b in range(4):
                pe.matmul(banks(b), zero_r[:, 0:P], zero_r[:, :], start=True, stop=True, skip_group_check=True)

        def gate_up_pe(pe, p, r, done_first):
            for half in range(2):
                q = p + half
                pe.wait_ge(split, q + 1 + scales_with(r, 3))
                for tt in range(TT):
                    for k in range(4):
                        kk = 4 * half + k
                        tok = slice(tt * P, (tt + 1) * P)
                        ins = product(pe, GU[tt], hT_high[:, kk, tok], hT_low[:, kk, tok], four_k(high, q)[:, k, :],
                                      four_k(low, q)[:, k, :], start=kk == 0, stop=kk == KD - 1)
                    if half == 1 and tt == 0:
                        ins.then_inc(done_first, 1)
                ins.then_inc(used, 1)

        def act_turn_pe(pe, count):
            for tt in range(TT):
                pe.wait_ge(act_ready, count + tt + 1 - 2)
                for k in range(2):
                    ins = pe.transpose(TURN_A[:, k * TOKENS + tt * P:k * TOKENS + (tt + 1) * P],
                                       act_tok[:, tt, k * P:(k + 1) * P], ident[:, :])
            ins.then_inc(a_turned, 1)

        def down_pe(pe, p, r, count_a):
            pe.wait_ge(a_low, count_a)
            pe.wait_ge(split, p + 1 + scales_with(r, 3))
            for k in range(2):
                for tt in range(TT):
                    for n in range(2):
                        tok, cols = slice(tt * P, (tt + 1) * P), slice(n * BANK, (n + 1) * BANK)
                        ins = product(pe, Y[tt][:, cols], aT_high[:, k, tok], aT_low[:, k, tok],
                                      two_k(high, p)[:, k, cols], two_k(low, p)[:, k, cols], start=False)
            ins.then_inc(used, 1)

        def ffn_pe(pe, i, turn):
            b, done = FIRST_PIECE[f"ffn{i}"], N_CHUNKS * i
            clear_Y(pe)
            pe.wait_ge(turn_low, 4 * (turn + 1))
            gate_up_pe(pe, b, 0, gu_first)
            act_turn_pe(pe, 2 * (done + 1))
            with pe.Fori(0, N_CHUNKS - 1) as c:
                gate_up_pe(pe, b + 2, c, gu_first)
                down_pe(pe, b + 4, c, c + (done + 1))
                act_turn_pe(pe, c * 2 + 2 * (done + 2))
            down_pe(pe, b + FFN_PIECES - 1, 0, done + N_CHUNKS)

        def gate_act(act, first, second):
            for tt, (counter, value) in enumerate(((gu_first, first), (used, second))):
                act.wait_ge(counter, value)
                act.activation(gate[:, tt, :], GU[tt][:, 0:CHUNK], ACT.Silu).then_inc(gate_ready, 1)

        def gate_dve(dve, count):
            for tt in range(TT):
                dve.wait_ge(gate_ready, count + tt + 1 - 2)
                dve.tensor_tensor(act_tok[:, tt, :], gate[:, tt, :], GU[tt][:, CHUNK:2 * CHUNK],
                                  ALU.mult).then_inc(act_ready, 1)

        def flat(buf):
            return buf[:, :, :].rearrange("p k n -> p (k n)")

        def ffn_act(act, i):
            b, done = FIRST_PIECE[f"ffn{i}"], N_CHUNKS * i

            def chunk(p, r, number, gu_used):
                round_piece(act, p, r)
                gate_act(act, number, gu_used)
                round_piece(act, p + 1, r)
                act.wait_ge(a_turned, number)
                act.activation(flat(aT_high), TURN_A, ACT.Copy).then_inc(a_high, 1)
                round_piece(act, p + 2, r)

            chunk(b + 2, 0, done + 1, b + 2)
            with act.Fori(0, N_CHUNKS - 1) as c:
                chunk(b + 5, c, c + (done + 2), c * 3 + (b + 4))

        def ffn_dve(dve, i):
            b, done = FIRST_PIECE[f"ffn{i}"], N_CHUNKS * i

            def chunk(p, r, number):
                split_piece(dve, p, r)
                gate_dve(dve, number * 2)
                split_piece(dve, p + 1, r)
                dve.wait_ge(a_high, number)
                dve.tensor_tensor(flat(aT_low), TURN_A, flat(aT_high).bitcast(F32), ALU.subtract).then_inc(a_low, 1)
                split_piece(dve, p + 2, r)

            chunk(b + 2, 0, done + 1)
            with dve.Fori(0, N_CHUNKS - 1) as c:
                chunk(b + 5, c, c + (done + 2))

        IN_ORDER = ["gla_in", "sb_in", "mix_in"]

        def in_pe(pe, name, turn):
            b, done = FIRST_PIECE[name], IN_CHUNKS * IN_ORDER.index(name)
            pe.wait_ge(turn_low, 4 * (turn + 1))
            for n in range(IN_CHUNKS):
                if n >= 3:
                    for c in in_copied:
                        pe.wait_ge(c, done + n - 2)
                for half in range(2):
                    q = b + 2 * n + half
                    pe.wait_ge(split, q + 1)
                    for tt in range(TT):
                        for k in range(4):
                            kk, tok = 4 * half + k, slice(tt * P, (tt + 1) * P)
                            ins = product(pe, banks(2 * (n % 3) + tt), hT_high[:, kk, tok], hT_low[:, kk, tok],
                                          four_k(high, q)[:, k, :], four_k(low, q)[:, k, :], start=kk == 0,
                                          stop=kk == KD - 1)
                        if half == 1 and tt == 0:
                            ins.then_inc(in_first, 1)
                    ins.then_inc(used, 1)

        def in_act(act, name):
            b, done = FIRST_PIECE[name], IN_CHUNKS * IN_ORDER.index(name)
            for n in range(IN_CHUNKS):
                round_piece(act, b + 2 * n + 2)
                round_piece(act, b + 2 * n + 3)
                act.wait_ge(in_first, done + n + 1)
                act.activation(proj[:, 0, n * BANK:(n + 1) * BANK], banks(2 * (n % 3)),
                               ACT.Copy).then_inc(in_copied[0], 1)

        def in_dve(dve, name):
            b = FIRST_PIECE[name]
            for n in range(IN_CHUNKS):
                split_piece(dve, b + 2 * n + 2)
                split_piece(dve, b + 2 * n + 3)
                dve.wait_ge(used, b + 2 * n + 2)
                dve.tensor_copy(proj[:, 1, n * BANK:(n + 1) * BANK], banks(2 * (n % 3) + 1)).then_inc(in_copied[1], 1)

        def wait_proj(eng, name):
            for c in in_copied:
                eng.wait_ge(c, IN_CHUNKS * (IN_ORDER.index(name) + 1))

        def out_pe(pe, name, turn):
            b = FIRST_PIECE[name]
            pe.wait_ge(turn_low, 4 * (turn + 1))
            for j in range(OUT_PIECES):
                p = b + j
                pe.wait_ge(split, p + 1)
                for k in range(2):
                    for tt in range(TT):
                        for n in range(2):
                            tok, cols = slice(tt * P, (tt + 1) * P), slice(n * BANK, (n + 1) * BANK)
                            ins = product(pe, Y[tt][:, cols], hT_high[:, 2 * j + k, tok], hT_low[:, 2 * j + k, tok],
                                          two_k(high, p)[:, k, cols], two_k(low, p)[:, k, cols],
                                          start=j == 0 and k == 0, stop=j == OUT_PIECES - 1 and k == 1)
                ins.then_inc(used, 1)

        def out_act(act, name):
            for j in range(3, 6):
                round_piece(act, FIRST_PIECE[name] + j)

        def out_dve(dve, name):
            for j in range(3, 6):
                split_piece(dve, FIRST_PIECE[name] + j)

        area = Area()
        gq = area.take(1024)
        gk = area.take(1024)
        gb = area.take(1024)
        gdiff = area.take(1024)
        geq, gek = square[:, 0:512], square[:, 512:1024]
        gqs = [area.take(1024) for _ in range(2)]
        gks = [area.take(1024) for _ in range(2)]
        gscore = area.take(1024)
        gcross = area.take(512)
        grank = area.take(TT * GLA_RANK)
        grankT = area.take(TOKENS)
        gsilu = [gqs[0], gqs[1]]
        gabs, glog = gks[0], gks[1]
        STEPS = [P] + LEVELS

        def pairs(v, B):
            return v.rearrange("p (m n) -> p m n", n=2 * B)

        def gla_pe(pe):
            pe.wait_ge(small_low, 1)
            pe.wait_ge(turn_low, 4 * 2)
            for tt in range(TT):
                for k in range(KD):
                    tok = slice(tt * P, (tt + 1) * P)
                    ins = product(pe, TURN_A[:, tt * GLA_RANK:(tt + 1) * GLA_RANK], hT_high[:, k, tok], hT_low[:, k, tok],
                                  gkw_high[:, k, :], gkw_low[:, k, :], start=tt == 0 and k == 0)
            ins.then_inc(g["rank"], 1)
            in_pe(pe, "gla_in", 1)
            wait_proj(pe, "gla_in")
            pe.wait_ge(g["rank_sb"], 1)
            for tt in range(TT):
                ins = pe.transpose(TURN_X[0:GLA_RANK, tt * P:(tt + 1) * P], grank[:, tt * GLA_RANK:(tt + 1) * GLA_RANK],
                                   ident[:, :])
            ins.then_inc(g["rankT"], 1)
            for w, off in ((2, 0), (4, 512)):
                for hd in range(GLA_HEADS):
                    for tt in range(TT):
                        dst = banks(w, 2)[:, hd * TOKENS + tt * P:hd * TOKENS + (tt + 1) * P]
                        ins = pe.transpose(dst, proj[:, tt, off + hd * P:off + (hd + 1) * P], ident[:, :])
                ins.then_inc(g["qkT"], 1)
            pe.wait_ge(g["rankT_sb"], 1)
            for hd in range(GLA_HEADS):
                ins = pe.matmul(banks(0, 2)[:, hd * TOKENS:(hd + 1) * TOKENS], wgk2[:, hd * P:(hd + 1) * P],
                                grankT[0:GLA_RANK, :], start=hd % 2 == 0, stop=True, skip_group_check=True)
            ins.then_inc(g["z"], 1)
            for n, B in enumerate(STEPS + [0]):
                if B:
                    pe.wait_ge(g["scaled"], n + 1)
                    q, k = gqs[n % 2], gks[n % 2]
                else:
                    q, k = gq, gk
                if n >= 2:
                    pe.wait_ge(g["kept"], n - 1)
                else:
                    pe.wait_ge(g["q_sb"], 1)
                    pe.wait_ge(g["k_sb"], 1)
                dst = banks(2 + 2 * (n % 2), 2)
                for hd in range(GLA_HEADS):
                    if B == P:
                        at = hd * TOKENS
                        ins = pe.matmul(dst[:, hd * P:(hd + 1) * P], k[:, at:at + P], q[:, at + P:at + 2 * P],
                                        start=hd == 0, stop=True, skip_group_check=True)
                        continue
                    for tt in range(TT):
                        at = hd * TOKENS + tt * P
                        ins = pe.matmul(dst[:, at:at + P], k[:, at:at + P], q[:, at:at + P],
                                        start=at % BANK == 0, stop=True, skip_group_check=True)
                ins.then_inc(g["scores"], 1)
            pe.wait_ge(g["kept"], len(STEPS) + 1)
            for hd in range(GLA_HEADS):
                def v(tt):
                    return proj[:, tt, 1024 + hd * GLA_V:1024 + (hd + 1) * GLA_V]

                def diag(tt):
                    return gscore[:, hd * TOKENS + tt * P:hd * TOKENS + (tt + 1) * P]
                cols = slice(hd * GLA_V, (hd + 1) * GLA_V)
                pe.matmul(Y[0][:, cols], diag(0), v(0), start=hd % 2 == 0, stop=True, skip_group_check=True)
                pe.matmul(Y[1][:, cols], diag(1), v(1), start=hd % 2 == 0, stop=False, skip_group_check=True)
                ins = pe.matmul(Y[1][:, cols], gcross[:, hd * P:(hd + 1) * P], v(0), start=False, stop=True,
                                skip_group_check=True)
            ins.then_inc(g["out"], 1)
            turn_pe(pe, GLA_TURN, "gla")
            out_pe(pe, "gla_out", GLA_TURN)

        def gla_act(act, step):
            in_act(act, "gla_in")
            round_piece(act, FIRST_PIECE["gla_out"] + 2)
            act.wait_ge(g["z"], 1)
            for hd in range(GLA_HEADS):
                c = slice(hd * TOKENS, (hd + 1) * TOKENS)
                ins = act.activation(gabs[:, c], banks(0, 2)[:, c], ACT.Abs, bias=bgk[:, hd:hd + 1])
            step(ins)
            act.wait_ge(g["qkT"], 1)
            step(act.activation(gabs, gabs, ACT.Exp, scale=-1.0))
            act.activation(glog, gabs, ACT.Ln, bias=ones[:, 0:1]).then_inc(g["ln"], 1)
            act.activation(gq, banks(2, 2), ACT.Copy, scale=float(GLA_K) ** -0.5).then_inc(g["q_sb"], 1)
            for n, B in enumerate(STEPS):
                act.wait_ge(g["diff"], n + 1)
                if n:
                    act.wait_ge(g["scaled"], n)
                v = pairs(gdiff, B)
                w = {"n": B}
                act.activation(geq.rearrange("p (m n) -> p m n", **w), v[:, :, B:2 * B], ACT.Exp, scale=1.0 / GLA_TAU)
                act.activation(gek.rearrange("p (m n) -> p m n", **w), v[:, :, 0:B], ACT.Exp,
                               scale=-1.0 / GLA_TAU).then_inc(g["decay"], 1)
            act.wait_ge(g["out"], 1)
            for tt in range(TT):
                act.activation((square[:, :], gdiff)[tt], Y[tt], ACT.Square).then_inc(g["sq"], 1)
            for tt in range(TT):
                act.activation(gsilu[tt], proj[:, tt, 2048:3072], ACT.Silu).then_inc(g["silu"], 1)
            act.wait_ge(g["summed"], 1)
            act.activation(stat[:, 16:24], stat[:, 8:16], ACT.Sqrt, scale=1.0 / GLA_V,
                           bias=eps[:, :]).then_inc(g["roots"], 1)
            turn_act(act, GLA_TURN)
            out_act(act, "gla_out")

        def gla_dve(dve, step):
            in_dve(dve, "gla_in")
            split_piece(dve, FIRST_PIECE["gla_out"] + 2)
            dve.wait_ge(g["rankT"], 1)
            dve.tensor_copy(grankT[0:GLA_RANK, :], TURN_X[0:GLA_RANK, 0:TOKENS]).then_inc(g["rankT_sb"], 1)
            dve.wait_ge(g["qkT"], 2)
            dve.tensor_copy(gk, banks(4, 2)).then_inc(g["k_sb"], 1)
            dve.wait_ge(g["ln"], 1)
            for hd in range(GLA_HEADS):
                c = slice(hd * TOKENS, (hd + 1) * TOKENS)
                ins = dve.tensor_scalar(gdiff[:, c], banks(0, 2)[:, c], bgk[:, hd:hd + 1], 0.0, ALU.add, ALU.min)
            step(ins)
            step(dve.tensor_tensor(gdiff, gdiff, glog, ALU.subtract))
            for hd in range(GLA_HEADS):
                c = slice(hd * TOKENS, (hd + 1) * TOKENS)
                ins = dve.tensor_tensor_scan(gb[:, c], ones[:, :], gdiff[:, c], 0.0, ALU.mult, ALU.add)
            step(ins)
            for i in range(2):
                dve.memset(gqs[i], 0.0)
                ins = dve.memset(gks[i], 0.0)
            step(ins)
            dve.wait_ge(g["q_sb"], 1)
            for n, B in enumerate(STEPS):
                v = pairs(gb, B)
                if n:
                    dve.wait_ge(g["decay"], n)
                dve.tensor_tensor(pairs(gdiff, B), v, v[:, :, B - 1:B].to_broadcast([P, TT * GLA_HEADS * P // (2 * B), 2 * B]),
                                  ALU.subtract).then_inc(g["diff"], 1)
                if n:
                    keep(dve, n - 1)
                dve.wait_ge(g["decay"], n + 1)
                if n >= 2:
                    dve.wait_ge(g["scores"], n - 1)
                w = {"n": B}
                dve.tensor_tensor(pairs(gqs[n % 2], B)[:, :, B:2 * B], pairs(gq, B)[:, :, B:2 * B],
                                  geq.rearrange("p (m n) -> p m n", **w), ALU.mult)
                dve.tensor_tensor(pairs(gks[n % 2], B)[:, :, 0:B], pairs(gk, B)[:, :, 0:B],
                                  gek.rearrange("p (m n) -> p m n", **w), ALU.mult).then_inc(g["scaled"], 1)
            keep(dve, len(STEPS) - 1)
            keep(dve, len(STEPS))
            dve.wait_ge(g["sq"], 2)
            for tt in range(TT):
                ins = dve.tensor_reduce(stat[:, 8 + 4 * tt:12 + 4 * tt],
                                        (square[:, :], gdiff)[tt].rearrange("p (a b) -> p a b", b=GLA_V), AX, ALU.add)
            ins.then_inc(g["summed"], 1)
            dve.wait_ge(g["roots"], 1)
            step(dve.reciprocal(stat[:, 24:32], stat[:, 16:24]))
            for tt in range(TT):
                for hd in range(GLA_HEADS):
                    c, n = slice(hd * GLA_V, (hd + 1) * GLA_V), 24 + 4 * tt + hd
                    ins = dve.scalar_tensor_tensor(h[:, tt, c], Y[tt][:, c], stat[:, n:n + 1], gla_gain[:, :],
                                                   ALU.mult, ALU.mult)
                step(ins)
                dve.wait_ge(g["silu"], tt + 1)
                dve.tensor_tensor(h[:, tt, :], h[:, tt, :], gsilu[tt], ALU.mult).then_inc(h_ready, 1)
            turn_dve(dve, GLA_TURN)
            out_dve(dve, "gla_out")

        def keep(dve, n):
            dve.wait_ge(g["scores"], n + 1)
            src = banks(2 + 2 * (n % 2), 2)
            if n == 0:
                ins = dve.tensor_copy(gcross, src[:, 0:GLA_HEADS * P])
                ins.then_inc(g["kept"], 1)
                return
            dve.wait_ge(g["kept"], n)
            B = (STEPS + [0])[n]
            mask = levels[:, LEVELS.index(B), :] if B else ident[:, :]
            mask = mask.bitcast(I32).rearrange("p (o n) -> p o n", o=1).to_broadcast([P, 2 * GLA_HEADS, P])
            dve.copy_predicated(gscore.rearrange("p (b n) -> p b n", n=P), mask,
                                src.rearrange("p (b n) -> p b n", n=P)).then_inc(g["kept"], 1)

        area = Area()
        sq_T, sk_T = area.take(2048), area.take(2048)
        GROUP_COLS = GROUP * (TOKENS + P)
        sz = [area.take(GROUP_COLS) for _ in range(2)]
        ssp = [area.take(GROUP_COLS) for _ in range(2)]

        def place(i):
            return (i % 2) * 2 + i // 2

        def early(v):
            return v[:, 0:GROUP * TOKENS].rearrange("p (a n) -> p a n", n=TOKENS)[:, :, 0:P]

        def late_part(v):
            return v[:, GROUP * TOKENS:].rearrange("p (a n) -> p a n", n=P)

        def turn_columns(pe, dst, off, tiles, signal):
            for k in range(tiles):
                for tt in range(TT):
                    ins = pe.transpose(dst[:, k * TOKENS + tt * P:k * TOKENS + (tt + 1) * P],
                                       proj[:, tt, off + k * P:off + (k + 1) * P], ident[:, :])
            ins.then_inc(signal, 1)

        def sb_pe(pe):
            in_pe(pe, "sb_in", 5)
            wait_proj(pe, "sb_in")
            turn_columns(pe, banks(0, 4), 0, KD, s["qkT"])
            turn_columns(pe, banks(4, 4), D, KD, s["qkT"])
            pe.wait_ge(s["q_sb"], 1)
            pe.wait_ge(s["k_sb"], 1)

            def dots(gr):
                if gr:
                    pe.wait_ge(s["z_sb"], gr)
                z = banks(0, 3)
                for i in (0, 2, 1, 3):
                    rows, at = slice(SB_HD * (i % 2), SB_HD * (i % 2 + 1)), (2 * gr + i // 2) * TOKENS
                    c = place(i)
                    pe.matmul(z[:, c * TOKENS:(c + 1) * TOKENS], sk_T[rows, at:at + P], sq_T[rows, at:at + TOKENS],
                              start=True, stop=True, skip_group_check=True)
                    if i >= 2:
                        if i == 3:
                            pe.wait_ge(s["even"], gr + 1)
                        for ii in (i - 2, i):
                            c, at = place(ii), (2 * gr + ii // 2) * TOKENS
                            ins = pe.matmul(z[:, GROUP * TOKENS + c * P:GROUP * TOKENS + (c + 1) * P],
                                            sk_T[rows, at + P:at + TOKENS], sq_T[rows, at + P:at + TOKENS],
                                            start=True, stop=True, skip_group_check=True)
                        if i == 2:
                            ins.then_inc(s["even"], 1)
                ins.then_inc(s["z"], 1)

            dots(0)
            for gr in range(SB_GROUPS):
                if gr + 1 < SB_GROUPS:
                    dots(gr + 1)
                pe.wait_ge(s["sp"], gr + 1)
                if gr:
                    pe.wait_ge(s["arg"], gr)
                v = ssp[gr % 2]
                for b in range(3):
                    ins = pe.matmul(banks(3 + b), suffix[:, :], v[:, b * BANK:(b + 1) * BANK], start=True, stop=b == 2,
                                    skip_group_check=True)
                    if b < 2:
                        dst = banks(3 + b).rearrange("p (a n) -> p a n", n=TOKENS)[:, :, P:TOKENS]
                        pe.matmul(dst, ones[:, 0:P], late_part(v)[:, 2 * b:2 * b + 2, :], start=False, stop=True,
                                  skip_group_check=True)
                ins.then_inc(s["sums"], 1)
                pe.wait_ge(s["w"], gr + 1)
                if gr >= 2:
                    pe.wait_ge(s["out_sb"], gr - 1)
                w, dst = sz[gr % 2], banks(6 + gr % 2)
                for i in range(GROUP):
                    c, col = place(i), 2 * D + (GROUP * gr + i) * SB_HD
                    v0, v1 = proj[:, 0, col:col + SB_HD], proj[:, 1, col:col + SB_HD]
                    pe.matmul(dst[:, i * SB_HD:(i + 1) * SB_HD], w[:, c * TOKENS:c * TOKENS + P], v0, start=i == 0,
                              stop=True, skip_group_check=True)
                    to = dst[:, TOKENS + i * SB_HD:TOKENS + (i + 1) * SB_HD]
                    pe.matmul(to, w[:, c * TOKENS + P:(c + 1) * TOKENS], v0, start=False, stop=False,
                              skip_group_check=True)
                    at = GROUP * TOKENS + c * P
                    ins = pe.matmul(to, w[:, at:at + P], v1, start=False, stop=True, skip_group_check=True)
                ins.then_inc(s["out"], 1)
            turn_pe(pe, SB_TURN, "sb")
            out_pe(pe, "sb_out", SB_TURN)

        def sb_act(act, step):
            in_act(act, "sb_in")
            round_piece(act, FIRST_PIECE["sb_out"] + 2)
            act.wait_ge(s["qkT"], 1)
            act.activation(sq_T, banks(0, 4), ACT.Copy, scale=float(SB_HD) ** -0.5).then_inc(s["q_sb"], 1)

            def softplus_tail(gr):
                act.wait_ge(s["z_sb"], gr + 1)
                if gr >= 2:
                    act.wait_ge(s["sums"], gr - 1)
                v = ssp[gr % 2]
                step(act.activation(v, sz[gr % 2], ACT.Abs))
                step(act.activation(v, v, ACT.Exp, scale=-1.0))
                act.activation(v, v, ACT.Ln, bias=ones[:, 0:1]).then_inc(s["ln"], 1)

            softplus_tail(0)
            for gr in range(SB_GROUPS):
                if gr + 1 < SB_GROUPS:
                    softplus_tail(gr + 1)
                act.wait_ge(s["arg"], gr + 1)
                act.activation(sz[gr % 2], sz[gr % 2], ACT.Exp).then_inc(s["exp"], 1)
            turn_act(act, SB_TURN)
            out_act(act, "sb_out")

        def sb_dve(dve, step):
            in_dve(dve, "sb_in")
            split_piece(dve, FIRST_PIECE["sb_out"] + 2)
            dve.wait_ge(s["qkT"], 2)
            dve.tensor_copy(sk_T, banks(4, 4)).then_inc(s["k_sb"], 1)
            mask = strict[:, :].rearrange("p (o n) -> p o n", o=1).to_broadcast([P, GROUP, P])

            def copy_z(gr):
                dve.wait_ge(s["z"], gr + 1)
                if gr >= 2:
                    dve.wait_ge(s["out"], gr - 1)
                dve.tensor_copy(sz[gr % 2], banks(0, 3)).then_inc(s["z_sb"], 1)

            def softplus(gr):
                v = ssp[gr % 2]
                dve.wait_ge(s["ln"], gr + 1)
                dve.wait_ge(s["z_sb"], gr + 1)
                step(dve.scalar_tensor_tensor(v, sz[gr % 2], 0.0, v, ALU.max, ALU.add))
                dve.tensor_tensor(early(v), early(v), mask, ALU.mult)
                dve.tensor_tensor(late_part(v), late_part(v), mask, ALU.mult).then_inc(s["sp"], 1)

            copy_z(0)
            softplus(0)
            for gr in range(SB_GROUPS):
                if gr + 1 < SB_GROUPS:
                    copy_z(gr + 1)
                w = sz[gr % 2]
                dve.wait_ge(s["sums"], gr + 1)
                dve.tensor_tensor(w, w, banks(3, 3), ALU.subtract).then_inc(s["arg"], 1)
                if gr + 1 < SB_GROUPS:
                    softplus(gr + 1)
                dve.wait_ge(s["exp"], gr + 1)
                for part in (early, late_part):
                    ins = dve.scalar_tensor_tensor(part(w), part(w), 1.0, mask, ALU.min, ALU.mult)
                ins.then_inc(s["w"], 1)
                dve.wait_ge(s["out"], gr + 1)
                src = banks(6 + gr % 2)
                for tt in range(TT):
                    last = gr == SB_GROUPS - 1
                    ins = dve.tensor_copy(h[:, tt, gr * TOKENS:(gr + 1) * TOKENS], src[:, tt * TOKENS:(tt + 1) * TOKENS])
                    if last:
                        ins.then_inc(h_ready, 1)
                if not last:
                    ins.then_inc(s["out_sb"], 1)
            turn_dve(dve, SB_TURN)
            out_dve(dve, "sb_out")

        area = Area()
        mqT, mkT = area.take(1024), area.take(1024)
        mdot = [area.take(2 * 3 * P) for _ in range(2)]
        mexp = [area.take(2 * 3 * P) for _ in range(2)]
        ma = [area.take(3 * P) for _ in range(2)]
        maT = [area.take(3 * P) for _ in range(2)]
        shifted = [area.take(TT * D_CONV) for _ in range(2)]
        conv_w = area.take(CONV_W * D_CONV)
        conv_gain = area.take(D_CONV)
        msquare = scratch[:, 2048:4096]
        params = levels[:, :, :].rearrange("p a n -> p (a n)")
        qk_gain, sub_gain, lam_in = params[:, 0:128], params[:, 128:256], params[:, 256:512]
        XC, BG, CG, QK, VV = 0, D_CONV, 2 * D_CONV, 3 * D_CONV, 5 * D_CONV
        QK_GROUPS = 2 * 2 * DA_HEADS

        def both(off, n):
            return proj[:, :, off:off + n]

        def by_tile(v):
            return v.rearrange("p (a n) -> p a n", a=TT)

        def mix_pe(pe):
            in_pe(pe, "mix_in", 8)
            pe.wait_ge(m["qk"], 1)
            turn_columns(pe, banks(0, 2), QK, DA_HEADS, m["qkT"])
            turn_columns(pe, banks(2, 2), QK + D_CONV, DA_HEADS, m["qkT"])
            pe.wait_ge(m["q_sb"], 1)
            pe.wait_ge(m["k_sb"], 1)

            def dots(hd):
                if hd >= 2:
                    pe.wait_ge(m["dots_sb"], hd - 1)
                for c in range(2):
                    rows, at, dst = slice(DA_HD * c, DA_HD * (c + 1)), hd * TOKENS, banks(2 * (hd % 2) + c)
                    pe.matmul(dst[:, 0:P], mqT[rows, at:at + P], mkT[rows, at:at + P], start=True, stop=True,
                              skip_group_check=True)
                    ins = pe.matmul(dst[:, P:3 * P], mqT[rows, at + P:at + TOKENS], mkT[rows, at:at + TOKENS],
                                    start=True, stop=True, skip_group_check=True)
                ins.then_inc(m["dots"], 1)

            dots(0)
            for hd in range(DA_HEADS):
                if hd + 1 < DA_HEADS:
                    dots(hd + 1)
                pe.wait_ge(m["a"], hd + 1)
                if hd >= 2:
                    pe.wait_ge(m["aT_sb"], hd - 1)
                for j in range(3):
                    ins = pe.transpose(banks(4 + hd % 2)[:, j * P:(j + 1) * P], ma[hd % 2][:, j * P:(j + 1) * P], ident[:, :])
                ins.then_inc(m["aT"], 1)
                pe.wait_ge(m["aT_sb"], hd + 1)
                a, col = maT[hd % 2], slice(hd * DA_V, (hd + 1) * DA_V)
                v0, v1 = (proj[:, tt, VV + hd * DA_V:VV + (hd + 1) * DA_V] for tt in range(TT))
                pe.matmul(banks(6)[:, col], a[:, 0:P], v0, start=hd == 0, stop=True, skip_group_check=True)
                pe.matmul(banks(7)[:, col], a[:, P:2 * P], v0, start=hd == 0, stop=False, skip_group_check=True)
                ins = pe.matmul(banks(7)[:, col], a[:, 2 * P:], v1, start=False, stop=True, skip_group_check=True)
            ins.then_inc(m["out"], 1)
            turn_pe(pe, MIX_TURN, "mix")
            out_pe(pe, "mix_out", MIX_TURN)

        def mix_act(act, step):
            in_act(act, "mix_in")
            round_piece(act, FIRST_PIECE["mix_out"] + 2)
            wait_proj(act, "mix_in")
            act.activation(by_tile(msquare), both(QK, 2 * D_CONV), ACT.Square).then_inc(m["qk_sq"], 1)
            act.wait_ge(m["qk_sum"], 1)
            act.activation(stat[:, 0:32], stat[:, 32:64], ACT.Sqrt, scale=1.0 / DA_HD, bias=eps[:, :]).then_inc(m["qk_root"], 1)
            act.wait_ge(m["lam"], 1)
            act.activation(params[:, 514:516], params[:, 512:514], ACT.Exp).then_inc(m["lam_exp"], 1)
            act.wait_ge(m["qkT"], 1)
            act.activation(mqT, banks(0, 2), ACT.Copy, scale=float(DA_HD) ** -0.5).then_inc(m["q_sb"], 1)

            def softmax(hd):
                act.wait_ge(m["bias"], hd + 1)
                for tt, lo, hi in ((0, 0, P), (1, P, 3 * P)):
                    for c in range(2):
                        at, col = c * 3 * P, 8 * (hd % 2) + 2 * tt + c
                        ins = act.activation(mexp[hd % 2][:, at + lo:at + hi], mdot[hd % 2][:, at + lo:at + hi], ACT.Exp,
                                             bias=stat[:, 4 + col:5 + col], accum_out=stat[:, 16 + col:17 + col])
                ins.then_inc(m["exp"], 1)

            softmax(0)
            for hd in range(DA_HEADS):
                if hd + 1 < DA_HEADS:
                    softmax(hd + 1)
                act.wait_ge(m["aT"], hd + 1)
                act.activation(maT[hd % 2], banks(4 + hd % 2)[:, 0:3 * P], ACT.Copy).then_inc(m["aT_sb"], 1)
            act.wait_ge(m["conv"], 1)
            act.wait_ge(m["out"], 1)
            act.activation(by_tile(scratch[:, 2048:3072]), both(XC, D_CONV), ACT.Square)
            act.activation(square[:, :], banks(6, 2), ACT.Square).then_inc(m["sq"], 1)
            act.wait_ge(m["sum"], 1)
            act.activation(stat[:, 32:48], stat[:, 0:16], ACT.Sqrt, scale=8.0 / D_CONV, bias=eps[:, :])
            act.activation(stat[:, 48:56], stat[:, 16:24], ACT.Sqrt, scale=1.0 / DA_V, bias=eps[:, :]).then_inc(m["root"], 1)
            turn_act(act, MIX_TURN)
            out_act(act, "mix_out")

        def mix_dve(dve, step):
            in_dve(dve, "mix_in")
            split_piece(dve, FIRST_PIECE["mix_out"] + 2)
            wait_proj(dve, "mix_in")
            dve.tensor_tensor(both(XC, D_CONV), both(XC, D_CONV), both(CG, D_CONV), ALU.mult).then_inc(m["u"], 1)
            dve.wait_ge(m["qk_sq"], 1)
            dve.tensor_reduce(stat[:, 32:64], msquare.rearrange("p (a n) -> p a n", n=DA_HD), AX, ALU.add).then_inc(m["qk_sum"], 1)
            dve.wait_ge(mix_loaded, 9 * 16)
            step(dve.tensor_tensor(lam_in[:, 0:128], lam_in[:, 0:128], lam_in[:, 128:256], ALU.mult))
            dve.tensor_reduce(params[:, 512:514], lam_in[:, 0:128].rearrange("p (a n) -> p a n", n=DA_HD), AX,
                              ALU.add).then_inc(m["lam"], 1)
            dve.wait_ge(m["qk_root"], 1)
            step(dve.reciprocal(stat[:, 32:64], stat[:, 0:32]))
            gains_qk = qk_gain.rearrange("p (a o n) -> p a o n", a=2, o=1).to_broadcast([P, 2, QK_GROUPS // 2, DA_HD])
            for tt in range(TT):
                v = proj[:, tt, QK:QK + 2 * D_CONV]
                v3, v4 = v.rearrange("p (a n) -> p a n", n=DA_HD), v.rearrange("p (a b n) -> p a b n", a=2, n=DA_HD)
                r = stat[:, 32 + 16 * tt:48 + 16 * tt].rearrange("p (a o) -> p a o", o=1).to_broadcast([P, QK_GROUPS, DA_HD])
                step(dve.tensor_tensor(v3, v3, r, ALU.mult))
                ins = dve.tensor_tensor(v4, v4, gains_qk, ALU.mult)
            ins.then_inc(m["qk"], 1)
            dve.wait_ge(m["lam_exp"], 1)
            step(dve.tensor_scalar(params[:, 516:517], params[:, 515:516], params[:, 514:515], LAMBDA_INIT, ALU.subtract,
                                   ALU.subtract))
            dve.wait_ge(m["qkT"], 2)
            dve.tensor_copy(mkT, banks(2, 2)).then_inc(m["k_sb"], 1)
            mask = causal[:, :].rearrange("p (o n) -> p o n", o=1).to_broadcast([P, 2, 3 * P])

            def scores(hd):
                v = mdot[hd % 2].rearrange("p (c n) -> p c n", c=2)
                src = psum[:, 2 * (hd % 2):2 * (hd % 2) + 2, 0:3 * P]
                dve.wait_ge(m["dots"], hd + 1)
                at = 8 * (hd % 2)
                ins = dve.tensor_tensor(v, src, mask, ALU.add)
                ins.then_inc(m["dots_sb"], 1)
                dve.wait_ge(m["dots_sb"], hd + 1)
                dve.tensor_reduce(stat[:, 32 + at:34 + at], v[:, :, 0:P], AX, ALU.max)
                step(dve.tensor_reduce(stat[:, 34 + at:36 + at], v[:, :, P:], AX, ALU.max))
                dve.tensor_scalar(stat[:, 4 + at:8 + at], stat[:, 32 + at:36 + at], -1.0, None, ALU.mult).then_inc(m["bias"], 1)

            scores(0)
            for hd in range(DA_HEADS):
                if hd + 1 < DA_HEADS:
                    scores(hd + 1)
                at = 8 * (hd % 2)
                dve.wait_ge(m["exp"], hd + 1)
                step(dve.reciprocal(stat[:, 48 + at:52 + at], stat[:, 16 + at:20 + at]))
                v = stat[:, 48 + at:52 + at].rearrange("p (a c) -> p a c", c=2)[:, :, 1]
                step(dve.tensor_scalar(v, v, params[:, 516:517], None, ALU.mult))
                if hd >= 2:
                    dve.wait_ge(m["aT"], hd - 1)
                for tt, lo, hi in ((0, 0, P), (1, P, 3 * P)):
                    n = 48 + at + 2 * tt
                    second = mexp[hd % 2][:, 3 * P + lo:3 * P + hi]
                    step(dve.tensor_scalar(second, second, stat[:, n + 1:n + 2], None, ALU.mult))
                    ins = dve.scalar_tensor_tensor(ma[hd % 2][:, lo:hi], mexp[hd % 2][:, lo:hi], stat[:, n:n + 1], second,
                                                   ALU.mult, ALU.add)
                ins.then_inc(m["a"], 1)
            dve.wait_ge(m["sq"], 1)
            dve.tensor_reduce(stat[:, 0:16], scratch[:, 2048:3072].rearrange("p (a n) -> p a n", n=D_CONV // 8), AX, ALU.add)
            dve.tensor_reduce(stat[:, 16:24], square[:, :].rearrange("p (a n) -> p a n", n=DA_V), AX,
                              ALU.add).then_inc(m["sum"], 1)
            dve.wait_ge(m["root"], 1)
            step(dve.reciprocal(stat[:, 0:24], stat[:, 32:56]))
            step(dve.tensor_scalar(stat[:, 16:24], stat[:, 16:24], 1.0 - LAMBDA_INIT, None, ALU.mult))
            for tt in range(TT):
                v = proj[:, tt, XC:XC + D_CONV].rearrange("p (a n) -> p a n", n=D_CONV // 8)
                r = stat[:, 8 * tt:8 * tt + 8].rearrange("p (a o) -> p a o", o=1).to_broadcast([P, 8, D_CONV // 8])
                step(dve.tensor_tensor(v, v, r, ALU.mult))
                dve.tensor_tensor(h[:, tt, 0:D_CONV], proj[:, tt, XC:XC + D_CONV], conv_gain, ALU.mult)
                for hd in range(DA_HEADS):
                    c = slice(hd * DA_V, (hd + 1) * DA_V)
                    n = 16 + 4 * tt + hd
                    ins = dve.scalar_tensor_tensor(h[:, tt, D_CONV + hd * DA_V:D_CONV + (hd + 1) * DA_V],
                                                   banks(6 + tt)[:, c], stat[:, n:n + 1], sub_gain, ALU.mult, ALU.mult)
                ins.then_inc(h_ready, 1)
            turn_dve(dve, MIX_TURN)
            out_dve(dve, "mix_out")

        def mix_pool(pool, step):
            pool.wait_ge(x_ready, X_COUNT[5] + 2)
            loads = [(conv_w, t["conv_w_2"][0].rearrange("k n -> (k n)")), (conv_gain, t["conv_out_g_2"][0]),
                     (qk_gain[:, 0:64], t["q_norm_g_2"][0]), (qk_gain[:, 64:128], t["k_norm_g_2"][0]),
                     (sub_gain, t["attn_subln_g_2"][0])]
            loads += [(lam_in[:, 64 * i:64 * i + 64], t[f"lambda_{n}_2"][0]) for i, n in enumerate(("q1", "q2", "k1", "k2"))]
            for dst, src in loads:
                pool.dma_start(dst, src.partition_broadcast(P)).then_inc(mix_loaded, 16)

        def mix_conv_pool(pool, step):
            pool.wait_ge(m["u"], 1)
            pool.dma_start(conv_rows[CONV_W - 1:, :].rearrange("(a p) n -> p a n", p=P), both(XC, D_CONV)).then_inc(m["stored"], 16)
            pool.wait_ge(m["stored"], 16)
            pool.wait_ge(m["zeros"], 16)
            for i in range(2):
                pool.dma_start(by_tile(shifted[i]), conv_rows[1 - i:1 - i + TOKENS, :].rearrange("(a p) n -> p a n", p=P)
                               ).then_inc(m["shifted"], 16)
            pool.wait_ge(m["shifted"], 32)
            pool.wait_ge(mix_loaded, 9 * 16)

            def weight(i):
                return conv_w[:, i * D_CONV:(i + 1) * D_CONV].rearrange("p (o n) -> p o n", o=1).to_broadcast([P, TT, D_CONV])
            acc = both(XC, D_CONV)
            pool.tensor_tensor(acc, acc, weight(2), ALU.mult)
            pool.tensor_tensor(by_tile(shifted[0]), by_tile(shifted[0]), weight(1), ALU.mult)
            step(pool.tensor_tensor(by_tile(shifted[1]), by_tile(shifted[1]), weight(0), ALU.mult))
            step(pool.tensor_tensor(acc, acc, by_tile(shifted[0]), ALU.add))
            step(pool.tensor_tensor(acc, acc, by_tile(shifted[1]), ALU.add))
            pool.tensor_tensor(acc, acc, both(BG, D_CONV), ALU.mult).then_inc(m["conv"], 1)

        pa = proj[:, :, :].rearrange("p a n -> p (a n)")
        taken = [0]

        def take(n, dt=F32):
            taken[0] += n
            assert taken[0] <= TT * GLA_COLS
            v = pa[:, taken[0] - n:taken[0]]
            return v if dt is F32 else v.bitcast(dt)
        iota = take(SLOTS)
        token = take(TT)
        logits = take(TT * (GROUPS + EXPERTS))
        group_pad, group_top, group_at = take(TT * 8), take(TT * 8), take(TT * 8, U32)
        group, group_off = take(TT), take(TT)
        group_exp, group_gate = take(TT * GROUPS), take(TT)
        group_hot, group_pick, mine = take(TT * GROUPS), take(TT * EXPERTS), take(TT * PER_GROUP)
        top, top_at, pick = take(TT * 8), take(TT * 8, U32), take(TT * 2)
        gap, gap_exp, share = take(TT), take(TT), take(2 * TT)
        takes, takes_any = take(2 * TT * EXPERTS), take(TT * EXPERTS)
        counts = take(3 * EXPERTS)
        count, rank = counts[:, 0:EXPERTS], counts[:, EXPERTS:]
        over, over_to, over_from, tile_base = take(EXPERTS), take(EXPERTS), take(EXPERTS), take(EXPERTS)
        tile_no, place_in, item = take(TT * EXPERTS), take(TT * EXPERTS), take(TT * EXPERTS)
        chosen = take(2 * TT * EXPERTS)
        item_of, place_of, slot_of = take(2 * TT), take(2 * TT), take(2 * TT)
        slot_index = take(2 * TT, I32)
        hot_place, hot_item = take(2 * TT * SLOTS), take(2 * TT * ITEM_COLS)
        index, x_index = take(ITEM_COLS, I32), take(1, I32)
        over_expert, over_test = take(MAX_OVER * EXPERTS), take(MAX_OVER * EXPERTS)
        plan_f, plan = take(1 + ITEMS), take(1 + ITEMS, I32)
        x_rows, y_sb = scratch[:, 0:D], scratch[:, D:2 * D]
        picked_rows = [scratch[:, (2 + q) * D:(3 + q) * D] for q in range(2 * TT)]
        ROUTE = banks(6)
        CNT, IDX = TT * (GROUPS + EXPERTS), 256
        experts = [t[f"w_exp_{n}_2"].rearrange("o g e k n -> (o g e) k n") for n in ("gate", "up", "down")]
        XT = [b[:, :, 0:P] for b in (hT_high, hT_low)]
        AT = [flat(b).rearrange("p (f n) -> p f n", f=4) for b in (aT_high, aT_low)]
        MOE = FIRST_PIECE["experts"]
        BODY = MOE + 4

        def k_of(v, k):
            return v[:, k * TT:(k + 1) * TT]

        def route_dve(dve, step):
            dve.wait_ge(e["iota"], 1)
            dve.memset(group_pad, -3e38)
            dve.memset(plan_f, 0.0)
            dve.wait_ge(e["logits"], 1)
            step(dve.tensor_copy(logits, ROUTE[:, 0:CNT]))
            lg = by_tile(logits)
            step(dve.tensor_copy(by_tile(group_pad)[:, :, 0:GROUPS], lg[:, :, 0:GROUPS]))
            for tt in range(TT):
                c = slice(8 * tt, 8 * tt + 8)
                step(dve.max(group_top[:, c], group_pad[:, c]))
                ins = dve.max_index(group_at[:, c], group_top[:, c], group_pad[:, c])
            step(ins)
            highest = by_tile(group_top)[:, :, 0:1]
            dve.tensor_tensor(by_tile(group_exp), lg[:, :, 0:GROUPS], highest.to_broadcast([P, TT, GROUPS]),
                              ALU.subtract).then_inc(e["gexp_in"], 1)
            step(dve.tensor_copy(group, by_tile(group_at)[:, :, 0]))
            dve.tensor_scalar(group_off, group, float(PER_GROUP), None, ALU.mult)
            for tt in range(TT):
                ins = dve.tensor_scalar(group_hot[:, GROUPS * tt:GROUPS * (tt + 1)], iota[:, 0:GROUPS], group[:, tt:tt + 1],
                                        None, ALU.is_equal)
            step(ins)
            for tt in range(TT):
                hot = group_hot[:, GROUPS * tt:GROUPS * (tt + 1)].rearrange("p (g o) -> p g o", o=1)
                ins = dve.tensor_tensor(group_pick[:, EXPERTS * tt:EXPERTS * (tt + 1)].rearrange("p (g e) -> p g e", g=GROUPS),
                                        lg[:, tt, GROUPS:].rearrange("p (g e) -> p g e", g=GROUPS),
                                        hot.to_broadcast([P, GROUPS, PER_GROUP]), ALU.mult)
            step(ins)
            step(dve.tensor_reduce(by_tile(mine), group_pick.rearrange("p (a g e) -> p a e g", a=TT, g=GROUPS), AX, ALU.add))
            for tt in range(TT):
                c = slice(8 * tt, 8 * tt + 8)
                step(dve.max(top[:, c], mine[:, c]))
                ins = dve.max_index(top_at[:, c], top[:, c], mine[:, c])
            step(ins)
            step(dve.tensor_copy(pick.rearrange("p (k a) -> p a k", k=2), by_tile(top_at)[:, :, 0:2]))
            dve.tensor_tensor(gap, by_tile(top)[:, :, 1], by_tile(top)[:, :, 0], ALU.subtract).then_inc(e["gexp_in"], 1)
            for k in range(2):
                ins = dve.tensor_tensor(k_of(pick, k), k_of(pick, k), group_off, ALU.add)
            step(ins)
            for k in range(2):
                for tt in range(TT):
                    q = k * TT + tt
                    ins = dve.tensor_scalar(takes[:, q * EXPERTS:(q + 1) * EXPERTS], iota[:, 0:EXPERTS], pick[:, q:q + 1], None,
                                            ALU.is_equal)
            step(ins)
            half = TT * EXPERTS
            dve.tensor_tensor(takes_any, takes[:, 0:half], takes[:, half:], ALU.add).then_inc(e["picked"], 1)
            dve.wait_ge(e["gexp"], 2)
            step(dve.tensor_reduce(group_gate, by_tile(group_exp), AX, ALU.add))
            dve.reciprocal(group_gate, group_gate)
            step(dve.tensor_scalar(share[:, 0:TT], gap_exp, 1.0, None, ALU.add))
            step(dve.reciprocal(share[:, 0:TT], share[:, 0:TT]))
            step(dve.tensor_tensor(share[:, 0:TT], share[:, 0:TT], group_gate, ALU.mult))
            step(dve.tensor_tensor(share[:, TT:], share[:, 0:TT], gap_exp, ALU.mult))
            dve.wait_ge(e["ranks"], 1)
            step(dve.tensor_copy(counts, ROUTE[:, CNT:CNT + 3 * EXPERTS]))
            for dst, src, edge in ((over, count, 0.5), (tile_no, rank, -0.5)):
                step(dve.tensor_scalar(dst, src, SLOTS + edge, None, ALU.is_gt))
                for n in range(2, MAX_TILES):
                    step(dve.scalar_tensor_tensor(dst, src, n * SLOTS + edge, dst, ALU.is_gt, ALU.add))
            step(dve.tensor_tensor_scan(over_to, ones[:, 0:EXPERTS], over, 0.0, ALU.mult, ALU.add))
            step(dve.tensor_tensor(over_from, over_to, over, ALU.subtract))
            dve.scalar_tensor_tensor(place_in, tile_no, -float(SLOTS), rank, ALU.mult, ALU.add)
            step(dve.tensor_tensor(tile_base, over_from, iota[:, 0:EXPERTS], ALU.subtract))
            step(dve.tensor_scalar(tile_base, tile_base, EXPERTS - 1.0, None, ALU.add))

            def per_tile(v):
                return v.rearrange("p (o n) -> p o n", o=1).to_broadcast([P, TT, EXPERTS])
            step(dve.tensor_tensor(by_tile(item), by_tile(tile_no), per_tile(tile_base), ALU.add))
            step(dve.scalar_tensor_tensor(item, tile_no, 0.0, item, ALU.is_gt, ALU.mult))
            step(dve.tensor_tensor(by_tile(item), by_tile(item), per_tile(iota[:, 0:EXPERTS]), ALU.add))
            for table, of in ((item, item_of), (place_in, place_of)):
                step(dve.tensor_tensor(chosen.rearrange("p (k n) -> p k n", k=2), takes.rearrange("p (k n) -> p k n", k=2),
                                       table.rearrange("p (o n) -> p o n", o=1).to_broadcast([P, 2, half]), ALU.mult))
                step(dve.tensor_reduce(of, chosen.rearrange("p (q n) -> p q n", n=EXPERTS), AX, ALU.add))
            step(dve.scalar_tensor_tensor(slot_of, item_of, float(SLOTS), place_of, ALU.mult, ALU.add))
            dve.tensor_copy(slot_index, slot_of)
            for q in range(2 * TT):
                dve.tensor_scalar(hot_place[:, q * SLOTS:(q + 1) * SLOTS], iota, place_of[:, q:q + 1], None, ALU.is_equal)
                ins = dve.tensor_scalar(hot_item[:, q * ITEM_COLS:(q + 1) * ITEM_COLS], iota[:, 0:ITEM_COLS],
                                        item_of[:, q:q + 1], token[:, q % TT:q % TT + 1], ALU.is_equal, ALU.mult)
            ins.then_inc(e["maps"], 1)
            n = MAX_OVER

            def grid(v):
                return v.rearrange("p (j n) -> p j n", j=n)

            def along(v):
                return v.rearrange("p (o n) -> p o n", o=1).to_broadcast([P, n, EXPERTS])
            j = iota[:, 0:n].rearrange("p (j o) -> p j o", o=1).to_broadcast([P, n, EXPERTS])
            dve.tensor_tensor(grid(over_expert), along(over_from), j, ALU.is_le)
            step(dve.tensor_tensor(grid(over_test), along(over_to), j, ALU.is_gt))
            step(dve.tensor_tensor(over_expert, over_expert, over_test, ALU.mult))
            step(dve.tensor_tensor(grid(over_expert), grid(over_expert), along(iota[:, 0:EXPERTS]), ALU.mult))
            dve.tensor_reduce(plan_f[:, 1 + EXPERTS:], grid(over_expert), AX, ALU.add)
            dve.tensor_copy(plan_f[:, 1:1 + EXPERTS], iota[:, 0:EXPERTS])
            step(dve.tensor_scalar(plan_f[:, 0:1], over_to[:, EXPERTS - 1:EXPERTS], EXPERTS - 1.0, None, ALU.add))
            dve.tensor_copy(plan, plan_f).then_inc(e["plan"], 1)
            dve.wait_ge(e["index"], 1)
            step(dve.tensor_copy(index[0:SLOTS, :], ROUTE[0:SLOTS, IDX:IDX + ITEM_COLS]))
            dve.tensor_copy(x_index[0:SLOTS, :], index[0:SLOTS, 0:1]).then_inc(e["x_index"], 1)

        def route_pe(pe):
            turn_pe(pe, TURN_OF_NORM[8], "n8")
            pe.wait_ge(turn_low, 4 * (TURN_OF_NORM[8] + 1))
            n = GROUPS + EXPERTS
            for tt in range(TT):
                for k in range(KD):
                    tok = slice(tt * P, (tt + 1) * P)
                    ins = product(pe, ROUTE[:, tt * n:(tt + 1) * n], hT_high[:, k, tok], hT_low[:, k, tok],
                                  router_high[:, k, :], router_low[:, k, :], start=tt == 0 and k == 0)
            ins.then_inc(e["logits"], 1)
            pe.wait_ge(e["picked"], 1)
            a = [takes_any[:, tt * EXPERTS:(tt + 1) * EXPERTS] for tt in range(TT)]
            for c, terms in enumerate((((ones[:, 0:P], a[0]), (ones[:, 0:P], a[1])), ((strict[:, :], a[0]),),
                                       ((ones[:, 0:P], a[0]), (strict[:, :], a[1])))):
                for i, (lhs, rhs) in enumerate(terms):
                    ins = pe.matmul(ROUTE[:, CNT + c * EXPERTS:CNT + (c + 1) * EXPERTS], lhs, rhs, start=c == 0 and i == 0,
                                    stop=i == len(terms) - 1, skip_group_check=True)
            ins.then_inc(e["ranks"], 1)
            pe.wait_ge(e["maps"], 1)
            for q in range(2 * TT):
                ins = pe.matmul(ROUTE[0:SLOTS, IDX:IDX + ITEM_COLS], hot_place[:, q * SLOTS:(q + 1) * SLOTS],
                                hot_item[:, q * ITEM_COLS:(q + 1) * ITEM_COLS], start=q == 0, stop=q == 2 * TT - 1,
                                skip_group_check=True)
            ins.then_inc(e["index"], 1)

        def rounds(eng):
            eng.wait_ge(e["plan"], 1)
            return eng.value_load(plan[0:1, 0:1], min_val=EXPERTS - 1, max_val=ITEMS - 1)

        def expert_gate_up_loads(sp, p, r, expert):
            for j in range(4):
                piece_loads(sp, p + j, r, gate_up_parts(p + j, experts[0][expert], experts[1][expert], j % 2, (j // 2) * CHUNK))

        def expert_down_loads(sp, p, r, expert):
            for j in range(2):
                piece_loads(sp, p + j, r, down_parts(p + j, experts[2][expert], j * 2 * P))

        def moe_sp(sp):
            expert_gate_up_loads(sp, MOE, 0, 0)
            n = rounds(sp)

            def expert_of(i):
                return sp.value_load(plan[0:1, bass.ds(i + 1, 1)], min_val=0, max_val=EXPERTS - 1)
            with sp.Fori(0, n) as i:
                expert_gate_up_loads(sp, BODY, i * 2, expert_of(i + 1))
                expert_down_loads(sp, BODY + 4, i * 2, expert_of(i))
            expert_down_loads(sp, BODY, n * 2, expert_of(n))

        def moe_pool(pool):
            pool.wait_ge(h_ready, 2 * H_ORDER.index("n8") + TT)
            pool.dma_start(h_rows.rearrange("(a p) n -> p a n", p=P), h[:, :, :]).then_inc(e["h_stored"], 16)
            pool.wait_ge(e["logits"], 1)
            for b in XT:
                pool.memset(b[:, :, SLOTS:].bitcast(F32), 0.0)
            for b in AT:
                ins = pool.memset(b[:, :, SLOTS:].bitcast(F32), 0.0)
            ins.then_inc(e["cleared"], 1)
            pool.wait_ge(e["h_stored"], 16)
            n = rounds(pool)

            def gather(i):
                pool.wait_ge(e["x_index"], i + 1)
                if not isinstance(i, int) or i:
                    pool.wait_ge(e["x_turned"], i)
                pool.sem_inc(e["pool_passed"], 1)
                pool.indirect_dma_start(out=x_rows[0:SLOTS, :], out_offset=None, in_=h_rows,
                                        in_offset=bass.IndirectOffsetOnAxis(ap=x_index[0:SLOTS, 0:1], axis=0)
                                        ).then_inc(e["x_landed"], 16)

            def store(i):
                pool.wait_ge(e["y_sb"], i + 1)
                pool.dma_start(y_rows[bass.ds(i * SLOTS, SLOTS), :], y_sb[0:SLOTS, :]).then_inc(e["y_stored"], 16)

            gather(0)
            gather(1)
            with pool.Fori(0, n) as i:
                gather(i + 2)
                store(i)
            store(n)
            pool.wait_ge(e["padded"], 16)
            pool.wait_ge(e["y_stored"], n * 16 + 16)
            pool.sem_inc(e["pool_passed"], 1)
            for q in range(2 * TT):
                pool.indirect_dma_start(out=picked_rows[q], out_offset=None, in_=y_rows,
                                        in_offset=bass.IndirectOffsetOnAxis(ap=slot_index[:, q:q + 1], axis=0)
                                        ).then_inc(e["picks"], 16)

        def moe_pe(pe):
            route_pe(pe)
            pe.wait_ge(e["cleared"], 1)

            def turn_rows(i):
                pe.wait_ge(e["x_landed"], (i + 1) * 16)
                pe.sem_inc(e["pe_passed"], 1)
                for k in range(KD):
                    ins = pe.transpose(TURN_X[:, k * SLOTS:(k + 1) * SLOTS], x_rows[0:SLOTS, k * P:(k + 1) * P],
                                       ident[0:SLOTS, 0:SLOTS])
                ins.then_inc(e["x_turned"], 1)

            def gate_up(p, r, i):
                pe.wait_ge(e["x_low"], i + 1)
                for j in range(4):
                    q = p + j
                    pe.wait_ge(split, q + 1 + scales_with(r, 3))
                    for k in range(4):
                        kk = 4 * (j % 2) + k
                        ins = product(pe, GU[j // 2], XT[0][:, kk, :], XT[1][:, kk, :], four_k(high, q)[:, k, :],
                                      four_k(low, q)[:, k, :], start=kk == 0, stop=kk == KD - 1)
                    ins.then_inc(used, 1)

            def turn_inner(i):
                pe.wait_ge(e["act"], i * 2 + 2)
                pe.sem_inc(e["pe_passed"], 1)
                for f in range(4):
                    ins = pe.transpose(TURN_A[:, f * SLOTS:(f + 1) * SLOTS], act_tok[0:SLOTS, f // 2, (f % 2) * P:(f % 2 + 1) * P],
                                       ident[0:SLOTS, 0:SLOTS])
                ins.then_inc(e["a_turned"], 1)

            def down(p, r, i):
                pe.wait_ge(e["a_low"], i + 1)
                pe.wait_ge(e["y_sb"], i)
                for j in range(2):
                    q = p + j
                    pe.wait_ge(split, q + 1 + scales_with(r, 3))
                    for k in range(2):
                        f = 2 * j + k
                        for c in range(2):
                            cols = slice(c * BANK, (c + 1) * BANK)
                            ins = product(pe, Y[0][:, cols], AT[0][:, f, :], AT[1][:, f, :], two_k(high, q)[:, k, cols],
                                          two_k(low, q)[:, k, cols], start=f == 0, stop=f == 3)
                    ins.then_inc(used, 1)

            n = rounds(pe)
            turn_rows(0)
            gate_up(MOE, 0, 0)
            with pe.Fori(0, n) as i:
                turn_inner(i)
                turn_rows(i + 1)
                gate_up(BODY, i * 2, i + 1)
                down(BODY + 4, i * 2, i)
            turn_inner(n)
            down(BODY, n * 2, n)

        slots_x = TURN_X.rearrange("p (k n) -> p k n", n=SLOTS)
        slots_a = TURN_A[:, 0:4 * SLOTS].rearrange("p (k n) -> p k n", n=SLOTS)

        def moe_act(act):
            act.wait_ge(e["gexp_in"], 1)
            act.activation(group_exp, group_exp, ACT.Exp).then_inc(e["gexp"], 1)
            act.wait_ge(e["gexp_in"], 2)
            act.activation(gap_exp, gap, ACT.Exp).then_inc(e["gexp"], 1)
            n = rounds(act)

            def inner_high(i):
                act.wait_ge(e["a_turned"], i + 1)
                act.activation(AT[0][:, :, 0:SLOTS], slots_a, ACT.Copy).then_inc(e["a_high"], 1)

            def rows_high(i):
                act.wait_ge(e["x_turned"], i + 1)
                act.activation(XT[0][:, :, 0:SLOTS], slots_x, ACT.Copy).then_inc(e["x_high"], 1)

            def silu(chunk, used_value):
                act.wait_ge(used, used_value)
                act.activation(gate[0:SLOTS, chunk, :], GU[chunk][0:SLOTS, 0:CHUNK], ACT.Silu).then_inc(e["silu"], 1)

            def result(i, used_value):
                act.wait_ge(used, used_value)
                if not isinstance(i, int) or i:
                    act.wait_ge(e["y_stored"], i * 16)
                act.activation(y_sb[0:SLOTS, :], Y[0][0:SLOTS, :], ACT.Copy).then_inc(e["y_sb"], 1)

            rows_high(0)
            round_piece(act, MOE + 2)
            round_piece(act, MOE + 3)
            silu(0, MOE + 2)
            round_piece(act, BODY)
            round_piece(act, BODY + 1)
            silu(1, MOE + 4)
            with act.Fori(0, n) as i:
                r = i * 2
                inner_high(i)
                rows_high(i + 1)
                round_piece(act, BODY + 2, r)
                round_piece(act, BODY + 3, r)
                silu(0, i * 6 + (BODY + 2))
                round_piece(act, BODY + 4, r)
                round_piece(act, BODY + 5, r)
                silu(1, i * 6 + (BODY + 4))
                round_piece(act, BODY + 6, r)
                round_piece(act, BODY + 7, r)
                result(i, i * 6 + (BODY + 6))
            inner_high(n)
            result(n, n * 6 + (BODY + 2))

        def moe_dve(dve, step):
            route_dve(dve, step)
            n = rounds(dve)

            def inner_low(i):
                dve.wait_ge(e["a_high"], i + 1)
                dve.tensor_tensor(AT[1][:, :, 0:SLOTS], slots_a, AT[0][:, :, 0:SLOTS].bitcast(F32),
                                  ALU.subtract).then_inc(e["a_low"], 1)

            def rows_low(i):
                dve.wait_ge(e["x_high"], i + 1)
                dve.tensor_tensor(XT[1][:, :, 0:SLOTS], slots_x, XT[0][:, :, 0:SLOTS].bitcast(F32),
                                  ALU.subtract).then_inc(e["x_low"], 1)

            def next_index(i):
                dve.wait_ge(e["x_landed"], i * 16)
                dve.tensor_copy(x_index[0:SLOTS, :], index[0:SLOTS, bass.ds(i, 1)]).then_inc(e["x_index"], 1)

            def inner(chunk, count):
                dve.wait_ge(e["silu"], count)
                dve.tensor_tensor(act_tok[0:SLOTS, chunk, :], gate[0:SLOTS, chunk, :], GU[chunk][0:SLOTS, CHUNK:2 * CHUNK],
                                  ALU.mult).then_inc(e["act"], 1)

            next_index(1)
            rows_low(0)
            split_piece(dve, MOE + 2)
            split_piece(dve, MOE + 3)
            inner(0, 1)
            split_piece(dve, BODY)
            split_piece(dve, BODY + 1)
            inner(1, 2)
            with dve.Fori(0, n) as i:
                r = i * 2
                inner_low(i)
                rows_low(i + 1)
                next_index(i + 2)
                split_piece(dve, BODY + 2, r)
                split_piece(dve, BODY + 3, r)
                inner(0, i * 2 + 3)
                split_piece(dve, BODY + 4, r)
                split_piece(dve, BODY + 5, r)
                inner(1, i * 2 + 4)
                split_piece(dve, BODY + 6, r)
                split_piece(dve, BODY + 7, r)
            inner_low(n)
            dve.wait_ge(e["picks"], 2 * TT * 16)
            for k in range(2):
                for tt in range(TT):
                    q = k * TT + tt
                    ins = dve.scalar_tensor_tensor(x[:, tt, :], picked_rows[q], share[:, q:q + 1], x[:, tt, :], ALU.mult,
                                                   ALU.add)
                if k == 0:
                    step(ins)
            ins.then_inc(final, 1)

        block = ctx.enter_context(nc.Block())

        @block.sync
        def _(sp):
            sp.dma_start(x[:, :, :], t["x"][0].rearrange("(a p) n -> p a n", p=P)).then_inc(x_loaded, 16)
            ffn_loads(sp, 0)
            if STOP == "ffn0":
                for half in range(2):
                    piece_loads(sp, 33+half, 0, in_parts(33+half, w_in["gla_in"], half, 0))
                return
            in_loads(sp, "gla_in")
            out_loads(sp, "gla_out")
            if STOP == "gla":
                b = FIRST_PIECE["ffn1"]
                for half in range(2):
                    piece_loads(sp, b + half, 0, gate_up_parts(b + half, ffns[1][0], ffns[1][1], half, 0))
                return
            ffn_loads(sp, 1)
            ffn_loads(sp, 2)
            in_loads(sp, "sb_in")
            out_loads(sp, "sb_out")
            ffn_loads(sp, 3)
            in_loads(sp, "mix_in")
            out_loads(sp, "mix_out")
            if STOP == "mix":
                b = FIRST_PIECE["experts"]
                for half in range(2):
                    piece_loads(sp, b + half, 0, gate_up_parts(b + half, ffns[1][0], ffns[1][1], half, 0))
                return
            moe_sp(sp)
            sp.wait_ge(final, 1)
            sp.dma_start(out[0].rearrange("(a p) n -> p a n", p=P), x[:, :, :]).then_inc(stored_out, 16)
            sp.wait_ge(stored_out, 16)

        @block.gpsimd
        def _(pool):
            n_steps = [0]

            def step(ins):
                n_steps[0] += 1
                ins.then_inc(pool_step, 1)
                pool.wait_ge(pool_step, n_steps[0])

            def select(v, op, fill, base, pattern, by_partition):
                step(nc.gpsimd.affine_select(out=v, in_=v, compare_op=op, fill=fill, base=base, pattern=pattern,
                                             channel_multiplier=by_partition))

            for k in range(2):
                pool.dma_start(gain[:, k, :], gains[k].partition_broadcast(P)).then_inc(gain_loaded[k], 16)
            pool.dma_start(wgk2[:, :], t["gla_w_gk2"][0]).then_inc(small_loaded, 16)
            pool.dma_start(bgk[:, :], t["gla_b_gk"][0].rearrange("(a p) -> p a", p=P),
                           allow_slow_non_contiguous=True).then_inc(small_loaded, 16)
            pool.dma_start(gla_gain[:, :], t["gla_o_norm"][0].partition_broadcast(P)).then_inc(small_loaded, 16)
            pool.dma_start(gkw[:, :, :], t["gla_w_in"][0][:, IN_CHUNKS * BANK:].rearrange("(k p) n -> p k n", p=P)
                           ).then_inc(small_loaded, 16)
            for dst, src in ((router[:, :, 0:GROUPS], t["w_router_group_2"]), (router[:, :, GROUPS:], t["w_router_expert_2"])):
                pool.dma_start(dst, src[0].rearrange("(k p) n -> p k n", p=P)).then_inc(small_loaded, 16)
            pool.memset(eps[:, :], EPS).then_inc(eps_set, 1)
            pool.memset(ident[:, :], 0.0)
            pool.memset(zero_r[:, :].bitcast(F32), 0.0)
            pool.memset(ones[:, :], 1.0)
            pool.memset(suffix[:, :], 1.0)
            pool.memset(strict[:, :], 1.0)
            pool.memset(levels[:, :, :], 0.0)
            step(pool.memset(causal[:, :], 0.0))
            select(ident[:, :], ALU.not_equal, 1.0, 0, [[-1, P]], 1)
            pool.dma_start(conv_rows[0:CONV_W - 1, :], zero_r[0:CONV_W - 1, :].bitcast(F32)).then_inc(m["zeros"], 16)
            rows = y_rows[EXPERTS * SLOTS:, :].rearrange("r n -> (r n)").rearrange("(j p n) -> p j n", p=P, n=BANK)
            pool.dma_start(rows, zero_r[:, :].bitcast(F32).rearrange("p (j n) -> p j n", j=1).to_broadcast(
                [P, MAX_OVER, BANK])).then_inc(e["padded"], 16)
            select(suffix[:, :], ALU.is_ge, 0.0, 0, [[-1, P]], 1)
            select(strict[:, :], ALU.is_gt, 0.0, 0, [[1, P]], -1)
            for c in (0, 2):
                select(causal[:, c * P:(c + 1) * P], ALU.is_ge, NEG, 0, [[-1, P]], 1)
            for j, B in enumerate(LEVELS):
                n = P // (2 * B)
                late = levels[:, j, :].rearrange("p (m n) -> p m n", n=2 * B)[:, :, B:2 * B]
                step(pool.memset(late, 1.0))
                select(late, ALU.is_ge, 0.0, 0, [[-2 * B, n], [0, B]], 1)
                select(late, ALU.is_ge, 0.0, B - 1, [[2 * B, n], [0, B]], -1)
            pool.memset(gscore, 0.0).then_inc(consts, 1)
            for k in range(2, 9):
                if k - 2 != 6:
                    pool.wait_ge(h_ready, 2 * H_ORDER.index(f"n{k - 2}") + 2)
                else:
                    pool.wait_ge(x_ready, 14)
                pool.dma_start(gain[:, k % 2, :], gains[k].partition_broadcast(P)).then_inc(gain_loaded[k % 2], 16)
                if STOP == "gla" and k == 3: return
                if STOP == "ffn0" and k == 2: return
                if k == 7:
                    mix_pool(pool, step)
            mix_conv_pool(pool, step)
            if STOP == "mix": return
            pool.wait_ge(x_ready, X_COUNT[8] + 2)
            pool.iota(iota, pattern=[[1, SLOTS]], base=0, channel_multiplier=0, allow_small_or_imprecise_dtypes=True)
            pool.iota(token, pattern=[[P, TT]], base=0, channel_multiplier=1,
                      allow_small_or_imprecise_dtypes=True).then_inc(e["iota"], 1)
            moe_pool(pool)

        @block.scalar
        def _(act):
            n_steps = [0]

            def step(ins):
                n_steps[0] += 1
                ins.then_inc(act_step, 1)
                act.wait_ge(act_step, n_steps[0])

            round_piece(act, 0)
            round_piece(act, 1)
            norm_act(act, 0)
            turn_act(act, 0)
            ffn_act(act, 0)
            norm_act(act, 1)
            if STOP == "ffn0": return
            act.wait_ge(small_loaded, 96)
            act.activation(flat(router_high), flat(router), ACT.Copy)
            act.activation(flat(gkw_high), flat(gkw), ACT.Copy).then_inc(small_high, 1)
            turn_act(act, 1)
            act.wait_ge(g["rank"], 1)
            act.activation(grank, TURN_A[:, 0:TT * GLA_RANK], ACT.Copy).then_inc(g["rank_sb"], 1)
            gla_act(act, step)
            norm_act(act, 2)
            if STOP == "gla": return
            turn_act(act, TURN_OF_NORM[2])
            ffn_act(act, 1)
            norm_act(act, 3)
            turn_act(act, TURN_OF_NORM[3])
            ffn_act(act, 2)
            norm_act(act, 4)
            turn_act(act, TURN_OF_NORM[4])
            sb_act(act, step)
            norm_act(act, 5)
            turn_act(act, TURN_OF_NORM[5])
            ffn_act(act, 3)
            norm_act(act, 6)
            norm_act(act, 7)
            turn_act(act, TURN_OF_NORM[7])
            mix_act(act, step)
            norm_act(act, 8)
            if STOP == "mix": return
            turn_act(act, TURN_OF_NORM[8])
            moe_act(act)

        @block.vector
        def _(dve):
            n_steps = [0]

            def step(ins):
                n_steps[0] += 1
                ins.then_inc(dve_step, 1)
                dve.wait_ge(dve_step, n_steps[0])

            split_piece(dve, 0)
            split_piece(dve, 1)
            norm_dve(dve, step, 0, 0, None)
            turn_dve(dve, 0)
            ffn_dve(dve, 0)
            norm_dve(dve, step, 1, 0.5, FIRST_PIECE["gla_in"] - 1)
            if STOP == "ffn0": return
            dve.wait_ge(small_high, 1)
            dve.tensor_tensor(flat(router_low), flat(router), flat(router_high).bitcast(F32), ALU.subtract)
            dve.tensor_tensor(flat(gkw_low), flat(gkw), flat(gkw_high).bitcast(F32), ALU.subtract).then_inc(small_low, 1)
            turn_dve(dve, 1)
            gla_dve(dve, step)
            norm_dve(dve, step, 2, 1.0, FIRST_PIECE["ffn1"] - 1)
            if STOP == "gla": return
            turn_dve(dve, TURN_OF_NORM[2])
            ffn_dve(dve, 1)
            norm_dve(dve, step, 3, 0.5, FIRST_PIECE["ffn2"] - 1)
            turn_dve(dve, TURN_OF_NORM[3])
            ffn_dve(dve, 2)
            norm_dve(dve, step, 4, 0.5, FIRST_PIECE["sb_in"] - 1)
            turn_dve(dve, TURN_OF_NORM[4])
            sb_dve(dve, step)
            norm_dve(dve, step, 5, 1.0, FIRST_PIECE["ffn3"] - 1)
            turn_dve(dve, TURN_OF_NORM[5])
            ffn_dve(dve, 3)
            norm_dve(dve, step, 6, 0.5, FIRST_PIECE["mix_in"] - 1)
            norm_dve(dve, step, 7, 0, None)
            turn_dve(dve, TURN_OF_NORM[7])
            mix_dve(dve, step)
            norm_dve(dve, step, 8, 1.0, FIRST_PIECE["experts"] - 1)
            if STOP == "mix": return
            turn_dve(dve, TURN_OF_NORM[8])
            moe_dve(dve, step)

        @block.tensor
        def _(pe):
            turn_pe(pe, 0, "n0")
            ffn_pe(pe, 0, 0)
            if STOP == "ffn0": return
            turn_pe(pe, 1, "n1")
            gla_pe(pe)
            if STOP == "gla": return
            turn_pe(pe, TURN_OF_NORM[2], "n2")
            ffn_pe(pe, 1, TURN_OF_NORM[2])
            turn_pe(pe, TURN_OF_NORM[3], "n3")
            ffn_pe(pe, 2, TURN_OF_NORM[3])
            turn_pe(pe, TURN_OF_NORM[4], "n4")
            sb_pe(pe)
            turn_pe(pe, TURN_OF_NORM[5], "n5")
            ffn_pe(pe, 3, TURN_OF_NORM[5])
            turn_pe(pe, TURN_OF_NORM[7], "n7")
            mix_pe(pe)
            if STOP == "mix": return
            moe_pe(pe)


_INS = ["x", "ffn1_norm", "ffn1_w_gate", "ffn1_w_up", "ffn1_w_down", "mix_norm", "ffn2_norm", "ffn2_w_gate",
        "ffn2_w_up", "ffn2_w_down", "gla_w_in", "gla_w_gk2", "gla_b_gk", "gla_o_norm", "gla_w_out", "sb_w_in",
        "sb_w_out", "final_norm", "attn_norm_g_2", "w_in_2", "conv_w_2", "conv_out_g_2", "q_norm_g_2", "k_norm_g_2",
        "lambda_q1_2", "lambda_k1_2", "lambda_q2_2", "lambda_k2_2", "attn_subln_g_2", "w_out_2", "ffn_norm_g_2",
        "w_router_group_2", "w_router_expert_2", "w_exp_gate_2", "w_exp_up_2", "w_exp_down_2"]


def arrays_of(inputs):
    return {f"in_{n}": np.ascontiguousarray(inputs[n]) for n in _INS}


def declare_and_build(nc, arrays):
    t = {n: nc.dram_tensor(f"in_{n}", arrays[f"in_{n}"].shape, F32, kind="ExternalInput").ap() for n in _INS}
    out = nc.dram_tensor("out", (1, TOKENS, D), F32, kind="ExternalOutput").ap()
    build(nc, t, out)


def kernel(**inputs):
    import concourse.bacc as bacc
    from concourse.bass_utils import run_bass_kernel_spmd

    nc = bacc.Bacc("TRN2", target_bir_lowering=False, num_devices=1)
    arrays = arrays_of(inputs)
    declare_and_build(nc, arrays)
    result = run_bass_kernel_spmd(nc, [arrays], core_ids=[0])
    return result.results[0]["out"]
```

```python
from contextlib import ExitStack

import numpy as np

import concourse.bass as bass
from concourse import mybir

F32 = mybir.dt.float32
F32R = mybir.dt.float32r
I32 = mybir.dt.int32
U32 = mybir.dt.uint32
ALU = mybir.AluOpType
ACT = mybir.ActivationFunctionType
AX = mybir.AxisListType.X

P = 128
TOKENS = 256
TT = TOKENS // P
D = 1024
KD = D // P
EPS = 1e-6
BANK = 512
SLOT = 2048
RING = 3

D_FF = 2816
CHUNK = 256
N_CHUNKS = D_FF // CHUNK
FFN_PIECES = 3 * N_CHUNKS
IN_CHUNKS = 6
IN_PIECES = 2 * IN_CHUNKS
OUT_PIECES = 4
HALF_D = 512

GLA_HEADS, GLA_K, GLA_V, GLA_RANK = 4, 128, 256, 16
GLA_TAU = 16.0
GLA_COLS = IN_CHUNKS * BANK + GLA_RANK
LEVELS = [64, 32, 16, 8, 4, 2, 1]

SB_HEADS, SB_HD = 16, 64
GROUP = 4
SB_GROUPS = SB_HEADS // GROUP

DA_HEADS, DA_HD, DA_V = 4, 64, 128
D_CONV = 512
CONV_W = 3
LAMBDA_INIT = 0.8 - 0.6 * float(np.exp(-0.3 * 0))
NEG = -1e30

GROUPS, PER_GROUP, EXPERTS = 4, 8, 32
D_EXP = 512
SLOTS = 64
MAX_OVER = 2 * TOKENS // (SLOTS + 1)
MAX_TILES = TOKENS // SLOTS
ITEMS = EXPERTS + MAX_OVER
ITEM_COLS = ITEMS + 1

FIRST_PIECE = {}
_at = 0
for _name, _n in [("ffn0", FFN_PIECES), ("gla_in", IN_PIECES), ("gla_out", OUT_PIECES), ("ffn1", FFN_PIECES),
                  ("ffn2", FFN_PIECES), ("sb_in", IN_PIECES), ("sb_out", OUT_PIECES), ("ffn3", FFN_PIECES),
                  ("mix_in", IN_PIECES), ("mix_out", OUT_PIECES), ("experts", 0)]:
    FIRST_PIECE[_name] = _at
    _at += _n

STOP = None


def build(nc, t, out):
    ctx = ExitStack()
    with ctx:
        def sb(name, shape, dt=F32):
            return ctx.enter_context(nc.sbuf_tensor(name, shape, dt))

        def sem(name):
            return ctx.enter_context(nc.semaphore(name))

        raw = sb("raw", [P, RING, SLOT])
        high = sb("high", [P, RING, SLOT], F32R)
        low = sb("low", [P, RING, SLOT], F32R)
        hT_high = sb("hT_high", [P, KD, TOKENS], F32R)
        hT_low = sb("hT_low", [P, KD, TOKENS], F32R)
        aT_high = sb("aT_high", [P, 2, TOKENS], F32R)
        aT_low = sb("aT_low", [P, 2, TOKENS], F32R)
        zero_r = sb("zero_r", [P, BANK], F32R)
        x = sb("x", [P, TT, D])
        h = sb("h", [P, TT, D])
        gate = sb("gate", [P, TT, CHUNK])
        act_tok = sb("act_tok", [P, TT, CHUNK])
        gain = sb("gain", [P, 2, D])
        square = sb("square", [P, D])
        proj = sb("proj", [P, TT, GLA_COLS])
        stat = sb("stat", [P, 64])
        eps = sb("eps", [P, 1])
        ident = sb("ident", [P, P])
        ones = sb("ones", [P, TOKENS])
        suffix = sb("suffix", [P, P])
        strict = sb("strict", [P, P])
        causal = sb("causal", [P, 3 * P])
        levels = sb("levels", [P, len(LEVELS), P])
        wgk2 = sb("wgk2", [GLA_RANK, GLA_HEADS * GLA_K])
        bgk = sb("bgk", [P, GLA_HEADS])
        gla_gain = sb("gla_gain", [P, GLA_V])
        gkw = sb("gkw", [P, KD, GLA_RANK])
        gkw_high = sb("gkw_high", [P, KD, GLA_RANK], F32R)
        gkw_low = sb("gkw_low", [P, KD, GLA_RANK], F32R)
        router = sb("router", [P, KD, GROUPS + EXPERTS])
        router_high = sb("router_high", [P, KD, GROUPS + EXPERTS], F32R)
        router_low = sb("router_low", [P, KD, GROUPS + EXPERTS], F32R)
        SCRATCH = 10752
        scratch = sb("scratch", [P, SCRATCH])

        class Area:

            def __init__(self):
                self.at = 0

            def take(self, n):
                self.at += n
                assert self.at <= SCRATCH, self.at
                return scratch[:, self.at - n:self.at]

        psum = ctx.enter_context(nc.psum_tensor("psum", [P, 8, BANK], F32))

        def banks(a, n=1):
            return psum[:, a:a + n, :].rearrange("p b n -> p (b n)")

        Y = [banks(0, 2), banks(2, 2)]
        GU = [banks(4), banks(5)]
        TURN_A = banks(6)
        TURN_X = banks(7)

        conv_rows = nc.dram_tensor("conv_rows", (TOKENS + CONV_W - 1, D_CONV), F32, kind="Internal").ap()

        landed = [sem(f"landed{i}") for i in range(2 * RING)]
        rounded, split, used = sem("rounded"), sem("split"), sem("used")
        consts = sem("consts")
        pool_step, dve_step, act_step = sem("pool_step"), sem("dve_step"), sem("act_step")
        x_loaded, gain_loaded = sem("x_loaded"), [sem("gain_loaded0"), sem("gain_loaded1")]
        small_loaded, mix_loaded = sem("small_loaded"), sem("mix_loaded")
        small_high, small_low = sem("small_high"), sem("small_low")
        x_ready, squares, h_ready = sem("x_ready"), sem("squares"), sem("h_ready")
        roots, eps_set = sem("roots"), sem("eps_set")
        turned, turn_high, turn_low = sem("turned"), sem("turn_high"), sem("turn_low")
        gu_first, gate_ready, act_ready = sem("gu_first"), sem("gate_ready"), sem("act_ready")
        a_turned, a_high, a_low = sem("a_turned"), sem("a_high"), sem("a_low")
        in_first, in_copied = sem("in_first"), [sem("in_copied0"), sem("in_copied1")]
        g = {n: sem("gla_" + n) for n in ("rank", "rank_sb", "rankT", "rankT_sb", "z", "abs", "ln", "qkT", "q_sb",
                                          "k_sb", "diff", "decay", "scaled", "scores", "kept", "out", "sq", "silu", "summed", "roots")}
        s = {n: sem("sb_" + n) for n in ("qkT", "q_sb", "k_sb", "z", "z_sb", "ln", "sp", "sums", "arg", "exp", "w",
                                         "out", "out_sb", "even")}
        m = {n: sem("mix_" + n) for n in ("u", "zeros", "stored", "shifted", "qk", "qkT", "q_sb", "k_sb", "dots",
                                          "bias", "exp", "a", "aT", "aT_sb", "out", "sq", "lam", "lam_exp",
                                          "qk_sq", "qk_sum", "qk_root", "dots_sb", "conv", "sum", "root")}
        e = {n: sem("moe_" + n) for n in ("logits", "gexp_in", "gexp", "picked", "ranks", "slots", "slot_rows",
                                          "slot_rows_sb", "plan", "tables", "pick_parts", "picks", "x_turned",
                                          "x_high", "x_low", "gu_rest", "gu_sum", "shares", "share_sb", "silu", "act",
                                          "a_turned", "a_high", "a_low", "y_high", "y_low", "spread_parts", "spreads",
                                          "scattered", "pe_passed", "pool_passed")}
        final, stored_out = sem("final"), sem("stored_out")

        w_in = {"gla_in": t["gla_w_in"][0], "sb_in": t["sb_w_in"][0], "mix_in": t["w_in_2"][0]}
        w_out = {"gla_out": t["gla_w_out"][0], "sb_out": t["sb_w_out"][0], "mix_out": t["w_out_2"][0]}
        ffns = [(t[f"ffn{1 + i % 2}_w_gate"][i // 2], t[f"ffn{1 + i % 2}_w_up"][i // 2],
                 t[f"ffn{1 + i % 2}_w_down"][i // 2]) for i in range(4)]
        gains = [t["ffn1_norm"][0], t["mix_norm"][0], t["ffn2_norm"][0], t["ffn1_norm"][1], t["mix_norm"][1],
                 t["ffn2_norm"][1], t["final_norm"], t["attn_norm_g_2"][0], t["ffn_norm_g_2"][0]]
        TURN_OF_NORM = {0: 0, 1: 1, 2: 3, 3: 4, 4: 5, 5: 7, 7: 8, 8: 10}
        GLA_TURN, SB_TURN, MIX_TURN = 2, 6, 9
        H_ORDER = ["n0", "n1", "gla", "n2", "n3", "n4", "sb", "n5", "n7", "mix", "n8"]

        def scales_with(r, n):
            return 0 if isinstance(r, int) and r == 0 else r * n

        MOE = FIRST_PIECE["experts"]
        more_raw = scratch[:, SCRATCH - RING * SLOT:]

        def raw_of(p):
            if p < MOE or p % (2 * RING) < RING:
                return raw[:, p % RING, :]
            return more_raw[:, (p % RING) * SLOT:(p % RING + 1) * SLOT]

        def landed_of(p, r):
            if p < MOE:
                return landed[p % RING], 32 * (p // RING + 1) + scales_with(r, 32)
            before = MOE // RING if p % (2 * RING) < RING else 0
            return landed[p % (2 * RING)], 32 * (before + (p - MOE) // (2 * RING) + 1) + scales_with(r, 16)

        def piece_loads(sp, p, r, parts):
            slots = RING if p < MOE + RING else 2 * RING
            if p >= RING or not isinstance(r, int):
                sp.wait_ge(split, p - slots + 1 + scales_with(r, 3))
            if p == MOE + RING:
                sp.wait_ge(h_ready, 2 * H_ORDER.index("mix") + TT)
            for dst, src in parts:
                sp.dma_start(dst, src).then_inc(landed_of(p, r)[0], 16)

        def round_piece(act, p, r=0):
            act.wait_ge(*landed_of(p, r))
            if p >= RING or not isinstance(r, int):
                act.wait_ge(used, p - RING + 1 + scales_with(r, 3))
            act.activation(high[:, p % RING, :], raw_of(p), ACT.Copy).then_inc(rounded, 1)

        def split_piece(dve, p, r=0):
            dve.wait_ge(rounded, p + 1 + scales_with(r, 3))
            dve.tensor_tensor(low[:, p % RING, :], raw_of(p), high[:, p % RING, :].bitcast(F32),
                              ALU.subtract).then_inc(split, 1)

        def product(pe, psum_out, lhs_high, lhs_low, rhs_high, rhs_low, start, stop=False):
            pe.matmul(psum_out, lhs_high, rhs_high, start=start, stop=False, skip_group_check=True)
            pe.matmul(psum_out, lhs_high, rhs_low, start=False, stop=False, skip_group_check=True)
            return pe.matmul(psum_out, lhs_low, rhs_high, start=False, stop=stop, skip_group_check=True)

        def gate_up_parts(p, w_gate, w_up, half, col):
            dst = raw_of(p).rearrange("p (k n) -> p k n", k=4)
            rows = slice(half * 4 * P, (half + 1) * 4 * P)
            return [(dst[:, :, i * CHUNK:(i + 1) * CHUNK],
                     w[rows, bass.ds(col, CHUNK)].rearrange("(k p) n -> p k n", p=P)) for i, w in enumerate((w_gate, w_up))]

        def down_parts(p, w_down, row):
            dst = raw_of(p).rearrange("p (k n) -> p k n", k=2)
            src = w_down[bass.ds(row, 2 * P), :].rearrange("(k p) n -> p k n", p=P)
            return [(dst[:, i, :], src[:, i, :]) for i in range(2)]

        def in_parts(p, w, half, n):
            dst = raw_of(p).rearrange("p (k n) -> p k n", k=4)
            src = w[half * 4 * P:(half + 1) * 4 * P, n * BANK:(n + 1) * BANK].rearrange("(k p) n -> p k n", p=P)
            return [(dst[:, 2 * i:2 * i + 2, :], src[:, 2 * i:2 * i + 2, :]) for i in range(2)]

        def four_k(buf, p):
            return buf[:, p % RING, :].rearrange("p (k n) -> p k n", k=4)

        def two_k(buf, p):
            return buf[:, p % RING, :].rearrange("p (k n) -> p k n", k=2)

        def ffn_loads(sp, i):
            b = FIRST_PIECE[f"ffn{i}"]
            w_gate, w_up, w_down = ffns[i]
            for half in range(2):
                piece_loads(sp, b + half, 0, gate_up_parts(b + half, w_gate, w_up, half, 0))
            with sp.Fori(0, N_CHUNKS - 1) as c:
                for half in range(2):
                    piece_loads(sp, b + 2 + half, c, gate_up_parts(b + 2 + half, w_gate, w_up, half, (c + 1) * CHUNK))
                piece_loads(sp, b + 4, c, down_parts(b + 4, w_down, c * CHUNK))
            last = b + FFN_PIECES - 1
            piece_loads(sp, last, 0, down_parts(last, w_down, (N_CHUNKS - 1) * CHUNK))

        def in_loads(sp, name):
            for n in range(IN_CHUNKS):
                for half in range(2):
                    p = FIRST_PIECE[name] + 2 * n + half
                    piece_loads(sp, p, 0, in_parts(p, w_in[name], half, n))

        def out_loads(sp, name):
            for j in range(OUT_PIECES):
                p = FIRST_PIECE[name] + j
                piece_loads(sp, p, 0, down_parts(p, w_out[name], j * 2 * P))

        def norm_dve(dve, step, k, scale, last_piece):
            for tt in range(TT):
                if k == 0:
                    dve.wait_ge(x_loaded, 16)
                elif k != 7:
                    dve.wait_ge(used, last_piece + 1)
                    dve.scalar_tensor_tensor(x[:, tt, :], Y[tt], scale, x[:, tt, :], ALU.mult,
                                             ALU.add).then_inc(x_ready, 1)
            dve.wait_ge(roots, k + 1)
            step(dve.reciprocal(stat[:, 4:6], stat[:, 2:4]))
            for tt in range(TT):
                dve.wait_ge(gain_loaded[k % 2], 16 * (k // 2 + 1))
                to = x if k == 6 else h
                if k != 0 and k != 7:
                    dve.wait_ge(x_ready, X_COUNT[k] + tt + 1)
                dve.scalar_tensor_tensor(to[:, tt, :], x[:, tt, :], stat[:, 4 + tt:5 + tt], gain[:, k % 2, :], ALU.mult,
                                         ALU.mult).then_inc(x_ready if k == 6 else h_ready, 1)

        X_COUNT = {1: 0, 2: 2, 3: 4, 4: 6, 5: 8, 6: 10, 8: 14}

        def norm_act(act, k):
            for tt in range(TT):
                if k == 0:
                    act.wait_ge(x_loaded, 16)
                elif k == 7:
                    act.wait_ge(x_ready, 12 + tt + 1)
                else:
                    act.wait_ge(x_ready, X_COUNT[k] + tt + 1)
                if 2 * k + tt:
                    act.wait_ge(squares, 2 * k + tt)
                act.activation(square[:, :], x[:, tt, :], ACT.Square,
                               accum_out=stat[:, tt:tt + 1]).then_inc(squares, 1)
            if k == 0:
                act.wait_ge(eps_set, 1)
            act.wait_ge(squares, 2 * k + TT)
            act.activation(stat[:, 2:4], stat[:, 0:2], ACT.Sqrt, scale=1.0 / D, bias=eps[:, :]).then_inc(roots, 1)

        def turn_pe(pe, n, who):
            if n == 0:
                pe.wait_ge(consts, 1)
            for tt in range(TT):
                pe.wait_ge(h_ready, 2 * H_ORDER.index(who) + (TT if who in ("sb", "mix") else tt + 1))
                for k in range(KD):
                    dst = psum[:, 4 + k // 2, (k % 2) * TOKENS + tt * P:(k % 2) * TOKENS + (tt + 1) * P]
                    ins = pe.transpose(dst, h[:, tt, k * P:(k + 1) * P], ident[:, :])
                    if tt == TT - 1 and k % 2:
                        ins.then_inc(turned, 1)

        def turn_bank(buf, j):
            return buf[:, 2 * j:2 * j + 2, :].rearrange("p k n -> p (k n)")

        def turn_act(act, n):
            for j in range(4):
                act.wait_ge(turned, 4 * n + j + 1)
                act.activation(turn_bank(hT_high, j), banks(4 + j), ACT.Copy).then_inc(turn_high, 1)

        def turn_dve(dve, n):
            for j in range(4):
                dve.wait_ge(turn_high, 4 * n + j + 1)
                dve.tensor_tensor(turn_bank(hT_low, j), banks(4 + j), turn_bank(hT_high, j).bitcast(F32),
                                  ALU.subtract).then_inc(turn_low, 1)

        def clear_Y(pe):
            for b in range(4):
                pe.matmul(banks(b), zero_r[:, 0:P], zero_r[:, :], start=True, stop=True, skip_group_check=True)

        def gate_up_pe(pe, p, r, done_first):
            for half in range(2):
                q = p + half
                pe.wait_ge(split, q + 1 + scales_with(r, 3))
                for tt in range(TT):
                    for k in range(4):
                        kk = 4 * half + k
                        tok = slice(tt * P, (tt + 1) * P)
                        ins = product(pe, GU[tt], hT_high[:, kk, tok], hT_low[:, kk, tok], four_k(high, q)[:, k, :],
                                      four_k(low, q)[:, k, :], start=kk == 0, stop=kk == KD - 1)
                    if half == 1 and tt == 0:
                        ins.then_inc(done_first, 1)
                ins.then_inc(used, 1)

        def act_turn_pe(pe, count):
            for tt in range(TT):
                pe.wait_ge(act_ready, count + tt + 1 - 2)
                for k in range(2):
                    ins = pe.transpose(TURN_A[:, k * TOKENS + tt * P:k * TOKENS + (tt + 1) * P],
                                       act_tok[:, tt, k * P:(k + 1) * P], ident[:, :])
            ins.then_inc(a_turned, 1)

        def down_pe(pe, p, r, count_a):
            pe.wait_ge(a_low, count_a)
            pe.wait_ge(split, p + 1 + scales_with(r, 3))
            for k in range(2):
                for tt in range(TT):
                    for n in range(2):
                        tok, cols = slice(tt * P, (tt + 1) * P), slice(n * BANK, (n + 1) * BANK)
                        ins = product(pe, Y[tt][:, cols], aT_high[:, k, tok], aT_low[:, k, tok],
                                      two_k(high, p)[:, k, cols], two_k(low, p)[:, k, cols], start=False)
            ins.then_inc(used, 1)

        def ffn_pe(pe, i, turn):
            b, done = FIRST_PIECE[f"ffn{i}"], N_CHUNKS * i
            clear_Y(pe)
            pe.wait_ge(turn_low, 4 * (turn + 1))
            gate_up_pe(pe, b, 0, gu_first)
            act_turn_pe(pe, 2 * (done + 1))
            with pe.Fori(0, N_CHUNKS - 1) as c:
                gate_up_pe(pe, b + 2, c, gu_first)
                down_pe(pe, b + 4, c, c + (done + 1))
                act_turn_pe(pe, c * 2 + 2 * (done + 2))
            down_pe(pe, b + FFN_PIECES - 1, 0, done + N_CHUNKS)

        def gate_act(act, first, second):
            for tt, (counter, value) in enumerate(((gu_first, first), (used, second))):
                act.wait_ge(counter, value)
                act.activation(gate[:, tt, :], GU[tt][:, 0:CHUNK], ACT.Silu).then_inc(gate_ready, 1)

        def gate_dve(dve, count):
            for tt in range(TT):
                dve.wait_ge(gate_ready, count + tt + 1 - 2)
                dve.tensor_tensor(act_tok[:, tt, :], gate[:, tt, :], GU[tt][:, CHUNK:2 * CHUNK],
                                  ALU.mult).then_inc(act_ready, 1)

        def flat(buf):
            return buf[:, :, :].rearrange("p k n -> p (k n)")

        def ffn_act(act, i):
            b, done = FIRST_PIECE[f"ffn{i}"], N_CHUNKS * i

            def chunk(p, r, number, gu_used):
                round_piece(act, p, r)
                gate_act(act, number, gu_used)
                round_piece(act, p + 1, r)
                act.wait_ge(a_turned, number)
                act.activation(flat(aT_high), TURN_A, ACT.Copy).then_inc(a_high, 1)
                round_piece(act, p + 2, r)

            chunk(b + 2, 0, done + 1, b + 2)
            with act.Fori(0, N_CHUNKS - 1) as c:
                chunk(b + 5, c, c + (done + 2), c * 3 + (b + 4))

        def ffn_dve(dve, i):
            b, done = FIRST_PIECE[f"ffn{i}"], N_CHUNKS * i

            def chunk(p, r, number):
                split_piece(dve, p, r)
                gate_dve(dve, number * 2)
                split_piece(dve, p + 1, r)
                dve.wait_ge(a_high, number)
                dve.tensor_tensor(flat(aT_low), TURN_A, flat(aT_high).bitcast(F32), ALU.subtract).then_inc(a_low, 1)
                split_piece(dve, p + 2, r)

            chunk(b + 2, 0, done + 1)
            with dve.Fori(0, N_CHUNKS - 1) as c:
                chunk(b + 5, c, c + (done + 2))

        IN_ORDER = ["gla_in", "sb_in", "mix_in"]

        def in_pe(pe, name, turn):
            b, done = FIRST_PIECE[name], IN_CHUNKS * IN_ORDER.index(name)
            pe.wait_ge(turn_low, 4 * (turn + 1))
            for n in range(IN_CHUNKS):
                if n >= 3:
                    for c in in_copied:
                        pe.wait_ge(c, done + n - 2)
                for half in range(2):
                    q = b + 2 * n + half
                    pe.wait_ge(split, q + 1)
                    for tt in range(TT):
                        for k in range(4):
                            kk, tok = 4 * half + k, slice(tt * P, (tt + 1) * P)
                            ins = product(pe, banks(2 * (n % 3) + tt), hT_high[:, kk, tok], hT_low[:, kk, tok],
                                          four_k(high, q)[:, k, :], four_k(low, q)[:, k, :], start=kk == 0,
                                          stop=kk == KD - 1)
                        if half == 1 and tt == 0:
                            ins.then_inc(in_first, 1)
                    ins.then_inc(used, 1)

        def in_act(act, name):
            b, done = FIRST_PIECE[name], IN_CHUNKS * IN_ORDER.index(name)
            for n in range(IN_CHUNKS):
                round_piece(act, b + 2 * n + 2)
                round_piece(act, b + 2 * n + 3)
                act.wait_ge(in_first, done + n + 1)
                act.activation(proj[:, 0, n * BANK:(n + 1) * BANK], banks(2 * (n % 3)),
                               ACT.Copy).then_inc(in_copied[0], 1)

        def in_dve(dve, name):
            b = FIRST_PIECE[name]
            for n in range(IN_CHUNKS):
                split_piece(dve, b + 2 * n + 2)
                split_piece(dve, b + 2 * n + 3)
                dve.wait_ge(used, b + 2 * n + 2)
                dve.tensor_copy(proj[:, 1, n * BANK:(n + 1) * BANK], banks(2 * (n % 3) + 1)).then_inc(in_copied[1], 1)

        def wait_proj(eng, name):
            for c in in_copied:
                eng.wait_ge(c, IN_CHUNKS * (IN_ORDER.index(name) + 1))

        def out_pe(pe, name, turn):
            b = FIRST_PIECE[name]
            pe.wait_ge(turn_low, 4 * (turn + 1))
            for j in range(OUT_PIECES):
                p = b + j
                pe.wait_ge(split, p + 1)
                for k in range(2):
                    for tt in range(TT):
                        for n in range(2):
                            tok, cols = slice(tt * P, (tt + 1) * P), slice(n * BANK, (n + 1) * BANK)
                            ins = product(pe, Y[tt][:, cols], hT_high[:, 2 * j + k, tok], hT_low[:, 2 * j + k, tok],
                                          two_k(high, p)[:, k, cols], two_k(low, p)[:, k, cols],
                                          start=j == 0 and k == 0, stop=j == OUT_PIECES - 1 and k == 1)
                ins.then_inc(used, 1)

        def out_act(act, name):
            for j in range(3, 6):
                round_piece(act, FIRST_PIECE[name] + j)

        def out_dve(dve, name):
            for j in range(3, 6):
                split_piece(dve, FIRST_PIECE[name] + j)

        area = Area()
        gq = area.take(1024)
        gk = area.take(1024)
        gb = area.take(1024)
        gdiff = area.take(1024)
        geq, gek = square[:, 0:512], square[:, 512:1024]
        gqs = [area.take(1024) for _ in range(2)]
        gks = [area.take(1024) for _ in range(2)]
        gscore = area.take(1024)
        gcross = area.take(512)
        grank = area.take(TT * GLA_RANK)
        grankT = area.take(TOKENS)
        gsilu = [gqs[0], gqs[1]]
        gabs, glog = gks[0], gks[1]
        STEPS = [P] + LEVELS

        def pairs(v, B):
            return v.rearrange("p (m n) -> p m n", n=2 * B)

        def gla_pe(pe):
            pe.wait_ge(small_low, 1)
            pe.wait_ge(turn_low, 4 * 2)
            for tt in range(TT):
                for k in range(KD):
                    tok = slice(tt * P, (tt + 1) * P)
                    ins = product(pe, TURN_A[:, tt * GLA_RANK:(tt + 1) * GLA_RANK], hT_high[:, k, tok], hT_low[:, k, tok],
                                  gkw_high[:, k, :], gkw_low[:, k, :], start=tt == 0 and k == 0)
            ins.then_inc(g["rank"], 1)
            in_pe(pe, "gla_in", 1)
            wait_proj(pe, "gla_in")
            pe.wait_ge(g["rank_sb"], 1)
            for tt in range(TT):
                ins = pe.transpose(TURN_X[0:GLA_RANK, tt * P:(tt + 1) * P], grank[:, tt * GLA_RANK:(tt + 1) * GLA_RANK],
                                   ident[:, :])
            ins.then_inc(g["rankT"], 1)
            for w, off in ((2, 0), (4, 512)):
                for hd in range(GLA_HEADS):
                    for tt in range(TT):
                        dst = banks(w, 2)[:, hd * TOKENS + tt * P:hd * TOKENS + (tt + 1) * P]
                        ins = pe.transpose(dst, proj[:, tt, off + hd * P:off + (hd + 1) * P], ident[:, :])
                ins.then_inc(g["qkT"], 1)
            pe.wait_ge(g["rankT_sb"], 1)
            for hd in range(GLA_HEADS):
                ins = pe.matmul(banks(0, 2)[:, hd * TOKENS:(hd + 1) * TOKENS], wgk2[:, hd * P:(hd + 1) * P],
                                grankT[0:GLA_RANK, :], start=hd % 2 == 0, stop=True, skip_group_check=True)
            ins.then_inc(g["z"], 1)
            for n, B in enumerate(STEPS + [0]):
                if B:
                    pe.wait_ge(g["scaled"], n + 1)
                    q, k = gqs[n % 2], gks[n % 2]
                else:
                    q, k = gq, gk
                if n >= 2:
                    pe.wait_ge(g["kept"], n - 1)
                else:
                    pe.wait_ge(g["q_sb"], 1)
                    pe.wait_ge(g["k_sb"], 1)
                dst = banks(2 + 2 * (n % 2), 2)
                for hd in range(GLA_HEADS):
                    if B == P:
                        at = hd * TOKENS
                        ins = pe.matmul(dst[:, hd * P:(hd + 1) * P], k[:, at:at + P], q[:, at + P:at + 2 * P],
                                        start=hd == 0, stop=True, skip_group_check=True)
                        continue
                    for tt in range(TT):
                        at = hd * TOKENS + tt * P
                        ins = pe.matmul(dst[:, at:at + P], k[:, at:at + P], q[:, at:at + P],
                                        start=at % BANK == 0, stop=True, skip_group_check=True)
                ins.then_inc(g["scores"], 1)
            pe.wait_ge(g["kept"], len(STEPS) + 1)
            for hd in range(GLA_HEADS):
                def v(tt):
                    return proj[:, tt, 1024 + hd * GLA_V:1024 + (hd + 1) * GLA_V]

                def diag(tt):
                    return gscore[:, hd * TOKENS + tt * P:hd * TOKENS + (tt + 1) * P]
                cols = slice(hd * GLA_V, (hd + 1) * GLA_V)
                pe.matmul(Y[0][:, cols], diag(0), v(0), start=hd % 2 == 0, stop=True, skip_group_check=True)
                pe.matmul(Y[1][:, cols], diag(1), v(1), start=hd % 2 == 0, stop=False, skip_group_check=True)
                ins = pe.matmul(Y[1][:, cols], gcross[:, hd * P:(hd + 1) * P], v(0), start=False, stop=True,
                                skip_group_check=True)
            ins.then_inc(g["out"], 1)
            turn_pe(pe, GLA_TURN, "gla")
            out_pe(pe, "gla_out", GLA_TURN)

        def gla_act(act, step):
            in_act(act, "gla_in")
            round_piece(act, FIRST_PIECE["gla_out"] + 2)
            act.wait_ge(g["z"], 1)
            for hd in range(GLA_HEADS):
                c = slice(hd * TOKENS, (hd + 1) * TOKENS)
                ins = act.activation(gabs[:, c], banks(0, 2)[:, c], ACT.Abs, bias=bgk[:, hd:hd + 1])
            step(ins)
            act.wait_ge(g["qkT"], 1)
            step(act.activation(gabs, gabs, ACT.Exp, scale=-1.0))
            act.activation(glog, gabs, ACT.Ln, bias=ones[:, 0:1]).then_inc(g["ln"], 1)
            act.activation(gq, banks(2, 2), ACT.Copy, scale=float(GLA_K) ** -0.5).then_inc(g["q_sb"], 1)
            for n, B in enumerate(STEPS):
                act.wait_ge(g["diff"], n + 1)
                if n:
                    act.wait_ge(g["scaled"], n)
                v = pairs(gdiff, B)
                w = {"n": B}
                act.activation(geq.rearrange("p (m n) -> p m n", **w), v[:, :, B:2 * B], ACT.Exp, scale=1.0 / GLA_TAU)
                act.activation(gek.rearrange("p (m n) -> p m n", **w), v[:, :, 0:B], ACT.Exp,
                               scale=-1.0 / GLA_TAU).then_inc(g["decay"], 1)
            act.wait_ge(g["out"], 1)
            for tt in range(TT):
                act.activation((square[:, :], gdiff)[tt], Y[tt], ACT.Square).then_inc(g["sq"], 1)
            for tt in range(TT):
                act.activation(gsilu[tt], proj[:, tt, 2048:3072], ACT.Silu).then_inc(g["silu"], 1)
            act.wait_ge(g["summed"], 1)
            act.activation(stat[:, 16:24], stat[:, 8:16], ACT.Sqrt, scale=1.0 / GLA_V,
                           bias=eps[:, :]).then_inc(g["roots"], 1)
            turn_act(act, GLA_TURN)
            out_act(act, "gla_out")

        def gla_dve(dve, step):
            in_dve(dve, "gla_in")
            split_piece(dve, FIRST_PIECE["gla_out"] + 2)
            dve.wait_ge(g["rankT"], 1)
            dve.tensor_copy(grankT[0:GLA_RANK, :], TURN_X[0:GLA_RANK, 0:TOKENS]).then_inc(g["rankT_sb"], 1)
            dve.wait_ge(g["qkT"], 2)
            dve.tensor_copy(gk, banks(4, 2)).then_inc(g["k_sb"], 1)
            dve.wait_ge(g["ln"], 1)
            for hd in range(GLA_HEADS):
                c = slice(hd * TOKENS, (hd + 1) * TOKENS)
                ins = dve.tensor_scalar(gdiff[:, c], banks(0, 2)[:, c], bgk[:, hd:hd + 1], 0.0, ALU.add, ALU.min)
            step(ins)
            step(dve.tensor_tensor(gdiff, gdiff, glog, ALU.subtract))
            for hd in range(GLA_HEADS):
                c = slice(hd * TOKENS, (hd + 1) * TOKENS)
                ins = dve.tensor_tensor_scan(gb[:, c], ones[:, :], gdiff[:, c], 0.0, ALU.mult, ALU.add)
            step(ins)
            for i in range(2):
                dve.memset(gqs[i], 0.0)
                ins = dve.memset(gks[i], 0.0)
            step(ins)
            dve.wait_ge(g["q_sb"], 1)
            for n, B in enumerate(STEPS):
                v = pairs(gb, B)
                if n:
                    dve.wait_ge(g["decay"], n)
                dve.tensor_tensor(pairs(gdiff, B), v, v[:, :, B - 1:B].to_broadcast([P, TT * GLA_HEADS * P // (2 * B), 2 * B]),
                                  ALU.subtract).then_inc(g["diff"], 1)
                if n:
                    keep(dve, n - 1)
                dve.wait_ge(g["decay"], n + 1)
                if n >= 2:
                    dve.wait_ge(g["scores"], n - 1)
                w = {"n": B}
                dve.tensor_tensor(pairs(gqs[n % 2], B)[:, :, B:2 * B], pairs(gq, B)[:, :, B:2 * B],
                                  geq.rearrange("p (m n) -> p m n", **w), ALU.mult)
                dve.tensor_tensor(pairs(gks[n % 2], B)[:, :, 0:B], pairs(gk, B)[:, :, 0:B],
                                  gek.rearrange("p (m n) -> p m n", **w), ALU.mult).then_inc(g["scaled"], 1)
            keep(dve, len(STEPS) - 1)
            keep(dve, len(STEPS))
            dve.wait_ge(g["sq"], 2)
            for tt in range(TT):
                ins = dve.tensor_reduce(stat[:, 8 + 4 * tt:12 + 4 * tt],
                                        (square[:, :], gdiff)[tt].rearrange("p (a b) -> p a b", b=GLA_V), AX, ALU.add)
            ins.then_inc(g["summed"], 1)
            dve.wait_ge(g["roots"], 1)
            step(dve.reciprocal(stat[:, 24:32], stat[:, 16:24]))
            for tt in range(TT):
                for hd in range(GLA_HEADS):
                    c, n = slice(hd * GLA_V, (hd + 1) * GLA_V), 24 + 4 * tt + hd
                    ins = dve.scalar_tensor_tensor(h[:, tt, c], Y[tt][:, c], stat[:, n:n + 1], gla_gain[:, :],
                                                   ALU.mult, ALU.mult)
                step(ins)
                dve.wait_ge(g["silu"], tt + 1)
                dve.tensor_tensor(h[:, tt, :], h[:, tt, :], gsilu[tt], ALU.mult).then_inc(h_ready, 1)
            turn_dve(dve, GLA_TURN)
            out_dve(dve, "gla_out")

        def keep(dve, n):
            dve.wait_ge(g["scores"], n + 1)
            src = banks(2 + 2 * (n % 2), 2)
            if n == 0:
                ins = dve.tensor_copy(gcross, src[:, 0:GLA_HEADS * P])
                ins.then_inc(g["kept"], 1)
                return
            dve.wait_ge(g["kept"], n)
            B = (STEPS + [0])[n]
            mask = levels[:, LEVELS.index(B), :] if B else ident[:, :]
            mask = mask.bitcast(I32).rearrange("p (o n) -> p o n", o=1).to_broadcast([P, 2 * GLA_HEADS, P])
            dve.copy_predicated(gscore.rearrange("p (b n) -> p b n", n=P), mask,
                                src.rearrange("p (b n) -> p b n", n=P)).then_inc(g["kept"], 1)

        area = Area()
        sq_T, sk_T = area.take(2048), area.take(2048)
        GROUP_COLS = GROUP * (TOKENS + P)
        sz = [area.take(GROUP_COLS) for _ in range(2)]
        ssp = [area.take(GROUP_COLS) for _ in range(2)]

        def place(i):
            return (i % 2) * 2 + i // 2

        def early(v):
            return v[:, 0:GROUP * TOKENS].rearrange("p (a n) -> p a n", n=TOKENS)[:, :, 0:P]

        def late_part(v):
            return v[:, GROUP * TOKENS:].rearrange("p (a n) -> p a n", n=P)

        def turn_columns(pe, dst, off, tiles, signal):
            for k in range(tiles):
                for tt in range(TT):
                    ins = pe.transpose(dst[:, k * TOKENS + tt * P:k * TOKENS + (tt + 1) * P],
                                       proj[:, tt, off + k * P:off + (k + 1) * P], ident[:, :])
            ins.then_inc(signal, 1)

        def sb_pe(pe):
            in_pe(pe, "sb_in", 5)
            wait_proj(pe, "sb_in")
            turn_columns(pe, banks(0, 4), 0, KD, s["qkT"])
            turn_columns(pe, banks(4, 4), D, KD, s["qkT"])
            pe.wait_ge(s["q_sb"], 1)
            pe.wait_ge(s["k_sb"], 1)

            def dots(gr):
                if gr:
                    pe.wait_ge(s["z_sb"], gr)
                z = banks(0, 3)
                for i in (0, 2, 1, 3):
                    rows, at = slice(SB_HD * (i % 2), SB_HD * (i % 2 + 1)), (2 * gr + i // 2) * TOKENS
                    c = place(i)
                    pe.matmul(z[:, c * TOKENS:(c + 1) * TOKENS], sk_T[rows, at:at + P], sq_T[rows, at:at + TOKENS],
                              start=True, stop=True, skip_group_check=True)
                    if i >= 2:
                        if i == 3:
                            pe.wait_ge(s["even"], gr + 1)
                        for ii in (i - 2, i):
                            c, at = place(ii), (2 * gr + ii // 2) * TOKENS
                            ins = pe.matmul(z[:, GROUP * TOKENS + c * P:GROUP * TOKENS + (c + 1) * P],
                                            sk_T[rows, at + P:at + TOKENS], sq_T[rows, at + P:at + TOKENS],
                                            start=True, stop=True, skip_group_check=True)
                        if i == 2:
                            ins.then_inc(s["even"], 1)
                ins.then_inc(s["z"], 1)

            dots(0)
            for gr in range(SB_GROUPS):
                if gr + 1 < SB_GROUPS:
                    dots(gr + 1)
                pe.wait_ge(s["sp"], gr + 1)
                if gr:
                    pe.wait_ge(s["arg"], gr)
                v = ssp[gr % 2]
                for b in range(3):
                    ins = pe.matmul(banks(3 + b), suffix[:, :], v[:, b * BANK:(b + 1) * BANK], start=True, stop=b == 2,
                                    skip_group_check=True)
                    if b < 2:
                        dst = banks(3 + b).rearrange("p (a n) -> p a n", n=TOKENS)[:, :, P:TOKENS]
                        pe.matmul(dst, ones[:, 0:P], late_part(v)[:, 2 * b:2 * b + 2, :], start=False, stop=True,
                                  skip_group_check=True)
                ins.then_inc(s["sums"], 1)
                pe.wait_ge(s["w"], gr + 1)
                if gr >= 2:
                    pe.wait_ge(s["out_sb"], gr - 1)
                w, dst = sz[gr % 2], banks(6 + gr % 2)
                for i in range(GROUP):
                    c, col = place(i), 2 * D + (GROUP * gr + i) * SB_HD
                    v0, v1 = proj[:, 0, col:col + SB_HD], proj[:, 1, col:col + SB_HD]
                    pe.matmul(dst[:, i * SB_HD:(i + 1) * SB_HD], w[:, c * TOKENS:c * TOKENS + P], v0, start=i == 0,
                              stop=True, skip_group_check=True)
                    to = dst[:, TOKENS + i * SB_HD:TOKENS + (i + 1) * SB_HD]
                    pe.matmul(to, w[:, c * TOKENS + P:(c + 1) * TOKENS], v0, start=False, stop=False,
                              skip_group_check=True)
                    at = GROUP * TOKENS + c * P
                    ins = pe.matmul(to, w[:, at:at + P], v1, start=False, stop=True, skip_group_check=True)
                ins.then_inc(s["out"], 1)
            turn_pe(pe, SB_TURN, "sb")
            out_pe(pe, "sb_out", SB_TURN)

        def sb_act(act, step):
            in_act(act, "sb_in")
            round_piece(act, FIRST_PIECE["sb_out"] + 2)
            act.wait_ge(s["qkT"], 1)
            act.activation(sq_T, banks(0, 4), ACT.Copy, scale=float(SB_HD) ** -0.5).then_inc(s["q_sb"], 1)

            def softplus_tail(gr):
                act.wait_ge(s["z_sb"], gr + 1)
                if gr >= 2:
                    act.wait_ge(s["sums"], gr - 1)
                v = ssp[gr % 2]
                step(act.activation(v, sz[gr % 2], ACT.Abs))
                step(act.activation(v, v, ACT.Exp, scale=-1.0))
                act.activation(v, v, ACT.Ln, bias=ones[:, 0:1]).then_inc(s["ln"], 1)

            softplus_tail(0)
            for gr in range(SB_GROUPS):
                if gr + 1 < SB_GROUPS:
                    softplus_tail(gr + 1)
                act.wait_ge(s["arg"], gr + 1)
                act.activation(sz[gr % 2], sz[gr % 2], ACT.Exp).then_inc(s["exp"], 1)
            turn_act(act, SB_TURN)
            out_act(act, "sb_out")

        def sb_dve(dve, step):
            in_dve(dve, "sb_in")
            split_piece(dve, FIRST_PIECE["sb_out"] + 2)
            dve.wait_ge(s["qkT"], 2)
            dve.tensor_copy(sk_T, banks(4, 4)).then_inc(s["k_sb"], 1)
            mask = strict[:, :].rearrange("p (o n) -> p o n", o=1).to_broadcast([P, GROUP, P])

            def copy_z(gr):
                dve.wait_ge(s["z"], gr + 1)
                if gr >= 2:
                    dve.wait_ge(s["out"], gr - 1)
                dve.tensor_copy(sz[gr % 2], banks(0, 3)).then_inc(s["z_sb"], 1)

            def softplus(gr):
                v = ssp[gr % 2]
                dve.wait_ge(s["ln"], gr + 1)
                dve.wait_ge(s["z_sb"], gr + 1)
                step(dve.scalar_tensor_tensor(v, sz[gr % 2], 0.0, v, ALU.max, ALU.add))
                dve.tensor_tensor(early(v), early(v), mask, ALU.mult)
                dve.tensor_tensor(late_part(v), late_part(v), mask, ALU.mult).then_inc(s["sp"], 1)

            copy_z(0)
            softplus(0)
            for gr in range(SB_GROUPS):
                if gr + 1 < SB_GROUPS:
                    copy_z(gr + 1)
                w = sz[gr % 2]
                dve.wait_ge(s["sums"], gr + 1)
                dve.tensor_tensor(w, w, banks(3, 3), ALU.subtract).then_inc(s["arg"], 1)
                if gr + 1 < SB_GROUPS:
                    softplus(gr + 1)
                dve.wait_ge(s["exp"], gr + 1)
                for part in (early, late_part):
                    ins = dve.scalar_tensor_tensor(part(w), part(w), 1.0, mask, ALU.min, ALU.mult)
                ins.then_inc(s["w"], 1)
                dve.wait_ge(s["out"], gr + 1)
                src = banks(6 + gr % 2)
                for tt in range(TT):
                    last = gr == SB_GROUPS - 1
                    ins = dve.tensor_copy(h[:, tt, gr * TOKENS:(gr + 1) * TOKENS], src[:, tt * TOKENS:(tt + 1) * TOKENS])
                    if last:
                        ins.then_inc(h_ready, 1)
                if not last:
                    ins.then_inc(s["out_sb"], 1)
            turn_dve(dve, SB_TURN)
            out_dve(dve, "sb_out")

        area = Area()
        mqT, mkT = area.take(1024), area.take(1024)
        mdot = [area.take(2 * 3 * P) for _ in range(2)]
        mexp = [area.take(2 * 3 * P) for _ in range(2)]
        ma = [area.take(3 * P) for _ in range(2)]
        maT = [area.take(3 * P) for _ in range(2)]
        shifted = [area.take(TT * D_CONV) for _ in range(2)]
        conv_w = area.take(CONV_W * D_CONV)
        conv_gain = area.take(D_CONV)
        msquare = scratch[:, 2048:4096]
        params = levels[:, :, :].rearrange("p a n -> p (a n)")
        qk_gain, sub_gain, lam_in = params[:, 0:128], params[:, 128:256], params[:, 256:512]
        XC, BG, CG, QK, VV = 0, D_CONV, 2 * D_CONV, 3 * D_CONV, 5 * D_CONV
        QK_GROUPS = 2 * 2 * DA_HEADS

        def both(off, n):
            return proj[:, :, off:off + n]

        def by_tile(v):
            return v.rearrange("p (a n) -> p a n", a=TT)

        def mix_pe(pe):
            in_pe(pe, "mix_in", 8)
            pe.wait_ge(m["qk"], 1)
            turn_columns(pe, banks(0, 2), QK, DA_HEADS, m["qkT"])
            turn_columns(pe, banks(2, 2), QK + D_CONV, DA_HEADS, m["qkT"])
            pe.wait_ge(m["q_sb"], 1)
            pe.wait_ge(m["k_sb"], 1)

            def dots(hd):
                if hd >= 2:
                    pe.wait_ge(m["dots_sb"], hd - 1)
                for c in range(2):
                    rows, at, dst = slice(DA_HD * c, DA_HD * (c + 1)), hd * TOKENS, banks(2 * (hd % 2) + c)
                    pe.matmul(dst[:, 0:P], mqT[rows, at:at + P], mkT[rows, at:at + P], start=True, stop=True,
                              skip_group_check=True)
                    ins = pe.matmul(dst[:, P:3 * P], mqT[rows, at + P:at + TOKENS], mkT[rows, at:at + TOKENS],
                                    start=True, stop=True, skip_group_check=True)
                ins.then_inc(m["dots"], 1)

            dots(0)
            for hd in range(DA_HEADS):
                if hd + 1 < DA_HEADS:
                    dots(hd + 1)
                pe.wait_ge(m["a"], hd + 1)
                if hd >= 2:
                    pe.wait_ge(m["aT_sb"], hd - 1)
                for j in range(3):
                    ins = pe.transpose(banks(4 + hd % 2)[:, j * P:(j + 1) * P], ma[hd % 2][:, j * P:(j + 1) * P], ident[:, :])
                ins.then_inc(m["aT"], 1)
                pe.wait_ge(m["aT_sb"], hd + 1)
                a, col = maT[hd % 2], slice(hd * DA_V, (hd + 1) * DA_V)
                v0, v1 = (proj[:, tt, VV + hd * DA_V:VV + (hd + 1) * DA_V] for tt in range(TT))
                pe.matmul(banks(6)[:, col], a[:, 0:P], v0, start=hd == 0, stop=True, skip_group_check=True)
                pe.matmul(banks(7)[:, col], a[:, P:2 * P], v0, start=hd == 0, stop=False, skip_group_check=True)
                ins = pe.matmul(banks(7)[:, col], a[:, 2 * P:], v1, start=False, stop=True, skip_group_check=True)
            ins.then_inc(m["out"], 1)
            turn_pe(pe, MIX_TURN, "mix")
            out_pe(pe, "mix_out", MIX_TURN)

        def mix_act(act, step):
            in_act(act, "mix_in")
            round_piece(act, FIRST_PIECE["mix_out"] + 2)
            wait_proj(act, "mix_in")
            act.activation(by_tile(msquare), both(QK, 2 * D_CONV), ACT.Square).then_inc(m["qk_sq"], 1)
            act.wait_ge(m["qk_sum"], 1)
            act.activation(stat[:, 0:32], stat[:, 32:64], ACT.Sqrt, scale=1.0 / DA_HD, bias=eps[:, :]).then_inc(m["qk_root"], 1)
            act.wait_ge(m["lam"], 1)
            act.activation(params[:, 514:516], params[:, 512:514], ACT.Exp).then_inc(m["lam_exp"], 1)
            act.wait_ge(m["qkT"], 1)
            act.activation(mqT, banks(0, 2), ACT.Copy, scale=float(DA_HD) ** -0.5).then_inc(m["q_sb"], 1)

            def softmax(hd):
                act.wait_ge(m["bias"], hd + 1)
                for tt, lo, hi in ((0, 0, P), (1, P, 3 * P)):
                    for c in range(2):
                        at, col = c * 3 * P, 8 * (hd % 2) + 2 * tt + c
                        ins = act.activation(mexp[hd % 2][:, at + lo:at + hi], mdot[hd % 2][:, at + lo:at + hi], ACT.Exp,
                                             bias=stat[:, 4 + col:5 + col], accum_out=stat[:, 16 + col:17 + col])
                ins.then_inc(m["exp"], 1)

            softmax(0)
            for hd in range(DA_HEADS):
                if hd + 1 < DA_HEADS:
                    softmax(hd + 1)
                act.wait_ge(m["aT"], hd + 1)
                act.activation(maT[hd % 2], banks(4 + hd % 2)[:, 0:3 * P], ACT.Copy).then_inc(m["aT_sb"], 1)
            act.wait_ge(m["conv"], 1)
            act.wait_ge(m["out"], 1)
            act.activation(by_tile(scratch[:, 2048:3072]), both(XC, D_CONV), ACT.Square)
            act.activation(square[:, :], banks(6, 2), ACT.Square).then_inc(m["sq"], 1)
            act.wait_ge(m["sum"], 1)
            act.activation(stat[:, 32:48], stat[:, 0:16], ACT.Sqrt, scale=8.0 / D_CONV, bias=eps[:, :])
            act.activation(stat[:, 48:56], stat[:, 16:24], ACT.Sqrt, scale=1.0 / DA_V, bias=eps[:, :]).then_inc(m["root"], 1)
            turn_act(act, MIX_TURN)
            out_act(act, "mix_out")

        def mix_dve(dve, step):
            in_dve(dve, "mix_in")
            split_piece(dve, FIRST_PIECE["mix_out"] + 2)
            wait_proj(dve, "mix_in")
            dve.tensor_tensor(both(XC, D_CONV), both(XC, D_CONV), both(CG, D_CONV), ALU.mult).then_inc(m["u"], 1)
            dve.wait_ge(m["qk_sq"], 1)
            dve.tensor_reduce(stat[:, 32:64], msquare.rearrange("p (a n) -> p a n", n=DA_HD), AX, ALU.add).then_inc(m["qk_sum"], 1)
            dve.wait_ge(mix_loaded, 9 * 16)
            step(dve.tensor_tensor(lam_in[:, 0:128], lam_in[:, 0:128], lam_in[:, 128:256], ALU.mult))
            dve.tensor_reduce(params[:, 512:514], lam_in[:, 0:128].rearrange("p (a n) -> p a n", n=DA_HD), AX,
                              ALU.add).then_inc(m["lam"], 1)
            dve.wait_ge(m["qk_root"], 1)
            step(dve.reciprocal(stat[:, 32:64], stat[:, 0:32]))
            gains_qk = qk_gain.rearrange("p (a o n) -> p a o n", a=2, o=1).to_broadcast([P, 2, QK_GROUPS // 2, DA_HD])
            for tt in range(TT):
                v = proj[:, tt, QK:QK + 2 * D_CONV]
                v3, v4 = v.rearrange("p (a n) -> p a n", n=DA_HD), v.rearrange("p (a b n) -> p a b n", a=2, n=DA_HD)
                r = stat[:, 32 + 16 * tt:48 + 16 * tt].rearrange("p (a o) -> p a o", o=1).to_broadcast([P, QK_GROUPS, DA_HD])
                step(dve.tensor_tensor(v3, v3, r, ALU.mult))
                ins = dve.tensor_tensor(v4, v4, gains_qk, ALU.mult)
            ins.then_inc(m["qk"], 1)
            dve.wait_ge(m["lam_exp"], 1)
            step(dve.tensor_scalar(params[:, 516:517], params[:, 515:516], params[:, 514:515], LAMBDA_INIT, ALU.subtract,
                                   ALU.subtract))
            dve.wait_ge(m["qkT"], 2)
            dve.tensor_copy(mkT, banks(2, 2)).then_inc(m["k_sb"], 1)
            mask = causal[:, :].rearrange("p (o n) -> p o n", o=1).to_broadcast([P, 2, 3 * P])

            def scores(hd):
                v = mdot[hd % 2].rearrange("p (c n) -> p c n", c=2)
                src = psum[:, 2 * (hd % 2):2 * (hd % 2) + 2, 0:3 * P]
                dve.wait_ge(m["dots"], hd + 1)
                at = 8 * (hd % 2)
                ins = dve.tensor_tensor(v, src, mask, ALU.add)
                ins.then_inc(m["dots_sb"], 1)
                dve.wait_ge(m["dots_sb"], hd + 1)
                dve.tensor_reduce(stat[:, 32 + at:34 + at], v[:, :, 0:P], AX, ALU.max)
                step(dve.tensor_reduce(stat[:, 34 + at:36 + at], v[:, :, P:], AX, ALU.max))
                dve.tensor_scalar(stat[:, 4 + at:8 + at], stat[:, 32 + at:36 + at], -1.0, None, ALU.mult).then_inc(m["bias"], 1)

            scores(0)
            for hd in range(DA_HEADS):
                if hd + 1 < DA_HEADS:
                    scores(hd + 1)
                at = 8 * (hd % 2)
                dve.wait_ge(m["exp"], hd + 1)
                step(dve.reciprocal(stat[:, 48 + at:52 + at], stat[:, 16 + at:20 + at]))
                v = stat[:, 48 + at:52 + at].rearrange("p (a c) -> p a c", c=2)[:, :, 1]
                step(dve.tensor_scalar(v, v, params[:, 516:517], None, ALU.mult))
                if hd >= 2:
                    dve.wait_ge(m["aT"], hd - 1)
                for tt, lo, hi in ((0, 0, P), (1, P, 3 * P)):
                    n = 48 + at + 2 * tt
                    second = mexp[hd % 2][:, 3 * P + lo:3 * P + hi]
                    step(dve.tensor_scalar(second, second, stat[:, n + 1:n + 2], None, ALU.mult))
                    ins = dve.scalar_tensor_tensor(ma[hd % 2][:, lo:hi], mexp[hd % 2][:, lo:hi], stat[:, n:n + 1], second,
                                                   ALU.mult, ALU.add)
                ins.then_inc(m["a"], 1)
            dve.wait_ge(m["sq"], 1)
            dve.tensor_reduce(stat[:, 0:16], scratch[:, 2048:3072].rearrange("p (a n) -> p a n", n=D_CONV // 8), AX, ALU.add)
            dve.tensor_reduce(stat[:, 16:24], square[:, :].rearrange("p (a n) -> p a n", n=DA_V), AX,
                              ALU.add).then_inc(m["sum"], 1)
            dve.wait_ge(m["root"], 1)
            step(dve.reciprocal(stat[:, 0:24], stat[:, 32:56]))
            step(dve.tensor_scalar(stat[:, 16:24], stat[:, 16:24], 1.0 - LAMBDA_INIT, None, ALU.mult))
            for tt in range(TT):
                v = proj[:, tt, XC:XC + D_CONV].rearrange("p (a n) -> p a n", n=D_CONV // 8)
                r = stat[:, 8 * tt:8 * tt + 8].rearrange("p (a o) -> p a o", o=1).to_broadcast([P, 8, D_CONV // 8])
                step(dve.tensor_tensor(v, v, r, ALU.mult))
                dve.tensor_tensor(h[:, tt, 0:D_CONV], proj[:, tt, XC:XC + D_CONV], conv_gain, ALU.mult)
                for hd in range(DA_HEADS):
                    c = slice(hd * DA_V, (hd + 1) * DA_V)
                    n = 16 + 4 * tt + hd
                    ins = dve.scalar_tensor_tensor(h[:, tt, D_CONV + hd * DA_V:D_CONV + (hd + 1) * DA_V],
                                                   banks(6 + tt)[:, c], stat[:, n:n + 1], sub_gain, ALU.mult, ALU.mult)
                ins.then_inc(h_ready, 1)
            turn_dve(dve, MIX_TURN)
            out_dve(dve, "mix_out")

        def mix_pool(pool, step):
            pool.wait_ge(x_ready, X_COUNT[5] + 2)
            loads = [(conv_w, t["conv_w_2"][0].rearrange("k n -> (k n)")), (conv_gain, t["conv_out_g_2"][0]),
                     (qk_gain[:, 0:64], t["q_norm_g_2"][0]), (qk_gain[:, 64:128], t["k_norm_g_2"][0]),
                     (sub_gain, t["attn_subln_g_2"][0])]
            loads += [(lam_in[:, 64 * i:64 * i + 64], t[f"lambda_{n}_2"][0]) for i, n in enumerate(("q1", "q2", "k1", "k2"))]
            for dst, src in loads:
                pool.dma_start(dst, src.partition_broadcast(P)).then_inc(mix_loaded, 16)

        def mix_conv_pool(pool, step):
            pool.wait_ge(m["u"], 1)
            pool.dma_start(conv_rows[CONV_W - 1:, :].rearrange("(a p) n -> p a n", p=P), both(XC, D_CONV)).then_inc(m["stored"], 16)
            pool.wait_ge(m["stored"], 16)
            pool.wait_ge(m["zeros"], 16)
            for i in range(2):
                pool.dma_start(by_tile(shifted[i]), conv_rows[1 - i:1 - i + TOKENS, :].rearrange("(a p) n -> p a n", p=P)
                               ).then_inc(m["shifted"], 16)
            pool.wait_ge(m["shifted"], 32)
            pool.wait_ge(mix_loaded, 9 * 16)

            def weight(i):
                return conv_w[:, i * D_CONV:(i + 1) * D_CONV].rearrange("p (o n) -> p o n", o=1).to_broadcast([P, TT, D_CONV])
            acc = both(XC, D_CONV)
            pool.tensor_tensor(acc, acc, weight(2), ALU.mult)
            pool.tensor_tensor(by_tile(shifted[0]), by_tile(shifted[0]), weight(1), ALU.mult)
            step(pool.tensor_tensor(by_tile(shifted[1]), by_tile(shifted[1]), weight(0), ALU.mult))
            step(pool.tensor_tensor(acc, acc, by_tile(shifted[0]), ALU.add))
            step(pool.tensor_tensor(acc, acc, by_tile(shifted[1]), ALU.add))
            pool.tensor_tensor(acc, acc, both(BG, D_CONV), ALU.mult).then_inc(m["conv"], 1)

        pa = proj[:, :, :].rearrange("p a n -> p (a n)")
        taken = [0]

        def take(n, dt=F32):
            taken[0] += n
            assert taken[0] <= TT * GLA_COLS
            v = pa[:, taken[0] - n:taken[0]]
            return v if dt is F32 else v.bitcast(dt)
        iota = take(SLOTS)
        own_slot = take(1)
        logits = take(TT * (GROUPS + EXPERTS))
        group_pad, group_top, group_at = take(TT * 8), take(TT * 8), take(TT * 8, U32)
        group, group_off = take(TT), take(TT)
        group_exp, group_gate = take(TT * GROUPS), take(TT)
        group_hot, group_pick, mine = take(TT * GROUPS), take(TT * EXPERTS), take(TT * PER_GROUP)
        top, top_at, pick = take(TT * 8), take(TT * 8, U32), take(TT * 2)
        gap, gap_exp, share = take(TT), take(TT), take(2 * TT)
        takes, takes_any = take(2 * TT * EXPERTS), take(TT * EXPERTS)
        counts = take(3 * EXPERTS)
        count, rank = counts[:, 0:EXPERTS], counts[:, EXPERTS:]
        over, over_to, over_from, tile_base = take(EXPERTS), take(EXPERTS), take(EXPERTS), take(EXPERTS)
        tile_no, place_in, item = take(TT * EXPERTS), take(TT * EXPERTS), take(TT * EXPERTS)
        chosen = take(2 * TT * EXPERTS)
        item_of, place_of, slot_of = take(2 * TT), take(2 * TT), take(2 * TT)
        from_slot = take(2 * TT)
        share_slot = take(1)
        pick_by_k, picks = take(2 * TT * SLOTS), take(TT * SLOTS)
        slot_rows = take(2 * TOKENS)
        spread_part = take(2 * TOKENS)
        over_expert, over_test = take(MAX_OVER * EXPERTS), take(MAX_OVER * EXPERTS)
        plan_f, plan = take(1 + ITEMS), take(1 + ITEMS, I32)
        y_high, y_low = flat(hT_low)[:, 0:D], flat(hT_low)[:, D:2 * D]
        spread = flat(aT_low)[:, 0:TOKENS]
        ROUTE = banks(6)
        CNT = TT * (GROUPS + EXPERTS)
        SLOT_ROWS = banks(7)
        experts = [t[f"w_exp_{n}_2"].rearrange("o g e k n -> (o g e) k n") for n in ("gate", "up", "down")]
        XT = hT_high[:, :, 0:P]
        AT = flat(aT_high).rearrange("p (f n) -> p f n", f=4)
        gu_rest, gu_sum = [[scratch[:, i * D + c * BANK:i * D + (c + 1) * BANK] for c in range(2)] for i in range(2)]
        ITEM_Y = banks(6, 2)
        BODY = MOE + 4

        def k_of(v, k):
            return v[:, k * TT:(k + 1) * TT]

        def route_dve(dve, step):
            dve.wait_ge(e["tables"], 1)
            dve.memset(group_pad, -3e38)
            dve.memset(plan_f, 0.0)
            dve.wait_ge(e["logits"], 1)
            step(dve.tensor_copy(logits, ROUTE[:, 0:CNT]))
            lg = by_tile(logits)
            step(dve.tensor_copy(by_tile(group_pad)[:, :, 0:GROUPS], lg[:, :, 0:GROUPS]))
            for tt in range(TT):
                c = slice(8 * tt, 8 * tt + 8)
                step(dve.max(group_top[:, c], group_pad[:, c]))
                ins = dve.max_index(group_at[:, c], group_top[:, c], group_pad[:, c])
            step(ins)
            highest = by_tile(group_top)[:, :, 0:1]
            dve.tensor_tensor(by_tile(group_exp), lg[:, :, 0:GROUPS], highest.to_broadcast([P, TT, GROUPS]),
                              ALU.subtract).then_inc(e["gexp_in"], 1)
            step(dve.tensor_copy(group, by_tile(group_at)[:, :, 0]))
            dve.tensor_scalar(group_off, group, float(PER_GROUP), None, ALU.mult)
            for tt in range(TT):
                ins = dve.tensor_scalar(group_hot[:, GROUPS * tt:GROUPS * (tt + 1)], iota[:, 0:GROUPS], group[:, tt:tt + 1],
                                        None, ALU.is_equal)
            step(ins)
            for tt in range(TT):
                hot = group_hot[:, GROUPS * tt:GROUPS * (tt + 1)].rearrange("p (g o) -> p g o", o=1)
                ins = dve.tensor_tensor(group_pick[:, EXPERTS * tt:EXPERTS * (tt + 1)].rearrange("p (g e) -> p g e", g=GROUPS),
                                        lg[:, tt, GROUPS:].rearrange("p (g e) -> p g e", g=GROUPS),
                                        hot.to_broadcast([P, GROUPS, PER_GROUP]), ALU.mult)
            step(ins)
            step(dve.tensor_reduce(by_tile(mine), group_pick.rearrange("p (a g e) -> p a e g", a=TT, g=GROUPS), AX, ALU.add))
            for tt in range(TT):
                c = slice(8 * tt, 8 * tt + 8)
                step(dve.max(top[:, c], mine[:, c]))
                ins = dve.max_index(top_at[:, c], top[:, c], mine[:, c])
            step(ins)
            step(dve.tensor_copy(pick.rearrange("p (k a) -> p a k", k=2), by_tile(top_at)[:, :, 0:2]))
            dve.tensor_tensor(gap, by_tile(top)[:, :, 1], by_tile(top)[:, :, 0], ALU.subtract).then_inc(e["gexp_in"], 1)
            for k in range(2):
                ins = dve.tensor_tensor(k_of(pick, k), k_of(pick, k), group_off, ALU.add)
            step(ins)
            for k in range(2):
                for tt in range(TT):
                    q = k * TT + tt
                    ins = dve.tensor_scalar(takes[:, q * EXPERTS:(q + 1) * EXPERTS], iota[:, 0:EXPERTS], pick[:, q:q + 1], None,
                                            ALU.is_equal)
            step(ins)
            half = TT * EXPERTS
            dve.tensor_tensor(takes_any, takes[:, 0:half], takes[:, half:], ALU.add).then_inc(e["picked"], 1)
            dve.wait_ge(e["gexp"], 2)
            step(dve.tensor_reduce(group_gate, by_tile(group_exp), AX, ALU.add))
            dve.reciprocal(group_gate, group_gate)
            step(dve.tensor_scalar(share[:, 0:TT], gap_exp, 1.0, None, ALU.add))
            step(dve.reciprocal(share[:, 0:TT], share[:, 0:TT]))
            step(dve.tensor_tensor(share[:, 0:TT], share[:, 0:TT], group_gate, ALU.mult))
            step(dve.tensor_tensor(share[:, TT:], share[:, 0:TT], gap_exp, ALU.mult))
            dve.wait_ge(e["ranks"], 1)
            step(dve.tensor_copy(counts, ROUTE[:, CNT:CNT + 3 * EXPERTS]))
            for dst, src, edge in ((over, count, 0.5), (tile_no, rank, -0.5)):
                step(dve.tensor_scalar(dst, src, SLOTS + edge, None, ALU.is_gt))
                for n in range(2, MAX_TILES):
                    step(dve.scalar_tensor_tensor(dst, src, n * SLOTS + edge, dst, ALU.is_gt, ALU.add))
            step(dve.tensor_tensor_scan(over_to, ones[:, 0:EXPERTS], over, 0.0, ALU.mult, ALU.add))
            step(dve.tensor_tensor(over_from, over_to, over, ALU.subtract))
            dve.scalar_tensor_tensor(place_in, tile_no, -float(SLOTS), rank, ALU.mult, ALU.add)
            step(dve.tensor_tensor(tile_base, over_from, iota[:, 0:EXPERTS], ALU.subtract))
            step(dve.tensor_scalar(tile_base, tile_base, EXPERTS - 1.0, None, ALU.add))

            def per_tile(v):
                return v.rearrange("p (o n) -> p o n", o=1).to_broadcast([P, TT, EXPERTS])
            step(dve.tensor_tensor(by_tile(item), by_tile(tile_no), per_tile(tile_base), ALU.add))
            step(dve.scalar_tensor_tensor(item, tile_no, 0.0, item, ALU.is_gt, ALU.mult))
            step(dve.tensor_tensor(by_tile(item), by_tile(item), per_tile(iota[:, 0:EXPERTS]), ALU.add))
            for table, of in ((item, item_of), (place_in, place_of)):
                step(dve.tensor_tensor(chosen.rearrange("p (k n) -> p k n", k=2), takes.rearrange("p (k n) -> p k n", k=2),
                                       table.rearrange("p (o n) -> p o n", o=1).to_broadcast([P, 2, half]), ALU.mult))
                step(dve.tensor_reduce(of, chosen.rearrange("p (q n) -> p q n", n=EXPERTS), AX, ALU.add))
            step(dve.scalar_tensor_tensor(slot_of, item_of, float(SLOTS), place_of, ALU.mult, ALU.add))
            dve.tensor_scalar(from_slot, slot_of, float(SLOTS), None, ALU.add).then_inc(e["slots"], 1)
            n = MAX_OVER

            def grid(v):
                return v.rearrange("p (j n) -> p j n", j=n)

            def along(v):
                return v.rearrange("p (o n) -> p o n", o=1).to_broadcast([P, n, EXPERTS])
            j = iota[:, 0:n].rearrange("p (j o) -> p j o", o=1).to_broadcast([P, n, EXPERTS])
            dve.tensor_tensor(grid(over_expert), along(over_from), j, ALU.is_le)
            step(dve.tensor_tensor(grid(over_test), along(over_to), j, ALU.is_gt))
            step(dve.tensor_tensor(over_expert, over_expert, over_test, ALU.mult))
            step(dve.tensor_tensor(grid(over_expert), grid(over_expert), along(iota[:, 0:EXPERTS]), ALU.mult))
            dve.tensor_reduce(plan_f[:, 1 + EXPERTS:], grid(over_expert), AX, ALU.add)
            dve.tensor_copy(plan_f[:, 1:1 + EXPERTS], iota[:, 0:EXPERTS])
            step(dve.tensor_scalar(plan_f[:, 0:1], over_to[:, EXPERTS - 1:EXPERTS], EXPERTS - 1.0, None, ALU.add))
            dve.tensor_copy(plan, plan_f).then_inc(e["plan"], 1)

        def route_pe(pe):
            turn_pe(pe, TURN_OF_NORM[8], "n8")
            pe.wait_ge(turn_low, 4 * (TURN_OF_NORM[8] + 1))
            n = GROUPS + EXPERTS
            for tt in range(TT):
                for k in range(KD):
                    tok = slice(tt * P, (tt + 1) * P)
                    ins = product(pe, ROUTE[:, tt * n:(tt + 1) * n], hT_high[:, k, tok], hT_low[:, k, tok],
                                  router_high[:, k, :], router_low[:, k, :], start=tt == 0 and k == 0)
            ins.then_inc(e["logits"], 1)
            pe.wait_ge(e["picked"], 1)
            a = [takes_any[:, tt * EXPERTS:(tt + 1) * EXPERTS] for tt in range(TT)]
            for c, terms in enumerate((((ones[:, 0:P], a[0]), (ones[:, 0:P], a[1])), ((strict[:, :], a[0]),),
                                       ((ones[:, 0:P], a[0]), (strict[:, :], a[1])))):
                for i, (lhs, rhs) in enumerate(terms):
                    ins = pe.matmul(ROUTE[:, CNT + c * EXPERTS:CNT + (c + 1) * EXPERTS], lhs, rhs, start=c == 0 and i == 0,
                                    stop=i == len(terms) - 1, skip_group_check=True)
            ins.then_inc(e["ranks"], 1)
            pe.wait_ge(e["slots"], 1)
            for q in range(2 * TT):
                ins = pe.matmul(SLOT_ROWS[:, q * P:(q + 1) * P], slot_of[:, q:q + 1].to_broadcast([P, P]), ident[:, :],
                                start=True, stop=True, skip_group_check=True)
            ins.then_inc(e["slot_rows"], 1)

        def rounds(eng):
            eng.wait_ge(e["plan"], 1)
            return eng.value_load(plan[0:1, 0:1], min_val=EXPERTS - 1, max_val=ITEMS - 1)

        def expert_gate_up_loads(sp, p, r, expert):
            for j in range(4):
                piece_loads(sp, p + j, r, gate_up_parts(p + j, experts[0][expert], experts[1][expert], j % 2, (j // 2) * CHUNK))

        def expert_down_loads(sp, p, r, expert):
            for j in range(2):
                piece_loads(sp, p + j, r, down_parts(p + j, experts[2][expert], j * 2 * P))

        def moe_sp(sp):
            expert_gate_up_loads(sp, MOE, 0, 0)
            expert_gate_up_loads(sp, BODY, 0, 1)
            expert_down_loads(sp, BODY + 4, 0, 0)
            n = rounds(sp)

            def expert_of(i):
                return sp.value_load(plan[0:1, bass.ds(i + 1, 1)], min_val=0, max_val=EXPERTS - 1)
            with sp.Fori(1, n) as i:
                expert_gate_up_loads(sp, BODY, i * 2, expert_of(i + 1))
                expert_down_loads(sp, BODY + 4, i * 2, expert_of(i))
            expert_down_loads(sp, BODY, n * 2, expert_of(n))

        def moe_pool(pool, step):
            pool.wait_ge(x_ready, X_COUNT[8] + 2)
            pool.iota(iota, pattern=[[1, SLOTS]], base=0, channel_multiplier=0, allow_small_or_imprecise_dtypes=True)
            step(pool.iota(own_slot, pattern=[[0, 1]], base=-SLOTS, channel_multiplier=1,
                           allow_small_or_imprecise_dtypes=True))
            step(pool.tensor_scalar(own_slot[SLOTS:, :], own_slot[SLOTS:, :], -float(SLOTS), None, ALU.add))
            pool.sem_inc(e["tables"], 1)
            pool.wait_ge(e["logits"], 1)
            pool.memset(y_high.bitcast(F32), 0.0)
            pool.memset(y_low.bitcast(F32), 0.0).then_inc(e["y_low"], 1)
            pool.memset(spread.bitcast(F32), 0.0).then_inc(e["spreads"], 1)

            def pick(i):
                if not isinstance(i, int) or i:
                    pool.wait_ge(e["shares"], i)
                pool.sem_inc(e["pool_passed"], 1)
                pool.tensor_scalar(from_slot, from_slot, -float(SLOTS), None, ALU.add).then_inc(e["pick_parts"], 1)
                pool.wait_ge(e["pick_parts"], i * 2 + 1)
                pool.sem_inc(e["pool_passed"], 1)
                for q in range(2 * TT):
                    ins = pool.tensor_scalar(pick_by_k[:, q * SLOTS:(q + 1) * SLOTS], iota, from_slot[:, q:q + 1], None,
                                             ALU.is_equal)
                ins.then_inc(e["pick_parts"], 1)
                pool.wait_ge(e["pick_parts"], i * 2 + 2)
                pool.tensor_tensor(picks, pick_by_k[:, 0:TT * SLOTS], pick_by_k[:, TT * SLOTS:], ALU.add).then_inc(e["picks"], 1)

            def spread_of(i):
                pool.tensor_scalar(own_slot, own_slot, float(SLOTS), None, ALU.add).then_inc(e["spread_parts"], 1)
                pool.wait_ge(e["spread_parts"], i * 3 + 1)
                pool.sem_inc(e["pool_passed"], 1)
                for k in range(2):
                    pool.tensor_scalar(spread_part[:, k * TOKENS:(k + 1) * TOKENS], slot_rows[:, k * TOKENS:(k + 1) * TOKENS],
                                       own_slot, None, ALU.is_equal).then_inc(e["spread_parts"], 1)
                pool.wait_ge(e["scattered"], i + 1)
                pool.wait_ge(e["spread_parts"], i * 3 + 3)
                pool.tensor_tensor(spread, spread_part[:, 0:TOKENS], spread_part[:, TOKENS:],
                                          ALU.add).then_inc(e["spreads"], 1)

            pool.wait_ge(e["slots"], 1)
            pick(0)
            pick(1)
            pool.wait_ge(e["slot_rows_sb"], 1)
            n = rounds(pool)
            with pool.Fori(0, n) as i:
                pick(i + 2)
                spread_of(i)
            spread_of(n)

        def moe_pe(pe):
            route_pe(pe)

            def turn_rows(i):
                pe.wait_ge(e["picks"], i + 1)
                for k in range(KD):
                    for tt in range(TT):
                        ins = pe.matmul(GU[0][:, k * SLOTS:(k + 1) * SLOTS], h[:, tt, k * P:(k + 1) * P],
                                        picks[:, tt * SLOTS:(tt + 1) * SLOTS], start=tt == 0, stop=tt == TT - 1,
                                        skip_group_check=True)
                ins.then_inc(e["x_turned"], 1)

            def shares():
                for q in range(2 * TT):
                    ins = pe.matmul(GU[1][0:SLOTS, 4 * SLOTS:4 * SLOTS + 1], pick_by_k[:, q * SLOTS:(q + 1) * SLOTS],
                                    share[:, q:q + 1], start=q == 0, stop=q == 2 * TT - 1, skip_group_check=True)
                ins.then_inc(e["shares"], 1)

            def both_parts(out, lhs, rhs_high, rhs_low, start, stop):
                pe.matmul(out, lhs, rhs_high, start=start, stop=False, skip_group_check=True)
                return pe.matmul(out, lhs, rhs_low, start=False, stop=stop, skip_group_check=True)

            def gate_up(j, p, r):
                q = p + j
                pe.wait_ge(split, q + 1 + scales_with(r, 3))
                for k in range(4):
                    kk = 4 * (j % 2) + k
                    ins = both_parts(GU[j // 2], XT[:, kk, :], four_k(high, q)[:, k, :], four_k(low, q)[:, k, :],
                                     start=kk == 0, stop=kk == KD - 1)
                ins.then_inc(used, 1)

            def turn_inner(i):
                pe.wait_ge(e["act"], i * 2 + 2)
                pe.sem_inc(e["pe_passed"], 1)
                for f in range(4):
                    ins = pe.transpose(GU[1][:, f * SLOTS:(f + 1) * SLOTS], act_tok[0:SLOTS, f // 2, (f % 2) * P:(f % 2 + 1) * P],
                                       ident[0:SLOTS, 0:SLOTS])
                ins.then_inc(e["a_turned"], 1)

            def down(p, r):
                for j in range(2):
                    q = p + j
                    pe.wait_ge(split, q + 1 + scales_with(r, 3))
                    for k in range(2):
                        f = 2 * j + k
                        for c in range(2):
                            cols = slice(c * BANK, (c + 1) * BANK)
                            ins = both_parts(ITEM_Y[:, cols], AT[:, f, :], two_k(high, q)[:, k, cols],
                                             two_k(low, q)[:, k, cols], start=f == 0, stop=f == 3)
                    ins.then_inc(used, 1)

            def scatter(i):
                pe.wait_ge(e["y_low"], i + 1)
                pe.wait_ge(e["spreads"], i + 1)
                for part in (y_high, y_low):
                    for tt in range(TT):
                        for c in range(2):
                            cols = slice(c * BANK, (c + 1) * BANK)
                            ins = pe.matmul(Y[tt][:, cols], spread[:, tt * P:(tt + 1) * P], part[:, cols], start=False,
                                            stop=False, skip_group_check=True)
                ins.then_inc(e["scattered"], 1)

            pe.wait_ge(x_ready, X_COUNT[8] + 2)
            clear_Y(pe)
            turn_rows(0)
            shares()
            pe.wait_ge(e["x_low"], 1)
            for j in range(2):
                gate_up(j, MOE, 0)
            pe.wait_ge(e["share_sb"], 1)
            for j in range(2, 4):
                gate_up(j, MOE, 0)
            n = rounds(pe)
            pe.wait_ge(e["gu_sum"], 1)
            turn_rows(1)
            with pe.Fori(0, n) as i:
                pe.wait_ge(e["x_low"], i + 2)
                gate_up(0, BODY, i * 2)
                pe.wait_ge(e["act"], i * 2 + 2)
                shares()
                turn_inner(i)
                gate_up(1, BODY, i * 2)
                scatter(i)
                pe.wait_ge(e["a_low"], i + 1)
                pe.wait_ge(e["share_sb"], i + 2)
                for j in range(2, 4):
                    gate_up(j, BODY, i * 2)
                pe.wait_ge(e["gu_sum"], i * 2 + 3)
                turn_rows(i + 2)
                down(BODY + 4, i * 2)
            turn_inner(n)
            scatter(n)
            pe.wait_ge(e["a_low"], n + 1)
            down(BODY, n * 2)
            scatter(n + 1)

        slots_x = GU[0].rearrange("p (k n) -> p k n", n=SLOTS)
        slots_a = GU[1][:, 0:4 * SLOTS].rearrange("p (k n) -> p k n", n=SLOTS)

        def moe_act(act):
            act.wait_ge(e["gexp_in"], 1)
            act.activation(group_exp, group_exp, ACT.Exp).then_inc(e["gexp"], 1)
            act.wait_ge(e["gexp_in"], 2)
            act.activation(gap_exp, gap, ACT.Exp).then_inc(e["gexp"], 1)

            def inner_high(i):
                act.wait_ge(e["a_turned"], i + 1)
                act.activation(AT[:, :, 0:SLOTS], slots_a, ACT.Copy).then_inc(e["a_high"], 1)

            def rows_high(i):
                act.wait_ge(e["x_turned"], i + 1)
                act.activation(XT[:, :, 0:SLOTS], slots_x, ACT.Copy).then_inc(e["x_high"], 1)

            def rest(chunk, used_value):
                act.wait_ge(used, used_value)
                act.activation(gu_rest[chunk][0:SLOTS, :], GU[chunk][SLOTS:P, :], ACT.Copy).then_inc(e["gu_rest"], 1)

            def silu(chunk, count):
                act.wait_ge(e["gu_sum"], count)
                act.activation(gate[0:SLOTS, chunk, :], gu_sum[chunk][0:SLOTS, 0:CHUNK], ACT.Silu).then_inc(e["silu"], 1)

            def result(used_value):
                act.wait_ge(used, used_value)
                act.activation(y_high, ITEM_Y, ACT.Copy).then_inc(e["y_high"], 1)

            round_piece(act, MOE + 2)
            act.wait_ge(e["slot_rows"], 1)
            act.activation(slot_rows, SLOT_ROWS, ACT.Copy).then_inc(e["slot_rows_sb"], 1)
            rows_high(0)
            round_piece(act, MOE + 3)
            rest(0, MOE + 2)
            round_piece(act, BODY)
            silu(0, 1)
            round_piece(act, BODY + 1)
            rest(1, MOE + 4)
            rows_high(1)
            silu(1, 2)
            n = rounds(act)
            with act.Fori(0, n) as i:
                r = i * 2
                round_piece(act, BODY + 2, r)
                inner_high(i)
                round_piece(act, BODY + 3, r)
                rest(0, i * 6 + (BODY + 2))
                round_piece(act, BODY + 4, r)
                silu(0, i * 2 + 3)
                round_piece(act, BODY + 5, r)
                rest(1, i * 6 + (BODY + 4))
                rows_high(i + 2)
                round_piece(act, BODY + 6, r)
                silu(1, i * 2 + 4)
                round_piece(act, BODY + 7, r)
                result(i * 6 + (BODY + 6))
            inner_high(n)
            result(n * 6 + (BODY + 2))

        def moe_dve(dve, step):
            route_dve(dve, step)

            def inner_low(i):
                dve.wait_ge(e["a_high"], i + 1)
                dve.tensor_tensor(AT[:, :, SLOTS:P], slots_a, AT[:, :, 0:SLOTS].bitcast(F32),
                                  ALU.subtract).then_inc(e["a_low"], 1)

            def rows_low(i):
                dve.wait_ge(e["x_high"], i + 1)
                dve.tensor_tensor(XT[:, :, SLOTS:P], slots_x, XT[:, :, 0:SLOTS].bitcast(F32),
                                  ALU.subtract).then_inc(e["x_low"], 1)

            def share_out(count):
                dve.wait_ge(e["shares"], count)
                dve.tensor_copy(share_slot[0:SLOTS, :], GU[1][0:SLOTS, 4 * SLOTS:4 * SLOTS + 1]).then_inc(e["share_sb"], 1)

            def add_rest(chunk, count):
                dve.wait_ge(e["gu_rest"], count)
                dve.tensor_tensor(gu_sum[chunk][0:SLOTS, :], GU[chunk][0:SLOTS, :], gu_rest[chunk][0:SLOTS, :],
                                  ALU.add).then_inc(e["gu_sum"], 1)

            def inner(chunk, count):
                dve.wait_ge(e["silu"], count)
                if isinstance(count, int) and count == 1:
                    dve.wait_ge(e["share_sb"], 1)
                dve.scalar_tensor_tensor(act_tok[0:SLOTS, chunk, :], gate[0:SLOTS, chunk, :], share_slot[0:SLOTS, :],
                                         gu_sum[chunk][0:SLOTS, CHUNK:2 * CHUNK], ALU.mult, ALU.mult).then_inc(e["act"], 1)

            def result(i):
                dve.wait_ge(e["y_high"], i + 1)
                dve.tensor_tensor(y_low, ITEM_Y, y_high.bitcast(F32), ALU.subtract).then_inc(e["y_low"], 1)

            split_piece(dve, MOE + 2)
            rows_low(0)
            share_out(1)
            split_piece(dve, MOE + 3)
            add_rest(0, 1)
            split_piece(dve, BODY)
            inner(0, 1)
            split_piece(dve, BODY + 1)
            add_rest(1, 2)
            rows_low(1)
            inner(1, 2)
            n = rounds(dve)
            with dve.Fori(0, n) as i:
                r = i * 2
                split_piece(dve, BODY + 2, r)
                inner_low(i)
                share_out(i + 2)
                split_piece(dve, BODY + 3, r)
                add_rest(0, i * 2 + 3)
                split_piece(dve, BODY + 4, r)
                inner(0, i * 2 + 3)
                split_piece(dve, BODY + 5, r)
                add_rest(1, i * 2 + 4)
                rows_low(i + 2)
                split_piece(dve, BODY + 6, r)
                inner(1, i * 2 + 4)
                split_piece(dve, BODY + 7, r)
                result(i)
            inner_low(n)
            result(n)
            dve.wait_ge(e["scattered"], n + 2)
            for tt in range(TT):
                dve.tensor_tensor(x[:, tt, :], Y[tt], x[:, tt, :], ALU.add).then_inc(final, 1)

        block = ctx.enter_context(nc.Block())

        @block.sync
        def _(sp):
            sp.dma_start(x[:, :, :], t["x"][0].rearrange("(a p) n -> p a n", p=P)).then_inc(x_loaded, 16)
            ffn_loads(sp, 0)
            if STOP == "ffn0":
                for half in range(2):
                    piece_loads(sp, 33+half, 0, in_parts(33+half, w_in["gla_in"], half, 0))
                return
            in_loads(sp, "gla_in")
            out_loads(sp, "gla_out")
            if STOP == "gla":
                b = FIRST_PIECE["ffn1"]
                for half in range(2):
                    piece_loads(sp, b + half, 0, gate_up_parts(b + half, ffns[1][0], ffns[1][1], half, 0))
                return
            ffn_loads(sp, 1)
            ffn_loads(sp, 2)
            in_loads(sp, "sb_in")
            out_loads(sp, "sb_out")
            ffn_loads(sp, 3)
            in_loads(sp, "mix_in")
            out_loads(sp, "mix_out")
            if STOP == "mix":
                b = FIRST_PIECE["experts"]
                for half in range(2):
                    piece_loads(sp, b + half, 0, gate_up_parts(b + half, ffns[1][0], ffns[1][1], half, 0))
                return
            moe_sp(sp)
            for tt in range(TT):
                sp.wait_ge(final, tt + 1)
                sp.dma_start(out[0, tt * P:(tt + 1) * P, :], x[:, tt, :]).then_inc(stored_out, 16)
            sp.wait_ge(stored_out, TT * 16)

        @block.gpsimd
        def _(pool):
            n_steps = [0]

            def step(ins):
                n_steps[0] += 1
                ins.then_inc(pool_step, 1)
                pool.wait_ge(pool_step, n_steps[0])

            def select(v, op, fill, base, pattern, by_partition):
                step(nc.gpsimd.affine_select(out=v, in_=v, compare_op=op, fill=fill, base=base, pattern=pattern,
                                             channel_multiplier=by_partition))

            for k in range(2):
                pool.dma_start(gain[:, k, :], gains[k].partition_broadcast(P)).then_inc(gain_loaded[k], 16)
            pool.dma_start(wgk2[:, :], t["gla_w_gk2"][0]).then_inc(small_loaded, 16)
            pool.dma_start(bgk[:, :], t["gla_b_gk"][0].rearrange("(a p) -> p a", p=P),
                           allow_slow_non_contiguous=True).then_inc(small_loaded, 16)
            pool.dma_start(gla_gain[:, :], t["gla_o_norm"][0].partition_broadcast(P)).then_inc(small_loaded, 16)
            pool.dma_start(gkw[:, :, :], t["gla_w_in"][0][:, IN_CHUNKS * BANK:].rearrange("(k p) n -> p k n", p=P)
                           ).then_inc(small_loaded, 16)
            for dst, src in ((router[:, :, 0:GROUPS], t["w_router_group_2"]), (router[:, :, GROUPS:], t["w_router_expert_2"])):
                pool.dma_start(dst, src[0].rearrange("(k p) n -> p k n", p=P)).then_inc(small_loaded, 16)
            pool.memset(eps[:, :], EPS).then_inc(eps_set, 1)
            pool.memset(ident[:, :], 0.0)
            pool.memset(zero_r[:, :].bitcast(F32), 0.0)
            pool.memset(ones[:, :], 1.0)
            pool.memset(suffix[:, :], 1.0)
            pool.memset(strict[:, :], 1.0)
            pool.memset(levels[:, :, :], 0.0)
            step(pool.memset(causal[:, :], 0.0))
            select(ident[:, :], ALU.not_equal, 1.0, 0, [[-1, P]], 1)
            pool.dma_start(conv_rows[0:CONV_W - 1, :], zero_r[0:CONV_W - 1, :].bitcast(F32)).then_inc(m["zeros"], 16)
            select(suffix[:, :], ALU.is_ge, 0.0, 0, [[-1, P]], 1)
            select(strict[:, :], ALU.is_gt, 0.0, 0, [[1, P]], -1)
            for c in (0, 2):
                select(causal[:, c * P:(c + 1) * P], ALU.is_ge, NEG, 0, [[-1, P]], 1)
            for j, B in enumerate(LEVELS):
                n = P // (2 * B)
                late = levels[:, j, :].rearrange("p (m n) -> p m n", n=2 * B)[:, :, B:2 * B]
                step(pool.memset(late, 1.0))
                select(late, ALU.is_ge, 0.0, 0, [[-2 * B, n], [0, B]], 1)
                select(late, ALU.is_ge, 0.0, B - 1, [[2 * B, n], [0, B]], -1)
            pool.memset(gscore, 0.0).then_inc(consts, 1)
            for k in range(2, 9):
                if k - 2 != 6:
                    pool.wait_ge(h_ready, 2 * H_ORDER.index(f"n{k - 2}") + 2)
                else:
                    pool.wait_ge(x_ready, 14)
                pool.dma_start(gain[:, k % 2, :], gains[k].partition_broadcast(P)).then_inc(gain_loaded[k % 2], 16)
                if STOP == "gla" and k == 3: return
                if STOP == "ffn0" and k == 2: return
                if k == 7:
                    mix_pool(pool, step)
            mix_conv_pool(pool, step)
            if STOP == "mix": return
            moe_pool(pool, step)

        @block.scalar
        def _(act):
            n_steps = [0]

            def step(ins):
                n_steps[0] += 1
                ins.then_inc(act_step, 1)
                act.wait_ge(act_step, n_steps[0])

            round_piece(act, 0)
            round_piece(act, 1)
            norm_act(act, 0)
            turn_act(act, 0)
            ffn_act(act, 0)
            norm_act(act, 1)
            if STOP == "ffn0": return
            act.wait_ge(small_loaded, 96)
            act.activation(flat(router_high), flat(router), ACT.Copy)
            act.activation(flat(gkw_high), flat(gkw), ACT.Copy).then_inc(small_high, 1)
            turn_act(act, 1)
            act.wait_ge(g["rank"], 1)
            act.activation(grank, TURN_A[:, 0:TT * GLA_RANK], ACT.Copy).then_inc(g["rank_sb"], 1)
            gla_act(act, step)
            norm_act(act, 2)
            if STOP == "gla": return
            turn_act(act, TURN_OF_NORM[2])
            ffn_act(act, 1)
            norm_act(act, 3)
            turn_act(act, TURN_OF_NORM[3])
            ffn_act(act, 2)
            norm_act(act, 4)
            turn_act(act, TURN_OF_NORM[4])
            sb_act(act, step)
            norm_act(act, 5)
            turn_act(act, TURN_OF_NORM[5])
            ffn_act(act, 3)
            norm_act(act, 6)
            norm_act(act, 7)
            turn_act(act, TURN_OF_NORM[7])
            mix_act(act, step)
            norm_act(act, 8)
            if STOP == "mix": return
            turn_act(act, TURN_OF_NORM[8])
            moe_act(act)

        @block.vector
        def _(dve):
            n_steps = [0]

            def step(ins):
                n_steps[0] += 1
                ins.then_inc(dve_step, 1)
                dve.wait_ge(dve_step, n_steps[0])

            split_piece(dve, 0)
            split_piece(dve, 1)
            norm_dve(dve, step, 0, 0, None)
            turn_dve(dve, 0)
            ffn_dve(dve, 0)
            norm_dve(dve, step, 1, 0.5, FIRST_PIECE["gla_in"] - 1)
            if STOP == "ffn0": return
            dve.wait_ge(small_high, 1)
            dve.tensor_tensor(flat(router_low), flat(router), flat(router_high).bitcast(F32), ALU.subtract)
            dve.tensor_tensor(flat(gkw_low), flat(gkw), flat(gkw_high).bitcast(F32), ALU.subtract).then_inc(small_low, 1)
            turn_dve(dve, 1)
            gla_dve(dve, step)
            norm_dve(dve, step, 2, 1.0, FIRST_PIECE["ffn1"] - 1)
            if STOP == "gla": return
            turn_dve(dve, TURN_OF_NORM[2])
            ffn_dve(dve, 1)
            norm_dve(dve, step, 3, 0.5, FIRST_PIECE["ffn2"] - 1)
            turn_dve(dve, TURN_OF_NORM[3])
            ffn_dve(dve, 2)
            norm_dve(dve, step, 4, 0.5, FIRST_PIECE["sb_in"] - 1)
            turn_dve(dve, TURN_OF_NORM[4])
            sb_dve(dve, step)
            norm_dve(dve, step, 5, 1.0, FIRST_PIECE["ffn3"] - 1)
            turn_dve(dve, TURN_OF_NORM[5])
            ffn_dve(dve, 3)
            norm_dve(dve, step, 6, 0.5, FIRST_PIECE["mix_in"] - 1)
            norm_dve(dve, step, 7, 0, None)
            turn_dve(dve, TURN_OF_NORM[7])
            mix_dve(dve, step)
            norm_dve(dve, step, 8, 1.0, FIRST_PIECE["experts"] - 1)
            if STOP == "mix": return
            turn_dve(dve, TURN_OF_NORM[8])
            moe_dve(dve, step)

        @block.tensor
        def _(pe):
            turn_pe(pe, 0, "n0")
            ffn_pe(pe, 0, 0)
            if STOP == "ffn0": return
            turn_pe(pe, 1, "n1")
            gla_pe(pe)
            if STOP == "gla": return
            turn_pe(pe, TURN_OF_NORM[2], "n2")
            ffn_pe(pe, 1, TURN_OF_NORM[2])
            turn_pe(pe, TURN_OF_NORM[3], "n3")
            ffn_pe(pe, 2, TURN_OF_NORM[3])
            turn_pe(pe, TURN_OF_NORM[4], "n4")
            sb_pe(pe)
            turn_pe(pe, TURN_OF_NORM[5], "n5")
            ffn_pe(pe, 3, TURN_OF_NORM[5])
            turn_pe(pe, TURN_OF_NORM[7], "n7")
            mix_pe(pe)
            if STOP == "mix": return
            moe_pe(pe)


_INS = ["x", "ffn1_norm", "ffn1_w_gate", "ffn1_w_up", "ffn1_w_down", "mix_norm", "ffn2_norm", "ffn2_w_gate",
        "ffn2_w_up", "ffn2_w_down", "gla_w_in", "gla_w_gk2", "gla_b_gk", "gla_o_norm", "gla_w_out", "sb_w_in",
        "sb_w_out", "final_norm", "attn_norm_g_2", "w_in_2", "conv_w_2", "conv_out_g_2", "q_norm_g_2", "k_norm_g_2",
        "lambda_q1_2", "lambda_k1_2", "lambda_q2_2", "lambda_k2_2", "attn_subln_g_2", "w_out_2", "ffn_norm_g_2",
        "w_router_group_2", "w_router_expert_2", "w_exp_gate_2", "w_exp_up_2", "w_exp_down_2"]


def arrays_of(inputs):
    return {f"in_{n}": np.ascontiguousarray(inputs[n]) for n in _INS}


def declare_and_build(nc, arrays):
    t = {n: nc.dram_tensor(f"in_{n}", arrays[f"in_{n}"].shape, F32, kind="ExternalInput").ap() for n in _INS}
    out = nc.dram_tensor("out", (1, TOKENS, D), F32, kind="ExternalOutput").ap()
    build(nc, t, out)


def kernel(**inputs):
    import concourse.bacc as bacc
    from concourse.bass_utils import run_bass_kernel_spmd

    nc = bacc.Bacc("TRN2", target_bir_lowering=False, num_devices=1)
    arrays = arrays_of(inputs)
    declare_and_build(nc, arrays)
    result = run_bass_kernel_spmd(nc, [arrays], core_ids=[0])
    return result.results[0]["out"]
```

```python
from contextlib import ExitStack

import numpy as np

import concourse.bass as bass
from concourse import mybir

F32 = mybir.dt.float32
F32R = mybir.dt.float32r
I32 = mybir.dt.int32
U32 = mybir.dt.uint32
ALU = mybir.AluOpType
ACT = mybir.ActivationFunctionType
AX = mybir.AxisListType.X

P = 128
TOKENS = 256
TT = TOKENS // P
D = 1024
KD = D // P
EPS = 1e-6
BANK = 512
SLOT = 2048
RING = 3

D_FF = 2816
CHUNK = 256
N_CHUNKS = D_FF // CHUNK
FFN_PIECES = 3 * N_CHUNKS
IN_CHUNKS = 6
IN_PIECES = 2 * IN_CHUNKS
OUT_PIECES = 4
HALF_D = 512

GLA_HEADS, GLA_K, GLA_V, GLA_RANK = 4, 128, 256, 16
GLA_TAU = 16.0
GLA_COLS = IN_CHUNKS * BANK + GLA_RANK
LEVELS = [64, 32, 16, 8, 4, 2, 1]

SB_HEADS, SB_HD = 16, 64
GROUP = 4
SB_GROUPS = SB_HEADS // GROUP

DA_HEADS, DA_HD, DA_V = 4, 64, 128
D_CONV = 512
CONV_W = 3
LAMBDA_INIT = 0.8 - 0.6 * float(np.exp(-0.3 * 0))
NEG = -1e30

GROUPS, PER_GROUP, EXPERTS = 4, 8, 32
D_EXP = 512
SLOTS = 64
MAX_OVER = 2 * TOKENS // (SLOTS + 1)
MAX_TILES = TOKENS // SLOTS
ITEMS = EXPERTS + MAX_OVER

FIRST_PIECE = {}
_at = 0
for _name, _n in [("ffn0", FFN_PIECES), ("gla_in", IN_PIECES), ("gla_out", OUT_PIECES), ("ffn1", FFN_PIECES),
                  ("ffn2", FFN_PIECES), ("sb_in", IN_PIECES), ("sb_out", OUT_PIECES), ("ffn3", FFN_PIECES),
                  ("mix_in", IN_PIECES), ("mix_out", OUT_PIECES), ("experts", 0)]:
    FIRST_PIECE[_name] = _at
    _at += _n


def build(nc, t, out):
    ctx = ExitStack()
    with ctx:
        def sb(name, shape, dt=F32):
            return ctx.enter_context(nc.sbuf_tensor(name, shape, dt))

        def sem(name):
            return ctx.enter_context(nc.semaphore(name))

        raw = sb("raw", [P, RING, SLOT])
        high = sb("high", [P, RING, SLOT], F32R)
        low = sb("low", [P, RING, SLOT], F32R)
        hT_high = sb("hT_high", [P, KD, TOKENS], F32R)
        hT_low = sb("hT_low", [P, KD, TOKENS], F32R)
        aT_high = sb("aT_high", [P, 2, TOKENS], F32R)
        aT_low = sb("aT_low", [P, 2, TOKENS], F32R)
        zero_r = sb("zero_r", [P, BANK], F32R)
        x = sb("x", [P, TT, D])
        h = sb("h", [P, TT, D])
        gate = sb("gate", [P, TT, CHUNK])
        act_tok = sb("act_tok", [P, TT, CHUNK])
        gain = sb("gain", [P, 2, D])
        square = sb("square", [P, D])
        proj = sb("proj", [P, TT, GLA_COLS])
        stat = sb("stat", [P, 64])
        eps = sb("eps", [P, 1])
        ident = sb("ident", [P, P])
        ones = sb("ones", [P, TOKENS])
        suffix = sb("suffix", [P, P])
        strict = sb("strict", [P, P])
        causal = sb("causal", [P, 3 * P])
        levels = sb("levels", [P, len(LEVELS), P])
        wgk2 = sb("wgk2", [GLA_RANK, GLA_HEADS * GLA_K])
        bgk = sb("bgk", [P, GLA_HEADS])
        gla_gain = sb("gla_gain", [P, GLA_V])
        gkw = sb("gkw", [P, KD, GLA_RANK])
        gkw_high = sb("gkw_high", [P, KD, GLA_RANK], F32R)
        gkw_low = sb("gkw_low", [P, KD, GLA_RANK], F32R)
        router = sb("router", [P, KD, GROUPS + EXPERTS])
        router_high = sb("router_high", [P, KD, GROUPS + EXPERTS], F32R)
        router_low = sb("router_low", [P, KD, GROUPS + EXPERTS], F32R)
        SCRATCH = 10752
        scratch = sb("scratch", [P, SCRATCH])

        class Area:

            def __init__(self):
                self.at = 0

            def take(self, n):
                self.at += n
                assert self.at <= SCRATCH, self.at
                return scratch[:, self.at - n:self.at]

        psum = ctx.enter_context(nc.psum_tensor("psum", [P, 8, BANK], F32))

        def banks(a, n=1):
            return psum[:, a:a + n, :].rearrange("p b n -> p (b n)")

        Y = [banks(0, 2), banks(2, 2)]
        GU = [banks(4), banks(5)]
        TURN_A = banks(6)
        TURN_X = banks(7)

        conv_rows = nc.dram_tensor("conv_rows", (TOKENS + CONV_W - 1, D_CONV), F32, kind="Internal").ap()

        landed = [sem(f"landed{i}") for i in range(2 * RING)]
        rounded, split, used = sem("rounded"), sem("split"), sem("used")
        consts = sem("consts")
        pool_step, dve_step, act_step = sem("pool_step"), sem("dve_step"), sem("act_step")
        x_loaded, gain_loaded = [sem("x_loaded0"), sem("x_loaded1")], [sem("gain_loaded0"), sem("gain_loaded1")]
        small_loaded, mix_loaded = sem("small_loaded"), sem("mix_loaded")
        small_high, small_low = sem("small_high"), sem("small_low")
        x_ready, squares, h_ready = sem("x_ready"), sem("squares"), sem("h_ready")
        y_first = sem("y_first")
        roots, eps_set = sem("roots"), sem("eps_set")
        turned, turn_high, turn_low = sem("turned"), sem("turn_high"), sem("turn_low")
        gu_first, gate_ready, act_ready = sem("gu_first"), sem("gate_ready"), sem("act_ready")
        a_turned, a_high, a_low = sem("a_turned"), sem("a_high"), sem("a_low")
        in_first, in_copied = sem("in_first"), [sem("in_copied0"), sem("in_copied1")]
        g = {n: sem("gla_" + n) for n in ("rank", "rank_sb", "rankT", "rankT_sb", "z", "z_read", "ln", "qkT", "q_sb",
                                          "k_sb", "diff", "decay", "scaled", "scores", "kept", "out", "sq", "silu", "summed", "roots")}
        s = {n: sem("sb_" + n) for n in ("qkT", "qk_sb", "z", "z_sb", "ln", "sp", "sums", "arg", "exp", "w",
                                         "out", "out_sb", "even")}
        m = {n: sem("mix_" + n) for n in ("u", "zeros", "stored", "shifted", "qk", "qkT", "q_sb", "k_sb", "dots",
                                          "bias", "exp", "a", "aT", "aT_sb", "out", "sq", "lam", "lam_exp",
                                          "qk_sq", "qk_sum", "qk_root", "dots_sb", "conv", "sum", "root")}
        e = {n: sem("moe_" + n) for n in ("logits", "gexp_in", "gexp", "picked", "ranks", "slots", "slot_rows",
                                          "slot_rows_sb", "plan", "tables", "pick_parts", "picks", "x_turned",
                                          "x_high", "x_low", "gu_rest", "gu_sum", "shares", "share_sb", "silu", "act",
                                          "a_turned", "a_high", "a_low", "y_high", "y_low", "spread_parts", "spreads",
                                          "scattered", "pe_passed", "pool_passed")}
        final, stored_out = sem("final"), sem("stored_out")

        w_in = {"gla_in": t["gla_w_in"][0], "sb_in": t["sb_w_in"][0], "mix_in": t["w_in_2"][0]}
        w_out = {"gla_out": t["gla_w_out"][0], "sb_out": t["sb_w_out"][0], "mix_out": t["w_out_2"][0]}
        ffns = [(t[f"ffn{1 + i % 2}_w_gate"][i // 2], t[f"ffn{1 + i % 2}_w_up"][i // 2],
                 t[f"ffn{1 + i % 2}_w_down"][i // 2]) for i in range(4)]
        gains = [t["ffn1_norm"][0], t["mix_norm"][0], t["ffn2_norm"][0], t["ffn1_norm"][1], t["mix_norm"][1],
                 t["ffn2_norm"][1], t["final_norm"], t["attn_norm_g_2"][0], t["ffn_norm_g_2"][0]]
        TURN_OF_NORM = {0: 0, 1: 1, 2: 3, 3: 4, 4: 5, 5: 7, 7: 8, 8: 10}
        GLA_TURN, SB_TURN, MIX_TURN = 2, 6, 9
        H_ORDER = ["n0", "n1", "gla", "n2", "n3", "n4", "sb", "n5", "n7", "mix", "n8"]

        def scales_with(r, n):
            return 0 if isinstance(r, int) and r == 0 else r * n

        MOE = FIRST_PIECE["experts"]
        more_raw = scratch[:, SCRATCH - RING * SLOT:]

        def raw_of(p):
            if p < MOE or p % (2 * RING) < RING:
                return raw[:, p % RING, :]
            return more_raw[:, (p % RING) * SLOT:(p % RING + 1) * SLOT]

        def landed_of(p, r):
            if p < MOE:
                return landed[p % RING], 32 * (p // RING + 1) + scales_with(r, 32)
            before = MOE // RING if p % (2 * RING) < RING else 0
            return landed[p % (2 * RING)], 32 * (before + (p - MOE) // (2 * RING) + 1) + scales_with(r, 16)

        def piece_loads(sp, p, r, parts):
            slots = RING if p < MOE + RING else 2 * RING
            if p >= RING or not isinstance(r, int):
                sp.wait_ge(split, p - slots + 1 + scales_with(r, 3))
            if p == MOE + RING:
                sp.wait_ge(h_ready, 2 * H_ORDER.index("mix") + TT)
            for dst, src in parts:
                sp.dma_start(dst, src).then_inc(landed_of(p, r)[0], 16)

        def round_piece(act, p, r=0):
            act.wait_ge(*landed_of(p, r))
            if p >= RING or not isinstance(r, int):
                act.wait_ge(used, p - RING + 1 + scales_with(r, 3))
            act.activation(high[:, p % RING, :], raw_of(p), ACT.Copy).then_inc(rounded, 1)

        def split_piece(dve, p, r=0):
            dve.wait_ge(rounded, p + 1 + scales_with(r, 3))
            dve.tensor_tensor(low[:, p % RING, :], raw_of(p), high[:, p % RING, :].bitcast(F32),
                              ALU.subtract).then_inc(split, 1)

        def product(pe, psum_out, lhs_high, lhs_low, rhs_high, rhs_low, start, stop=False):
            pe.matmul(psum_out, lhs_high, rhs_high, start=start, stop=False, skip_group_check=True)
            pe.matmul(psum_out, lhs_high, rhs_low, start=False, stop=False, skip_group_check=True)
            return pe.matmul(psum_out, lhs_low, rhs_high, start=False, stop=stop, skip_group_check=True)

        def gate_up_parts(p, w_gate, w_up, half, col):
            dst = raw_of(p).rearrange("p (k n) -> p k n", k=4)
            rows = slice(half * 4 * P, (half + 1) * 4 * P)
            return [(dst[:, :, i * CHUNK:(i + 1) * CHUNK],
                     w[rows, bass.ds(col, CHUNK)].rearrange("(k p) n -> p k n", p=P)) for i, w in enumerate((w_gate, w_up))]

        def down_parts(p, w_down, row):
            dst = raw_of(p).rearrange("p (k n) -> p k n", k=2)
            src = w_down[bass.ds(row, 2 * P), :].rearrange("(k p) n -> p k n", p=P)
            return [(dst[:, i, :], src[:, i, :]) for i in range(2)]

        def in_parts(p, w, half, n, name):
            dst = raw_of(p).rearrange("p (k n) -> p k n", k=4)
            src = w[half * 4 * P:(half + 1) * 4 * P, columns(name, n)].rearrange("(k p) n -> p k n", p=P)
            return [(dst[:, 2 * i:2 * i + 2, :], src[:, 2 * i:2 * i + 2, :]) for i in range(2)]

        def four_k(buf, p):
            return buf[:, p % RING, :].rearrange("p (k n) -> p k n", k=4)

        def two_k(buf, p):
            return buf[:, p % RING, :].rearrange("p (k n) -> p k n", k=2)

        def ffn_loads(sp, i, after_first=lambda: None):
            b = FIRST_PIECE[f"ffn{i}"]
            w_gate, w_up, w_down = ffns[i]
            for half in range(2):
                piece_loads(sp, b + half, 0, gate_up_parts(b + half, w_gate, w_up, half, 0))
                if half == 0:
                    after_first()
            with sp.Fori(0, N_CHUNKS - 1) as c:
                for half in range(2):
                    piece_loads(sp, b + 2 + half, c, gate_up_parts(b + 2 + half, w_gate, w_up, half, (c + 1) * CHUNK))
                piece_loads(sp, b + 4, c, down_parts(b + 4, w_down, c * CHUNK))
            last = b + FFN_PIECES - 1
            piece_loads(sp, last, 0, down_parts(last, w_down, (N_CHUNKS - 1) * CHUNK))

        def in_loads(sp, name):
            for n in range(IN_CHUNKS):
                for half in range(2):
                    p = FIRST_PIECE[name] + 2 * n + half
                    piece_loads(sp, p, 0, in_parts(p, w_in[name], half, n, name))

        def out_loads(sp, name):
            for j in range(OUT_PIECES):
                p = FIRST_PIECE[name] + j
                piece_loads(sp, p, 0, down_parts(p, w_out[name], j * 2 * P))

        X_COUNT = {1: 0, 2: 2, 3: 4, 4: 6, 5: 8, 6: 10, 8: 14}
        Y_COUNT = {1: 0, 2: 1, 3: 2, 4: 3, 5: 4, 6: 5, 8: 6}

        def x_count(k, tt):
            if k == 7:
                return X_COUNT[6] + 2 * tt + 2
            return X_COUNT[k] + (2 * tt if k == 6 else tt) + 1

        def norm_no(k, tt):
            return 12 + 2 * tt + k - 6 if k in (6, 7) else 2 * k + tt

        def add_y(dve, k, tt, scale, last_piece):
            if tt == 0:
                dve.wait_ge(y_first, Y_COUNT[k] + 1)
            else:
                dve.wait_ge(used, last_piece + 1)
            dve.scalar_tensor_tensor(x[:, tt, :], Y[tt], scale, x[:, tt, :], ALU.mult, ALU.add).then_inc(x_ready, 1)

        def scale_x(dve, step, k, tt):
            dve.wait_ge(roots, norm_no(k, tt) + 1)
            step(dve.reciprocal(stat[:, 4 + tt:5 + tt], stat[:, 2 + tt:3 + tt]))
            if tt == 0:
                dve.wait_ge(gain_loaded[k % 2], 16 * (k // 2 + 1))
            if k:
                dve.wait_ge(x_ready, x_count(k, tt))
            to = x if k == 6 else h
            dve.scalar_tensor_tensor(to[:, tt, :], x[:, tt, :], stat[:, 4 + tt:5 + tt], gain[:, k % 2, :], ALU.mult,
                                     ALU.mult).then_inc(x_ready if k == 6 else h_ready, 1)

        def norm_dve(dve, step, k, scale, last_piece):
            n = TURN_OF_NORM[k]
            add_y(dve, k, 0, scale, last_piece)
            scale_x(dve, step, k, 0)
            add_y(dve, k, 1, scale, last_piece)
            turn_dve(dve, n, 0)
            scale_x(dve, step, k, 1)
            turn_dve(dve, n, 1)

        def norm_6_7_dve(dve, step, last_piece):
            n = TURN_OF_NORM[7]
            add_y(dve, 6, 0, 0.5, last_piece)
            scale_x(dve, step, 6, 0)
            add_y(dve, 6, 1, 0.5, last_piece)
            scale_x(dve, step, 7, 0)
            scale_x(dve, step, 6, 1)
            turn_dve(dve, n, 0)
            scale_x(dve, step, 7, 1)
            turn_dve(dve, n, 1)

        def root(act, k, tt):
            if k == 0:
                act.wait_ge(x_loaded[tt], 16)
            else:
                act.wait_ge(x_ready, x_count(k, tt))
            if norm_no(k, tt):
                act.wait_ge(squares, norm_no(k, tt))
            act.activation(square[:, :], x[:, tt, :], ACT.Square, accum_out=stat[:, tt:tt + 1]).then_inc(squares, 1)
            act.wait_ge(squares, norm_no(k, tt) + 1)
            act.activation(stat[:, 2 + tt:3 + tt], stat[:, tt:tt + 1], ACT.Sqrt, scale=1.0 / D,
                           bias=eps[:, :]).then_inc(roots, 1)

        def load_roots(act):
            act.wait_ge(eps_set, 1)
            act.activation(stat[:, 60:61], eps[:, :], ACT.Sqrt)

        def norm_act(act, k):
            load_roots(act)
            if k == 6:
                root(act, 6, 0)
                root(act, 7, 0)
                root(act, 6, 1)
                turn_act(act, TURN_OF_NORM[7], 0)
                root(act, 7, 1)
                turn_act(act, TURN_OF_NORM[7], 1)
                return
            for tt in range(TT):
                root(act, k, tt)
                turn_act(act, TURN_OF_NORM[k], tt)

        def turn_pe(pe, n, who, tt):
            if n == 0 and tt == 0:
                pe.wait_ge(consts, 1)
            pe.wait_ge(h_ready, 2 * H_ORDER.index(who) + tt + 1)
            for k in range(KD):
                ins = pe.transpose(psum[:, 4 + 2 * tt + k // 4, (k % 4) * P:(k % 4 + 1) * P], h[:, tt, k * P:(k + 1) * P],
                                   ident[:, :])
                if k % 4 == 3:
                    ins.then_inc(turned, 1)

        def turn_bank(buf, tt, j):
            return buf[:, 4 * j:4 * j + 4, tt * P:(tt + 1) * P]

        def bank_of_turn(tt, j):
            return banks(4 + 2 * tt + j).rearrange("p (k n) -> p k n", n=P)

        def turn_act(act, n, tt):
            for j in range(2):
                act.wait_ge(turned, 4 * n + 2 * tt + j + 1)
                act.activation(turn_bank(hT_high, tt, j), bank_of_turn(tt, j), ACT.Copy).then_inc(turn_high, 1)

        def turn_dve(dve, n, tt):
            for j in range(2):
                dve.wait_ge(turn_high, 4 * n + 2 * tt + j + 1)
                dve.tensor_tensor(turn_bank(hT_low, tt, j), bank_of_turn(tt, j), turn_bank(hT_high, tt, j).bitcast(F32),
                                  ALU.subtract).then_inc(turn_low, 1)

        def turned_tile(pe, n, tt):
            pe.wait_ge(turn_low, 4 * n + 2 * tt + 2)

        def clear_Y(pe, of=range(4)):
            for b in of:
                pe.matmul(banks(b), zero_r[:, 0:P], zero_r[:, :], start=True, stop=True, skip_group_check=True)

        def gate_up_pe(pe, q, half, tt):
            for k in range(4):
                kk, tok = 4 * half + k, slice(tt * P, (tt + 1) * P)
                ins = product(pe, GU[tt], hT_high[:, kk, tok], hT_low[:, kk, tok], four_k(high, q)[:, k, :],
                              four_k(low, q)[:, k, :], start=kk == 0, stop=kk == KD - 1)
            if tt == 1:
                ins.then_inc(used, 1)
            elif half == 1:
                ins.then_inc(gu_first, 1)

        def first_gate_up_pe(pe, b, n, who):
            turn_pe(pe, n, who, 0)
            clear_Y(pe, (0, 1))
            turned_tile(pe, n, 0)
            pe.wait_ge(split, b + 1)
            gate_up_pe(pe, b, 0, 0)
            turn_pe(pe, n, who, 1)
            clear_Y(pe, (2, 3))
            pe.wait_ge(split, b + 2)
            gate_up_pe(pe, b + 1, 1, 0)
            turned_tile(pe, n, 1)
            for half in range(2):
                gate_up_pe(pe, b + half, half, 1)

        def act_turn_pe(pe, count):
            for tt in range(TT):
                pe.wait_ge(act_ready, count + tt + 1 - 2)
                for k in range(2):
                    ins = pe.transpose(TURN_A[:, k * TOKENS + tt * P:k * TOKENS + (tt + 1) * P],
                                       act_tok[:, tt, k * P:(k + 1) * P], ident[:, :])
            ins.then_inc(a_turned, 1)

        def down_pe(pe, p, r, count_a, last=False):
            pe.wait_ge(a_low, count_a)
            pe.wait_ge(split, p + 1 + scales_with(r, 3))
            for tt in range(TT):
                for k in range(2):
                    for n in range(2):
                        tok, cols = slice(tt * P, (tt + 1) * P), slice(n * BANK, (n + 1) * BANK)
                        ins = product(pe, Y[tt][:, cols], aT_high[:, k, tok], aT_low[:, k, tok],
                                      two_k(high, p)[:, k, cols], two_k(low, p)[:, k, cols], start=False)
                if last and tt == 0:
                    ins.then_inc(y_first, 1)
            ins.then_inc(used, 1)

        def ffn_pe(pe, i, turn, who):
            b, done = FIRST_PIECE[f"ffn{i}"], N_CHUNKS * i
            first_gate_up_pe(pe, b, turn, who)
            with pe.Fori(0, N_CHUNKS - 1) as c:
                pe.wait_ge(split, b + 3 + scales_with(c, 3))
                for tt in range(TT):
                    pe.wait_ge(act_ready, c * 2 + 2 * done + tt + 1)
                    gate_up_pe(pe, b + 2, 0, tt)
                act_turn_pe(pe, c * 2 + 2 * (done + 1))
                pe.wait_ge(split, b + 4 + scales_with(c, 3))
                for tt in range(TT):
                    gate_up_pe(pe, b + 3, 1, tt)
                down_pe(pe, b + 4, c, c + (done + 1))
            act_turn_pe(pe, 2 * (done + N_CHUNKS))
            down_pe(pe, b + FFN_PIECES - 1, 0, done + N_CHUNKS, last=True)

        def gate_act(act, first, second):
            for tt, (counter, value) in enumerate(((gu_first, first), (used, second))):
                act.wait_ge(counter, value)
                act.activation(gate[:, tt, :], GU[tt][:, 0:CHUNK], ACT.Silu).then_inc(gate_ready, 1)

        def gate_dve(dve, count):
            for tt in range(TT):
                dve.wait_ge(gate_ready, count + tt + 1 - 2)
                dve.tensor_tensor(act_tok[:, tt, :], gate[:, tt, :], GU[tt][:, CHUNK:2 * CHUNK],
                                  ALU.mult).then_inc(act_ready, 1)

        def flat(buf):
            return buf[:, :, :].rearrange("p k n -> p (k n)")

        def ffn_act(act, i):
            b, done = FIRST_PIECE[f"ffn{i}"], N_CHUNKS * i

            def chunk(p, r, number, gu_used):
                round_piece(act, p, r)
                gate_act(act, number, gu_used)
                round_piece(act, p + 1, r)
                act.wait_ge(a_turned, number)
                act.activation(flat(aT_high), TURN_A, ACT.Copy).then_inc(a_high, 1)
                round_piece(act, p + 2, r)

            chunk(b + 2, 0, done + 1, b + 2)
            with act.Fori(0, N_CHUNKS - 1) as c:
                chunk(b + 5, c, c + (done + 2), c * 3 + (b + 4))

        def ffn_dve(dve, i):
            b, done = FIRST_PIECE[f"ffn{i}"], N_CHUNKS * i

            def chunk(p, r, number):
                split_piece(dve, p, r)
                gate_dve(dve, number * 2)
                split_piece(dve, p + 1, r)
                dve.wait_ge(a_high, number)
                dve.tensor_tensor(flat(aT_low), TURN_A, flat(aT_high).bitcast(F32), ALU.subtract).then_inc(a_low, 1)
                split_piece(dve, p + 2, r)

            chunk(b + 2, 0, done + 1)
            with dve.Fori(0, N_CHUNKS - 1) as c:
                chunk(b + 5, c, c + (done + 2))

        IN_ORDER = ["gla_in", "sb_in", "mix_in"]

        def columns(name, n):
            c = (3, 4, 0, 2, 1, 5)[n] if name == "mix_in" else n
            return slice(c * BANK, (c + 1) * BANK)

        def in_pe(pe, name, turn, who, between=lambda n: None):
            b, done = FIRST_PIECE[name], IN_CHUNKS * IN_ORDER.index(name)

            def products(n, half, tt):
                q = b + 2 * n + half
                pe.wait_ge(split, q + 1)
                for k in range(4):
                    kk, tok = 4 * half + k, slice(tt * P, (tt + 1) * P)
                    ins = product(pe, banks(2 * (n % 3) + tt), hT_high[:, kk, tok], hT_low[:, kk, tok],
                                  four_k(high, q)[:, k, :], four_k(low, q)[:, k, :], start=kk == 0, stop=kk == KD - 1)
                if tt == 1:
                    ins.then_inc(used, 1)
                elif half == 1:
                    ins.then_inc(in_first, 1)

            turn_pe(pe, turn, who, 0)
            turned_tile(pe, turn, 0)
            products(0, 0, 0)
            turn_pe(pe, turn, who, 1)
            products(0, 1, 0)
            turned_tile(pe, turn, 1)
            for half in range(2):
                products(0, half, 1)
            for n in range(1, IN_CHUNKS):
                between(n)
                if n >= 3:
                    for c in in_copied:
                        pe.wait_ge(c, done + n - 2)
                for half in range(2):
                    for tt in range(TT):
                        products(n, half, tt)

        def in_act(act, name, between=lambda n: None):
            b, done = FIRST_PIECE[name], IN_CHUNKS * IN_ORDER.index(name)
            for n in range(IN_CHUNKS):
                round_piece(act, b + 2 * n + 2)
                round_piece(act, b + 2 * n + 3)
                act.wait_ge(in_first, done + n + 1)
                act.activation(proj[:, 0, columns(name, n)], banks(2 * (n % 3)),
                               ACT.Copy).then_inc(in_copied[0], 1)
                between(n)

        def in_dve(dve, name, between=lambda n: None):
            b = FIRST_PIECE[name]
            for n in range(IN_CHUNKS):
                split_piece(dve, b + 2 * n + 2)
                split_piece(dve, b + 2 * n + 3)
                dve.wait_ge(used, b + 2 * n + 2)
                dve.tensor_copy(proj[:, 1, columns(name, n)], banks(2 * (n % 3) + 1)).then_inc(in_copied[1], 1)
                between(n)

        def wait_proj(eng, name):
            for c in in_copied:
                eng.wait_ge(c, IN_CHUNKS * (IN_ORDER.index(name) + 1))

        def out_pe(pe, name, turn, who):
            b = FIRST_PIECE[name]

            def products(j, tt):
                p = b + j
                pe.wait_ge(split, p + 1)
                for k in range(2):
                    for n in range(2):
                        tok, cols = slice(tt * P, (tt + 1) * P), slice(n * BANK, (n + 1) * BANK)
                        ins = product(pe, Y[tt][:, cols], hT_high[:, 2 * j + k, tok], hT_low[:, 2 * j + k, tok],
                                      two_k(high, p)[:, k, cols], two_k(low, p)[:, k, cols],
                                      start=j == 0 and k == 0, stop=j == OUT_PIECES - 1 and k == 1)
                if tt == 1:
                    ins.then_inc(used, 1)
                elif j == OUT_PIECES - 1:
                    ins.then_inc(y_first, 1)

            turn_pe(pe, turn, who, 0)
            turned_tile(pe, turn, 0)
            products(0, 0)
            turn_pe(pe, turn, who, 1)
            products(1, 0)
            turned_tile(pe, turn, 1)
            for j in range(2):
                products(j, 1)
            for j in range(2, OUT_PIECES):
                for tt in range(TT):
                    products(j, tt)

        def out_act(act, name):
            for j in range(3, 6):
                round_piece(act, FIRST_PIECE[name] + j)

        def out_dve(dve, name):
            for j in range(3, 6):
                split_piece(dve, FIRST_PIECE[name] + j)

        area = Area()
        gq = area.take(1024)
        gk = area.take(1024)
        gb = area.take(1024)
        gdiff = area.take(1024)
        geq, gek = square[:, 0:512], square[:, 512:1024]
        gqs = [area.take(1024) for _ in range(2)]
        gks = [area.take(1024) for _ in range(2)]
        gscore = area.take(1024)
        gcross = area.take(512)
        grank = area.take(TT * GLA_RANK)
        grankT = area.take(TOKENS)
        glogsig = gqs[0]
        gabs, glog = gks[0], gks[1]
        STEPS = [0, P] + LEVELS
        GATE_Z = banks(6, 2)
        gdiff_q = [gdiff[:, 0:512], gate[:, :, :].rearrange("p a n -> p (a n)")]
        gdiff_k = [gdiff[:, 512:1024], act_tok[:, :, :].rearrange("p a n -> p (a n)")]

        def pairs(v, B):
            return v.rearrange("p (m n) -> p m n", n=2 * B)

        def gla_pe(pe):
            def between(n):
                if n == 1:
                    pe.wait_ge(small_low, 1)
                    for tt in range(TT):
                        for k in range(KD):
                            tok = slice(tt * P, (tt + 1) * P)
                            ins = product(pe, TURN_A[:, tt * GLA_RANK:(tt + 1) * GLA_RANK], hT_high[:, k, tok],
                                          hT_low[:, k, tok], gkw_high[:, k, :], gkw_low[:, k, :], start=tt == 0 and k == 0)
                    ins.then_inc(g["rank"], 1)
                elif n == 2:
                    pe.wait_ge(g["rank_sb"], 1)
                    for tt in range(TT):
                        ins = pe.transpose(TURN_X[0:GLA_RANK, tt * P:(tt + 1) * P],
                                           grank[:, tt * GLA_RANK:(tt + 1) * GLA_RANK], ident[:, :])
                    ins.then_inc(g["rankT"], 1)
                elif n == 3:
                    pe.wait_ge(g["rankT_sb"], 1)
                    for hd in range(GLA_HEADS):
                        ins = pe.matmul(GATE_Z[:, hd * TOKENS:(hd + 1) * TOKENS], wgk2[:, hd * P:(hd + 1) * P],
                                        grankT[0:GLA_RANK, :], start=hd % 2 == 0, stop=True, skip_group_check=True)
                    ins.then_inc(g["z"], 1)
                elif n in (4, 5):
                    if n == 4:
                        pe.wait_ge(g["z_read"], 2)
                    else:
                        pe.wait_ge(g["q_sb"], 1)
                    for c in in_copied:
                        pe.wait_ge(c, n - 3)
                    for hd in range(GLA_HEADS):
                        for tt in range(TT):
                            off = (n - 4) * BANK + hd * P
                            ins = pe.transpose(GATE_Z[:, hd * TOKENS + tt * P:hd * TOKENS + (tt + 1) * P],
                                               proj[:, tt, off:off + P], ident[:, :])
                    ins.then_inc(g["qkT"], 1)

            pe.wait_ge(consts, 2)
            in_pe(pe, "gla_in", 1, "n1", between)
            wait_proj(pe, "gla_in")
            for n, B in enumerate(STEPS):
                if B:
                    pe.wait_ge(g["scaled"], n)
                    q, k = gqs[n % 2], gks[n % 2]
                else:
                    q, k = gq, gk
                    pe.wait_ge(g["q_sb"], 1)
                    pe.wait_ge(g["k_sb"], 1)
                if n >= 2:
                    pe.wait_ge(g["kept"], n - 1)
                dst = banks(2 + 2 * (n % 2), 2)
                for hd in range(GLA_HEADS):
                    if B == P:
                        at = hd * TOKENS
                        ins = pe.matmul(dst[:, hd * P:(hd + 1) * P], k[:, at:at + P], q[:, at + P:at + 2 * P],
                                        start=hd == 0, stop=True, skip_group_check=True)
                        continue
                    for tt in range(TT):
                        at = hd * TOKENS + tt * P
                        ins = pe.matmul(dst[:, at:at + P], k[:, at:at + P], q[:, at:at + P],
                                        start=at % BANK == 0, stop=True, skip_group_check=True)
                ins.then_inc(g["scores"], 1)
            pe.wait_ge(g["kept"], len(STEPS))
            for tt in range(TT):
                for hd in range(GLA_HEADS):
                    cols = slice(hd * GLA_V, (hd + 1) * GLA_V)
                    diag = gscore[:, hd * TOKENS + tt * P:hd * TOKENS + (tt + 1) * P]
                    ins = pe.matmul(Y[tt][:, cols], diag, proj[:, tt, 1024 + hd * GLA_V:1024 + (hd + 1) * GLA_V],
                                    start=hd % 2 == 0, stop=tt == 0, skip_group_check=True)
                    if tt:
                        ins = pe.matmul(Y[1][:, cols], gcross[:, hd * P:(hd + 1) * P],
                                        proj[:, 0, 1024 + hd * GLA_V:1024 + (hd + 1) * GLA_V], start=False, stop=True,
                                        skip_group_check=True)
                ins.then_inc(g["out"], 1)
            out_pe(pe, "gla_out", GLA_TURN, "gla")

        def gla_act(act, step):
            def between(n):
                if n == 0:
                    act.wait_ge(g["rank"], 1)
                    act.activation(grank, TURN_A[:, 0:TT * GLA_RANK], ACT.Copy).then_inc(g["rank_sb"], 1)
                elif n == 2:
                    act.wait_ge(g["z"], 1)
                    for hd in range(GLA_HEADS):
                        c = slice(hd * TOKENS, (hd + 1) * TOKENS)
                        ins = act.activation(gabs[:, c], GATE_Z[:, c], ACT.Abs, bias=bgk[:, hd:hd + 1])
                    ins.then_inc(g["z_read"], 1)
                    act.wait_ge(g["z_read"], 2)
                    step(act.activation(gabs, gabs, ACT.Exp, scale=-1.0))
                    act.activation(glog, gabs, ACT.Ln, bias=ones[:, 0:1]).then_inc(g["ln"], 1)
                elif n == 3:
                    act.wait_ge(g["qkT"], 1)
                    act.activation(gq, GATE_Z, ACT.Copy, scale=float(GLA_K) ** -0.5).then_inc(g["q_sb"], 1)

            in_act(act, "gla_in", between)
            round_piece(act, FIRST_PIECE["gla_out"] + 2)
            for n, B in enumerate(STEPS[1:]):
                act.wait_ge(g["diff"], n + 1)
                if n:
                    act.wait_ge(g["scaled"], n)
                act.activation(geq, gdiff_q[n % 2], ACT.Exp, scale=1.0 / GLA_TAU)
                act.activation(gek, gdiff_k[n % 2], ACT.Exp, scale=-1.0 / GLA_TAU).then_inc(g["decay"], 1)
            for tt in range(TT):
                act.activation(proj[:, tt, 2048:3072], proj[:, tt, 2048:3072], ACT.Silu).then_inc(g["silu"], 1)
            act.activation(stat[:, 60:61], eps[:, :], ACT.Sqrt)
            for tt in range(TT):
                act.wait_ge(g["out"], tt + 1)
                if tt:
                    act.wait_ge(g["summed"], tt)
                act.activation(square[:, :], Y[tt], ACT.Square).then_inc(g["sq"], 1)
                act.wait_ge(g["summed"], tt + 1)
                act.activation(stat[:, 16 + 4 * tt:20 + 4 * tt], stat[:, 8 + 4 * tt:12 + 4 * tt], ACT.Sqrt, scale=1.0 / GLA_V,
                               bias=eps[:, :]).then_inc(g["roots"], 1)
            for tt in range(TT):
                turn_act(act, GLA_TURN, tt)
            out_act(act, "gla_out")

        def gla_dve(dve, step):
            def diff(n):
                B = STEPS[n + 1]
                if n >= 2:
                    dve.wait_ge(g["decay"], n - 1)
                v = pairs(gb, B)
                boundary = v[:, :, B - 1:B].to_broadcast([P, TT * GLA_HEADS * P // (2 * B), B])
                w = {"n": B}
                dve.tensor_tensor(gdiff_q[n % 2].rearrange("p (m n) -> p m n", **w), v[:, :, B:2 * B], boundary, ALU.subtract)
                dve.tensor_tensor(gdiff_k[n % 2].rearrange("p (m n) -> p m n", **w), v[:, :, 0:B], boundary,
                                  ALU.subtract).then_inc(g["diff"], 1)

            def between(n):
                if n == 1:
                    dve.wait_ge(g["rankT"], 1)
                    dve.tensor_copy(grankT[0:GLA_RANK, :], TURN_X[0:GLA_RANK, 0:TOKENS]).then_inc(g["rankT_sb"], 1)
                elif n == 2:
                    dve.wait_ge(g["z_read"], 1)
                    for hd in range(GLA_HEADS):
                        c = slice(hd * TOKENS, (hd + 1) * TOKENS)
                        ins = dve.tensor_scalar(glogsig[:, c], GATE_Z[:, c], bgk[:, hd:hd + 1], 0.0, ALU.add, ALU.min)
                    ins.then_inc(g["z_read"], 1)
                elif n == 3:
                    dve.wait_ge(g["z_read"], 2)
                    dve.wait_ge(g["ln"], 1)
                    step(dve.tensor_tensor(glogsig, glogsig, glog, ALU.subtract))
                    for hd in range(GLA_HEADS):
                        c = slice(hd * TOKENS, (hd + 1) * TOKENS)
                        ins = dve.tensor_tensor_scan(gb[:, c], ones[:, :], glogsig[:, c], 0.0, ALU.mult, ALU.add)
                    step(ins)
                elif n == 4:
                    for i in range(2):
                        dve.memset(gqs[i], 0.0)
                        ins = dve.memset(gks[i], 0.0)
                    step(ins)
                    diff(0)
                    diff(1)
                    dve.wait_ge(g["qkT"], 2)
                    dve.tensor_copy(gk, GATE_Z).then_inc(g["k_sb"], 1)

            in_dve(dve, "gla_in", between)
            split_piece(dve, FIRST_PIECE["gla_out"] + 2)
            dve.wait_ge(g["q_sb"], 1)
            dve.wait_ge(g["k_sb"], 1)
            for n, B in enumerate(STEPS[1:]):
                dve.wait_ge(g["decay"], n + 1)
                if n >= 2:
                    dve.wait_ge(g["scores"], n)
                w = {"n": B}
                to = (n + 1) % 2
                dve.tensor_tensor(pairs(gqs[to], B)[:, :, B:2 * B], pairs(gq, B)[:, :, B:2 * B],
                                  geq.rearrange("p (m n) -> p m n", **w), ALU.mult)
                dve.tensor_tensor(pairs(gks[to], B)[:, :, 0:B], pairs(gk, B)[:, :, 0:B],
                                  gek.rearrange("p (m n) -> p m n", **w), ALU.mult).then_inc(g["scaled"], 1)
                if n + 2 < len(STEPS) - 1:
                    diff(n + 2)
                keep(dve, n)
            keep(dve, len(STEPS) - 1)
            for tt in range(TT):
                sums, root, inverse = (stat[:, a + 4 * tt:a + 4 * tt + 4] for a in (8, 16, 24))
                dve.wait_ge(g["sq"], tt + 1)
                dve.tensor_reduce(sums, square[:, :].rearrange("p (a b) -> p a b", b=GLA_V), AX, ALU.add).then_inc(g["summed"], 1)
                dve.wait_ge(g["roots"], tt + 1)
                step(dve.reciprocal(inverse, root))
                for hd in range(GLA_HEADS):
                    c = slice(hd * GLA_V, (hd + 1) * GLA_V)
                    ins = dve.scalar_tensor_tensor(h[:, tt, c], Y[tt][:, c], inverse[:, hd:hd + 1], gla_gain[:, :],
                                                   ALU.mult, ALU.mult)
                step(ins)
                dve.wait_ge(g["silu"], tt + 1)
                dve.tensor_tensor(h[:, tt, :], h[:, tt, :], proj[:, tt, 2048:3072], ALU.mult).then_inc(h_ready, 1)
            for tt in range(TT):
                turn_dve(dve, GLA_TURN, tt)
            out_dve(dve, "gla_out")

        def keep(dve, n):
            dve.wait_ge(g["scores"], n + 1)
            src = banks(2 + 2 * (n % 2), 2)
            if n:
                dve.wait_ge(g["kept"], n)
            B = STEPS[n]
            if B == P:
                dve.tensor_copy(gcross, src[:, 0:GLA_HEADS * P]).then_inc(g["kept"], 1)
                return
            mask = levels[:, LEVELS.index(B), :] if B else ident[:, :]
            mask = mask.bitcast(I32).rearrange("p (o n) -> p o n", o=1).to_broadcast([P, 2 * GLA_HEADS, P])
            dve.copy_predicated(gscore.rearrange("p (b n) -> p b n", n=P), mask,
                                src.rearrange("p (b n) -> p b n", n=P)).then_inc(g["kept"], 1)

        area = Area()
        sq_T, sk_T = area.take(2048), area.take(2048)
        GROUP_COLS = GROUP * (TOKENS + P)
        sz = [area.take(GROUP_COLS) for _ in range(2)] + [proj[:, tt, 0:GROUP_COLS] for tt in range(TT)]
        ssp = [area.take(GROUP_COLS) for _ in range(2)]

        def place(i):
            return (i % 2) * 2 + i // 2

        def early(v):
            return v[:, 0:GROUP * TOKENS].rearrange("p (a n) -> p a n", n=TOKENS)[:, :, 0:P]

        def late_part(v):
            return v[:, GROUP * TOKENS:].rearrange("p (a n) -> p a n", n=P)

        def turn_columns(pe, dst, off, tiles, signal):
            for k in range(tiles):
                for tt in range(TT):
                    ins = pe.transpose(dst[:, k * TOKENS + tt * P:k * TOKENS + (tt + 1) * P],
                                       proj[:, tt, off + k * P:off + (k + 1) * P], ident[:, :])
            ins.then_inc(signal, 1)

        def sb_pe(pe):
            def between(n):
                if n < 2:
                    return
                for c in in_copied:
                    pe.wait_ge(c, IN_CHUNKS + n - 1)
                if n > 2:
                    pe.wait_ge(s["qk_sb"], n - 2)
                turn_columns(pe, banks(6, 2), (n - 2) * BANK, KD // 2, s["qkT"])

            in_pe(pe, "sb_in", 5, "n4", between)
            wait_proj(pe, "sb_in")
            pe.wait_ge(s["qk_sb"], 4)

            def dots(gr):
                if gr:
                    pe.wait_ge(s["z_sb"], gr)
                z = banks(0, 3)
                for i in (0, 2, 1, 3):
                    rows, at = slice(SB_HD * (i % 2), SB_HD * (i % 2 + 1)), (2 * gr + i // 2) * TOKENS
                    c = place(i)
                    pe.matmul(z[:, c * TOKENS:(c + 1) * TOKENS], sk_T[rows, at:at + P], sq_T[rows, at:at + TOKENS],
                              start=True, stop=True, skip_group_check=True)
                    if i >= 2:
                        if i == 3:
                            pe.wait_ge(s["even"], gr + 1)
                        for ii in (i - 2, i):
                            c, at = place(ii), (2 * gr + ii // 2) * TOKENS
                            ins = pe.matmul(z[:, GROUP * TOKENS + c * P:GROUP * TOKENS + (c + 1) * P],
                                            sk_T[rows, at + P:at + TOKENS], sq_T[rows, at + P:at + TOKENS],
                                            start=True, stop=True, skip_group_check=True)
                        if i == 2:
                            ins.then_inc(s["even"], 1)
                ins.then_inc(s["z"], 1)

            dots(0)
            dots(1)
            for gr in range(SB_GROUPS):
                pe.wait_ge(s["sp"], gr + 1)
                if gr:
                    pe.wait_ge(s["arg"], gr)
                v = ssp[gr % 2]
                for b in range(3):
                    ins = pe.matmul(banks(3 + b), suffix[:, :], v[:, b * BANK:(b + 1) * BANK], start=True, stop=b == 2,
                                    skip_group_check=True)
                    if b < 2:
                        dst = banks(3 + b).rearrange("p (a n) -> p a n", n=TOKENS)[:, :, P:TOKENS]
                        pe.matmul(dst, ones[:, 0:P], late_part(v)[:, 2 * b:2 * b + 2, :], start=False, stop=True,
                                  skip_group_check=True)
                ins.then_inc(s["sums"], 1)
                if gr + 2 < SB_GROUPS:
                    dots(gr + 2)
                pe.wait_ge(s["w"], gr + 1)
                if gr >= 2:
                    pe.wait_ge(s["out_sb"], gr - 1)
                w, dst = sz[gr], banks(6 + gr % 2)
                for i in range(GROUP):
                    c, col = place(i), 2 * D + (GROUP * gr + i) * SB_HD
                    v0, v1 = proj[:, 0, col:col + SB_HD], proj[:, 1, col:col + SB_HD]
                    pe.matmul(dst[:, i * SB_HD:(i + 1) * SB_HD], w[:, c * TOKENS:c * TOKENS + P], v0, start=i == 0,
                              stop=True, skip_group_check=True)
                    to = dst[:, TOKENS + i * SB_HD:TOKENS + (i + 1) * SB_HD]
                    pe.matmul(to, w[:, c * TOKENS + P:(c + 1) * TOKENS], v0, start=False, stop=False,
                              skip_group_check=True)
                    at = GROUP * TOKENS + c * P
                    ins = pe.matmul(to, w[:, at:at + P], v1, start=False, stop=True, skip_group_check=True)
                ins.then_inc(s["out"], 1)
            out_pe(pe, "sb_out", SB_TURN, "sb")

        def sb_act(act, step):
            def between(n):
                if n in (1, 2):
                    act.wait_ge(s["qkT"], n)
                    act.activation(sq_T[:, (n - 1) * D:n * D], banks(6, 2), ACT.Copy,
                                   scale=float(SB_HD) ** -0.5).then_inc(s["qk_sb"], 1)

            in_act(act, "sb_in", between)
            round_piece(act, FIRST_PIECE["sb_out"] + 2)

            def softplus_tail(gr):
                act.wait_ge(s["z_sb"], gr + 1)
                if gr >= 2:
                    act.wait_ge(s["sums"], gr - 1)
                v = ssp[gr % 2]
                step(act.activation(v, sz[gr], ACT.Abs))
                step(act.activation(v, v, ACT.Exp, scale=-1.0))
                act.activation(v, v, ACT.Ln, bias=ones[:, 0:1]).then_inc(s["ln"], 1)

            softplus_tail(0)
            softplus_tail(1)
            for gr in range(SB_GROUPS):
                act.wait_ge(s["arg"], gr + 1)
                act.activation(sz[gr], sz[gr], ACT.Exp).then_inc(s["exp"], 1)
                if gr + 2 < SB_GROUPS:
                    softplus_tail(gr + 2)
            for tt in range(TT):
                turn_act(act, SB_TURN, tt)
            out_act(act, "sb_out")

        def sb_dve(dve, step):
            def between(n):
                if n in (3, 4):
                    dve.wait_ge(s["qkT"], n)
                    dve.tensor_copy(sk_T[:, (n - 3) * D:(n - 2) * D], banks(6, 2)).then_inc(s["qk_sb"], 1)

            in_dve(dve, "sb_in", between)
            split_piece(dve, FIRST_PIECE["sb_out"] + 2)
            mask = strict[:, :].rearrange("p (o n) -> p o n", o=1).to_broadcast([P, GROUP, P])

            def copy_z(gr):
                dve.wait_ge(s["z"], gr + 1)
                dve.tensor_copy(sz[gr], banks(0, 3)).then_inc(s["z_sb"], 1)

            def softplus(gr):
                v = ssp[gr % 2]
                dve.wait_ge(s["ln"], gr + 1)
                dve.wait_ge(s["z_sb"], gr + 1)
                step(dve.scalar_tensor_tensor(v, sz[gr], 0.0, v, ALU.max, ALU.add))
                dve.tensor_tensor(early(v), early(v), mask, ALU.mult)
                dve.tensor_tensor(late_part(v), late_part(v), mask, ALU.mult).then_inc(s["sp"], 1)

            def copy_out(gr):
                dve.wait_ge(s["out"], gr + 1)
                src = banks(6 + gr % 2)
                for tt in range(TT):
                    ins = dve.tensor_copy(h[:, tt, gr * TOKENS:(gr + 1) * TOKENS], src[:, tt * TOKENS:(tt + 1) * TOKENS])
                    if gr == SB_GROUPS - 1:
                        ins.then_inc(h_ready, 1)
                if gr < SB_GROUPS - 1:
                    ins.then_inc(s["out_sb"], 1)

            copy_z(0)
            copy_z(1)
            softplus(0)
            softplus(1)
            for gr in range(SB_GROUPS):
                w = sz[gr]
                dve.wait_ge(s["sums"], gr + 1)
                dve.tensor_tensor(w, w, banks(3, 3), ALU.subtract).then_inc(s["arg"], 1)
                dve.wait_ge(s["exp"], gr + 1)
                for part in (early, late_part):
                    ins = dve.scalar_tensor_tensor(part(w), part(w), 1.0, mask, ALU.min, ALU.mult)
                ins.then_inc(s["w"], 1)
                if gr + 2 < SB_GROUPS:
                    copy_z(gr + 2)
                copy_out(gr)
                if gr + 2 < SB_GROUPS:
                    softplus(gr + 2)
            for tt in range(TT):
                turn_dve(dve, SB_TURN, tt)
            out_dve(dve, "sb_out")

        area = Area()
        mqT, mkT = area.take(1024), area.take(1024)
        mdot = [area.take(2 * 3 * P) for _ in range(2)]
        mexp = [area.take(2 * 3 * P) for _ in range(2)]
        ma = [area.take(3 * P) for _ in range(2)]
        maT = [area.take(3 * P) for _ in range(2)]
        shifted = [area.take(TT * D_CONV) for _ in range(2)]
        conv_w = area.take(CONV_W * D_CONV)
        conv_gain = area.take(D_CONV)
        msquare = scratch[:, 2048:4096]
        params = levels[:, :, :].rearrange("p a n -> p (a n)")
        qk_gain, sub_gain, lam_in = params[:, 0:128], params[:, 128:256], params[:, 256:512]
        XC, BG, CG, QK, VV = 0, D_CONV, 2 * D_CONV, 3 * D_CONV, 5 * D_CONV
        QK_GROUPS = 2 * 2 * DA_HEADS

        conv_sum, conv_root = params[:, 520:536], params[:, 536:552]

        def both(off, n):
            return proj[:, :, off:off + n]

        def by_tile(v):
            return v.rearrange("p (a n) -> p a n", a=TT)

        def mix_pe(pe):
            def between(n):
                if n == 5:
                    pe.wait_ge(m["qk"], 1)
                    turn_columns(pe, banks(6, 2), QK, DA_HEADS, m["qkT"])

            in_pe(pe, "mix_in", 8, "n7", between)
            wait_proj(pe, "mix_in")
            turn_columns(pe, banks(0, 2), QK + D_CONV, DA_HEADS, m["qkT"])
            pe.wait_ge(m["q_sb"], 1)
            pe.wait_ge(m["k_sb"], 1)

            def dots(hd):
                if hd >= 2:
                    pe.wait_ge(m["dots_sb"], hd - 1)
                for c in range(2):
                    rows, at, dst = slice(DA_HD * c, DA_HD * (c + 1)), hd * TOKENS, banks(2 * (hd % 2) + c)
                    pe.matmul(dst[:, 0:P], mqT[rows, at:at + P], mkT[rows, at:at + P], start=True, stop=True,
                              skip_group_check=True)
                    ins = pe.matmul(dst[:, P:3 * P], mqT[rows, at + P:at + TOKENS], mkT[rows, at:at + TOKENS],
                                    start=True, stop=True, skip_group_check=True)
                ins.then_inc(m["dots"], 1)

            dots(0)
            dots(1)
            for hd in range(DA_HEADS):
                pe.wait_ge(m["a"], hd + 1)
                if hd >= 2:
                    pe.wait_ge(m["aT_sb"], hd - 1)
                for j in range(3):
                    ins = pe.transpose(banks(4 + hd % 2)[:, j * P:(j + 1) * P], ma[hd % 2][:, j * P:(j + 1) * P], ident[:, :])
                ins.then_inc(m["aT"], 1)
                if hd + 2 < DA_HEADS:
                    dots(hd + 2)
                pe.wait_ge(m["aT_sb"], hd + 1)
                a, col = maT[hd % 2], slice(hd * DA_V, (hd + 1) * DA_V)
                v0, v1 = (proj[:, tt, VV + hd * DA_V:VV + (hd + 1) * DA_V] for tt in range(TT))
                pe.matmul(banks(6)[:, col], a[:, 0:P], v0, start=hd == 0, stop=True, skip_group_check=True)
                pe.matmul(banks(7)[:, col], a[:, P:2 * P], v0, start=hd == 0, stop=False, skip_group_check=True)
                ins = pe.matmul(banks(7)[:, col], a[:, 2 * P:], v1, start=False, stop=True, skip_group_check=True)
            ins.then_inc(m["out"], 1)
            out_pe(pe, "mix_out", MIX_TURN, "mix")

        def mix_act(act, step):
            def between(n):
                if n == 1:
                    for c in in_copied:
                        act.wait_ge(c, 2 * IN_CHUNKS + 2)
                    act.activation(by_tile(msquare), both(QK, 2 * D_CONV), ACT.Square).then_inc(m["qk_sq"], 1)
                elif n == 3:
                    act.wait_ge(m["qk_sum"], 1)
                    act.activation(stat[:, 0:32], stat[:, 32:64], ACT.Sqrt, scale=1.0 / DA_HD,
                                   bias=eps[:, :]).then_inc(m["qk_root"], 1)
                elif n == 4:
                    act.wait_ge(m["qkT"], 1)
                    act.activation(mqT, banks(6, 2), ACT.Copy, scale=float(DA_HD) ** -0.5).then_inc(m["q_sb"], 1)

            in_act(act, "mix_in", between)
            round_piece(act, FIRST_PIECE["mix_out"] + 2)
            act.wait_ge(m["lam"], 1)
            act.activation(params[:, 514:516], params[:, 512:514], ACT.Exp).then_inc(m["lam_exp"], 1)

            def softmax(hd):
                act.wait_ge(m["bias"], hd + 1)
                for tt, lo, hi in ((0, 0, P), (1, P, 3 * P)):
                    for c in range(2):
                        at, col = c * 3 * P, 8 * (hd % 2) + 2 * tt + c
                        ins = act.activation(mexp[hd % 2][:, at + lo:at + hi], mdot[hd % 2][:, at + lo:at + hi], ACT.Exp,
                                             bias=stat[:, 4 + col:5 + col], accum_out=stat[:, 16 + col:17 + col])
                ins.then_inc(m["exp"], 1)

            softmax(0)
            softmax(1)
            for hd in range(DA_HEADS):
                act.wait_ge(m["aT"], hd + 1)
                act.activation(maT[hd % 2], banks(4 + hd % 2)[:, 0:3 * P], ACT.Copy).then_inc(m["aT_sb"], 1)
                if hd + 2 < DA_HEADS:
                    softmax(hd + 2)
                if hd == 1:
                    act.wait_ge(m["conv"], 1)
                    act.activation(both(CG, D_CONV), both(XC, D_CONV), ACT.Square).then_inc(m["sq"], 1)
                if hd == 2:
                    act.wait_ge(m["sum"], 1)
                    act.activation(conv_root, conv_sum, ACT.Sqrt, scale=8.0 / D_CONV, bias=eps[:, :]).then_inc(m["root"], 1)
            act.wait_ge(m["out"], 1)
            for tt in range(TT):
                act.activation(square[:, tt * D_CONV:(tt + 1) * D_CONV], banks(6 + tt), ACT.Square).then_inc(m["sq"], 1)
                act.wait_ge(m["sum"], tt + 2)
                act.activation(stat[:, 48 + 4 * tt:52 + 4 * tt], stat[:, 16 + 4 * tt:20 + 4 * tt], ACT.Sqrt,
                               scale=1.0 / DA_V, bias=eps[:, :]).then_inc(m["root"], 1)
            for tt in range(TT):
                turn_act(act, MIX_TURN, tt)
            out_act(act, "mix_out")

        def mix_dve(dve, step):
            def between(n):
                if n == 2:
                    dve.wait_ge(m["qk_sq"], 1)
                    dve.tensor_reduce(stat[:, 32:64], msquare.rearrange("p (a n) -> p a n", n=DA_HD), AX,
                                      ALU.add).then_inc(m["qk_sum"], 1)
                elif n == 3:
                    dve.wait_ge(mix_loaded, 9 * 16)
                    dve.wait_ge(m["qk_root"], 1)
                    step(dve.reciprocal(stat[:, 32:64], stat[:, 0:32]))
                    gains_qk = qk_gain.rearrange("p (a o n) -> p a o n", a=2, o=1).to_broadcast([P, 2, QK_GROUPS // 2, DA_HD])
                    for tt in range(TT):
                        v = proj[:, tt, QK:QK + 2 * D_CONV]
                        v3, v4 = v.rearrange("p (a n) -> p a n", n=DA_HD), v.rearrange("p (a b n) -> p a b n", a=2, n=DA_HD)
                        r = stat[:, 32 + 16 * tt:48 + 16 * tt].rearrange("p (a o) -> p a o", o=1).to_broadcast(
                            [P, QK_GROUPS, DA_HD])
                        step(dve.tensor_tensor(v3, v3, r, ALU.mult))
                        ins = dve.tensor_tensor(v4, v4, gains_qk, ALU.mult)
                    ins.then_inc(m["qk"], 1)
                elif n == 4:
                    for c in in_copied:
                        dve.wait_ge(c, 2 * IN_CHUNKS + 4)
                    dve.tensor_tensor(both(XC, D_CONV), both(XC, D_CONV), both(CG, D_CONV), ALU.mult).then_inc(m["u"], 1)
                    step(dve.tensor_tensor(lam_in[:, 0:128], lam_in[:, 0:128], lam_in[:, 128:256], ALU.mult))
                    dve.tensor_reduce(params[:, 512:514], lam_in[:, 0:128].rearrange("p (a n) -> p a n", n=DA_HD), AX,
                                      ALU.add).then_inc(m["lam"], 1)
                    dve.tensor_scalar(sub_gain, sub_gain, 1.0 - LAMBDA_INIT, None, ALU.mult)

            in_dve(dve, "mix_in", between)
            split_piece(dve, FIRST_PIECE["mix_out"] + 2)
            dve.wait_ge(m["lam_exp"], 1)
            step(dve.tensor_scalar(params[:, 516:517], params[:, 515:516], params[:, 514:515], LAMBDA_INIT, ALU.subtract,
                                   ALU.subtract))
            dve.wait_ge(m["qkT"], 2)
            dve.tensor_copy(mkT, banks(0, 2)).then_inc(m["k_sb"], 1)
            mask = causal[:, :].rearrange("p (o n) -> p o n", o=1).to_broadcast([P, 2, 3 * P])

            def scores(hd):
                v = mdot[hd % 2].rearrange("p (c n) -> p c n", c=2)
                src = psum[:, 2 * (hd % 2):2 * (hd % 2) + 2, 0:3 * P]
                dve.wait_ge(m["dots"], hd + 1)
                at = 8 * (hd % 2)
                ins = dve.tensor_tensor(v, src, mask, ALU.add)
                ins.then_inc(m["dots_sb"], 1)
                dve.wait_ge(m["dots_sb"], hd + 1)
                dve.tensor_reduce(stat[:, 32 + at:34 + at], v[:, :, 0:P], AX, ALU.max)
                step(dve.tensor_reduce(stat[:, 34 + at:36 + at], v[:, :, P:], AX, ALU.max))
                dve.tensor_scalar(stat[:, 4 + at:8 + at], stat[:, 32 + at:36 + at], -1.0, None, ALU.mult).then_inc(m["bias"], 1)

            scores(0)
            scores(1)
            for hd in range(DA_HEADS):
                at = 8 * (hd % 2)
                dve.wait_ge(m["exp"], hd + 1)
                step(dve.reciprocal(stat[:, 48 + at:52 + at], stat[:, 16 + at:20 + at]))
                v = stat[:, 48 + at:52 + at].rearrange("p (a c) -> p a c", c=2)[:, :, 1]
                step(dve.tensor_scalar(v, v, params[:, 516:517], None, ALU.mult))
                if hd >= 2:
                    dve.wait_ge(m["aT"], hd - 1)
                for tt, lo, hi in ((0, 0, P), (1, P, 3 * P)):
                    n = 48 + at + 2 * tt
                    second = mexp[hd % 2][:, 3 * P + lo:3 * P + hi]
                    step(dve.tensor_scalar(second, second, stat[:, n + 1:n + 2], None, ALU.mult))
                    ins = dve.scalar_tensor_tensor(ma[hd % 2][:, lo:hi], mexp[hd % 2][:, lo:hi], stat[:, n:n + 1], second,
                                                   ALU.mult, ALU.add)
                ins.then_inc(m["a"], 1)
                if hd + 2 < DA_HEADS:
                    scores(hd + 2)
                if hd == 2:
                    dve.wait_ge(m["sq"], 1)
                    for tt in range(TT):
                        ins = dve.tensor_reduce(conv_sum[:, 8 * tt:8 * tt + 8], proj[:, tt, CG:CG + D_CONV].rearrange(
                            "p (a n) -> p a n", n=D_CONV // 8), AX, ALU.add)
                    ins.then_inc(m["sum"], 1)
            dve.wait_ge(m["root"], 1)
            step(dve.reciprocal(conv_sum, conv_root))
            for tt in range(TT):
                v = proj[:, tt, XC:XC + D_CONV].rearrange("p (a n) -> p a n", n=D_CONV // 8)
                r = conv_sum[:, 8 * tt:8 * tt + 8].rearrange("p (a o) -> p a o", o=1).to_broadcast([P, 8, D_CONV // 8])
                step(dve.tensor_tensor(v, v, r, ALU.mult))
                dve.tensor_tensor(h[:, tt, 0:D_CONV], proj[:, tt, XC:XC + D_CONV], conv_gain, ALU.mult)
            for tt in range(TT):
                dve.wait_ge(m["sq"], tt + 2)
                dve.tensor_reduce(stat[:, 16 + 4 * tt:20 + 4 * tt],
                                  square[:, tt * D_CONV:(tt + 1) * D_CONV].rearrange("p (a n) -> p a n", n=DA_V), AX,
                                  ALU.add).then_inc(m["sum"], 1)
                dve.wait_ge(m["root"], tt + 2)
                step(dve.reciprocal(stat[:, 56 + 4 * tt:60 + 4 * tt], stat[:, 48 + 4 * tt:52 + 4 * tt]))
                for hd in range(DA_HEADS):
                    c = slice(hd * DA_V, (hd + 1) * DA_V)
                    n = 56 + 4 * tt + hd
                    ins = dve.scalar_tensor_tensor(h[:, tt, D_CONV + hd * DA_V:D_CONV + (hd + 1) * DA_V],
                                                   banks(6 + tt)[:, c], stat[:, n:n + 1], sub_gain, ALU.mult, ALU.mult)
                ins.then_inc(h_ready, 1)
            for tt in range(TT):
                turn_dve(dve, MIX_TURN, tt)
            out_dve(dve, "mix_out")

        def mix_pool(pool, step):
            pool.wait_ge(x_ready, X_COUNT[5] + 2)
            loads = [(conv_w, t["conv_w_2"][0].rearrange("k n -> (k n)")), (conv_gain, t["conv_out_g_2"][0]),
                     (qk_gain[:, 0:64], t["q_norm_g_2"][0]), (qk_gain[:, 64:128], t["k_norm_g_2"][0]),
                     (sub_gain, t["attn_subln_g_2"][0])]
            loads += [(lam_in[:, 64 * i:64 * i + 64], t[f"lambda_{n}_2"][0]) for i, n in enumerate(("q1", "q2", "k1", "k2"))]
            for dst, src in loads:
                pool.dma_start(dst, src.partition_broadcast(P)).then_inc(mix_loaded, 16)

        def mix_conv_pool(pool, step):
            pool.wait_ge(m["u"], 1)
            pool.dma_start(conv_rows[CONV_W - 1:, :].rearrange("(a p) n -> p a n", p=P), both(XC, D_CONV)).then_inc(m["stored"], 16)
            pool.wait_ge(m["stored"], 16)
            pool.wait_ge(m["zeros"], 16)
            for i in range(2):
                pool.dma_start(by_tile(shifted[i]), conv_rows[1 - i:1 - i + TOKENS, :].rearrange("(a p) n -> p a n", p=P)
                               ).then_inc(m["shifted"], 16)
            pool.wait_ge(m["shifted"], 32)
            pool.wait_ge(mix_loaded, 9 * 16)

            def weight(i):
                return conv_w[:, i * D_CONV:(i + 1) * D_CONV].rearrange("p (o n) -> p o n", o=1).to_broadcast([P, TT, D_CONV])
            acc = both(XC, D_CONV)
            pool.tensor_tensor(acc, acc, weight(2), ALU.mult)
            pool.tensor_tensor(by_tile(shifted[0]), by_tile(shifted[0]), weight(1), ALU.mult)
            step(pool.tensor_tensor(by_tile(shifted[1]), by_tile(shifted[1]), weight(0), ALU.mult))
            step(pool.tensor_tensor(acc, acc, by_tile(shifted[0]), ALU.add))
            step(pool.tensor_tensor(acc, acc, by_tile(shifted[1]), ALU.add))
            for c in in_copied:
                pool.wait_ge(c, 2 * IN_CHUNKS + 5)
            pool.tensor_tensor(acc, acc, both(BG, D_CONV), ALU.mult).then_inc(m["conv"], 1)

        pa = proj[:, :, :].rearrange("p a n -> p (a n)")
        taken = [0]

        def take(n, dt=F32):
            taken[0] += n
            assert taken[0] <= TT * GLA_COLS
            v = pa[:, taken[0] - n:taken[0]]
            return v if dt is F32 else v.bitcast(dt)
        iota = take(SLOTS)
        own_slot = take(1)
        logits = take(TT * (GROUPS + EXPERTS))
        group_pad, group_top, group_at = take(TT * 8), take(TT * 8), take(TT * 8, U32)
        group, group_off = take(TT), take(TT)
        group_exp, group_gate = take(TT * GROUPS), take(TT)
        group_hot, group_pick, mine = take(TT * GROUPS), take(TT * EXPERTS), take(TT * PER_GROUP)
        top, top_at, pick = take(TT * 8), take(TT * 8, U32), take(TT * 2)
        gap, gap_exp, share = take(TT), take(TT), take(2 * TT)
        takes, takes_any = take(2 * TT * EXPERTS), take(TT * EXPERTS)
        counts = take(3 * EXPERTS)
        count, rank = counts[:, 0:EXPERTS], counts[:, EXPERTS:]
        over, over_to, over_from, tile_base = take(EXPERTS), take(EXPERTS), take(EXPERTS), take(EXPERTS)
        tile_no, place_in, item = take(TT * EXPERTS), take(TT * EXPERTS), take(TT * EXPERTS)
        chosen = take(2 * TT * EXPERTS)
        item_of, place_of, slot_of = take(2 * TT), take(2 * TT), take(2 * TT)
        from_slot = take(2 * TT)
        share_slot = take(1)
        pick_by_k, picks = take(2 * TT * SLOTS), take(TT * SLOTS)
        slot_rows = take(2 * TOKENS)
        spread_part = take(2 * TOKENS)
        over_expert, over_test = take(MAX_OVER * EXPERTS), take(MAX_OVER * EXPERTS)
        plan_f, plan = take(1 + ITEMS), take(1 + ITEMS, I32)
        y_high, y_low = flat(hT_low)[:, 0:D], flat(hT_low)[:, D:2 * D]
        spread = flat(aT_low)[:, 0:TOKENS]
        ROUTE = banks(0)
        CNT = TT * (GROUPS + EXPERTS)
        SLOT_ROWS = banks(7)
        experts = [t[f"w_exp_{n}_2"].rearrange("o g e k n -> (o g e) k n") for n in ("gate", "up", "down")]
        XT = hT_high[:, :, 0:P]
        AT = flat(aT_high).rearrange("p (f n) -> p f n", f=4)
        gu_rest, gu_sum = [[scratch[:, i * D + c * BANK:i * D + (c + 1) * BANK] for c in range(2)] for i in range(2)]
        ITEM_Y = banks(6, 2)
        BODY = MOE + 4

        def k_of(v, k):
            return v[:, k * TT:(k + 1) * TT]

        def route_dve(dve, step):
            dve.wait_ge(e["tables"], 1)
            dve.memset(group_pad, -3e38)
            dve.memset(plan_f, 0.0)
            dve.wait_ge(e["logits"], 1)
            step(dve.tensor_copy(logits, ROUTE[:, 0:CNT]))
            lg = by_tile(logits)
            step(dve.tensor_copy(by_tile(group_pad)[:, :, 0:GROUPS], lg[:, :, 0:GROUPS]))
            for tt in range(TT):
                c = slice(8 * tt, 8 * tt + 8)
                step(dve.max(group_top[:, c], group_pad[:, c]))
                ins = dve.max_index(group_at[:, c], group_top[:, c], group_pad[:, c])
            step(ins)
            highest = by_tile(group_top)[:, :, 0:1]
            dve.tensor_tensor(by_tile(group_exp), lg[:, :, 0:GROUPS], highest.to_broadcast([P, TT, GROUPS]),
                              ALU.subtract).then_inc(e["gexp_in"], 1)
            step(dve.tensor_copy(group, by_tile(group_at)[:, :, 0]))
            dve.tensor_scalar(group_off, group, float(PER_GROUP), None, ALU.mult)
            for tt in range(TT):
                ins = dve.tensor_scalar(group_hot[:, GROUPS * tt:GROUPS * (tt + 1)], iota[:, 0:GROUPS], group[:, tt:tt + 1],
                                        None, ALU.is_equal)
            step(ins)
            for tt in range(TT):
                hot = group_hot[:, GROUPS * tt:GROUPS * (tt + 1)].rearrange("p (g o) -> p g o", o=1)
                ins = dve.tensor_tensor(group_pick[:, EXPERTS * tt:EXPERTS * (tt + 1)].rearrange("p (g e) -> p g e", g=GROUPS),
                                        lg[:, tt, GROUPS:].rearrange("p (g e) -> p g e", g=GROUPS),
                                        hot.to_broadcast([P, GROUPS, PER_GROUP]), ALU.mult)
            step(ins)
            step(dve.tensor_reduce(by_tile(mine), group_pick.rearrange("p (a g e) -> p a e g", a=TT, g=GROUPS), AX, ALU.add))
            for tt in range(TT):
                c = slice(8 * tt, 8 * tt + 8)
                step(dve.max(top[:, c], mine[:, c]))
                ins = dve.max_index(top_at[:, c], top[:, c], mine[:, c])
            step(ins)
            step(dve.tensor_copy(pick.rearrange("p (k a) -> p a k", k=2), by_tile(top_at)[:, :, 0:2]))
            dve.tensor_tensor(gap, by_tile(top)[:, :, 1], by_tile(top)[:, :, 0], ALU.subtract).then_inc(e["gexp_in"], 1)
            for k in range(2):
                ins = dve.tensor_tensor(k_of(pick, k), k_of(pick, k), group_off, ALU.add)
            step(ins)
            for k in range(2):
                for tt in range(TT):
                    q = k * TT + tt
                    ins = dve.tensor_scalar(takes[:, q * EXPERTS:(q + 1) * EXPERTS], iota[:, 0:EXPERTS], pick[:, q:q + 1], None,
                                            ALU.is_equal)
            step(ins)
            half = TT * EXPERTS
            dve.tensor_tensor(takes_any, takes[:, 0:half], takes[:, half:], ALU.add).then_inc(e["picked"], 1)
            dve.wait_ge(e["gexp"], 2)
            step(dve.tensor_reduce(group_gate, by_tile(group_exp), AX, ALU.add))
            dve.reciprocal(group_gate, group_gate)
            step(dve.tensor_scalar(share[:, 0:TT], gap_exp, 1.0, None, ALU.add))
            step(dve.reciprocal(share[:, 0:TT], share[:, 0:TT]))
            step(dve.tensor_tensor(share[:, 0:TT], share[:, 0:TT], group_gate, ALU.mult))
            step(dve.tensor_tensor(share[:, TT:], share[:, 0:TT], gap_exp, ALU.mult))
            dve.wait_ge(e["ranks"], 1)
            step(dve.tensor_copy(counts, ROUTE[:, CNT:CNT + 3 * EXPERTS]))
            for dst, src, edge in ((over, count, 0.5), (tile_no, rank, -0.5)):
                step(dve.tensor_scalar(dst, src, SLOTS + edge, None, ALU.is_gt))
                for n in range(2, MAX_TILES):
                    step(dve.scalar_tensor_tensor(dst, src, n * SLOTS + edge, dst, ALU.is_gt, ALU.add))
            step(dve.tensor_tensor_scan(over_to, ones[:, 0:EXPERTS], over, 0.0, ALU.mult, ALU.add))
            step(dve.tensor_tensor(over_from, over_to, over, ALU.subtract))
            dve.scalar_tensor_tensor(place_in, tile_no, -float(SLOTS), rank, ALU.mult, ALU.add)
            step(dve.tensor_tensor(tile_base, over_from, iota[:, 0:EXPERTS], ALU.subtract))
            step(dve.tensor_scalar(tile_base, tile_base, EXPERTS - 1.0, None, ALU.add))

            def per_tile(v):
                return v.rearrange("p (o n) -> p o n", o=1).to_broadcast([P, TT, EXPERTS])
            step(dve.tensor_tensor(by_tile(item), by_tile(tile_no), per_tile(tile_base), ALU.add))
            step(dve.scalar_tensor_tensor(item, tile_no, 0.0, item, ALU.is_gt, ALU.mult))
            step(dve.tensor_tensor(by_tile(item), by_tile(item), per_tile(iota[:, 0:EXPERTS]), ALU.add))
            for table, of in ((item, item_of), (place_in, place_of)):
                step(dve.tensor_tensor(chosen.rearrange("p (k n) -> p k n", k=2), takes.rearrange("p (k n) -> p k n", k=2),
                                       table.rearrange("p (o n) -> p o n", o=1).to_broadcast([P, 2, half]), ALU.mult))
                step(dve.tensor_reduce(of, chosen.rearrange("p (q n) -> p q n", n=EXPERTS), AX, ALU.add))
            step(dve.scalar_tensor_tensor(slot_of, item_of, float(SLOTS), place_of, ALU.mult, ALU.add))
            dve.tensor_scalar(from_slot, slot_of, float(SLOTS), None, ALU.add).then_inc(e["slots"], 1)
            n = MAX_OVER

            def grid(v):
                return v.rearrange("p (j n) -> p j n", j=n)

            def along(v):
                return v.rearrange("p (o n) -> p o n", o=1).to_broadcast([P, n, EXPERTS])
            j = iota[:, 0:n].rearrange("p (j o) -> p j o", o=1).to_broadcast([P, n, EXPERTS])
            dve.tensor_tensor(grid(over_expert), along(over_from), j, ALU.is_le)
            step(dve.tensor_tensor(grid(over_test), along(over_to), j, ALU.is_gt))
            step(dve.tensor_tensor(over_expert, over_expert, over_test, ALU.mult))
            step(dve.tensor_tensor(grid(over_expert), grid(over_expert), along(iota[:, 0:EXPERTS]), ALU.mult))
            dve.tensor_reduce(plan_f[:, 1 + EXPERTS:], grid(over_expert), AX, ALU.add)
            dve.tensor_copy(plan_f[:, 1:1 + EXPERTS], iota[:, 0:EXPERTS])
            step(dve.tensor_scalar(plan_f[:, 0:1], over_to[:, EXPERTS - 1:EXPERTS], EXPERTS - 1.0, None, ALU.add))
            dve.tensor_copy(plan, plan_f).then_inc(e["plan"], 1)

        def route_pe(pe):
            n = GROUPS + EXPERTS
            for tt in range(TT):
                turn_pe(pe, TURN_OF_NORM[8], "n8", tt)
                turned_tile(pe, TURN_OF_NORM[8], tt)
                for k in range(KD):
                    tok = slice(tt * P, (tt + 1) * P)
                    ins = product(pe, ROUTE[:, tt * n:(tt + 1) * n], hT_high[:, k, tok], hT_low[:, k, tok],
                                  router_high[:, k, :], router_low[:, k, :], start=tt == 0 and k == 0)
            ins.then_inc(e["logits"], 1)
            pe.wait_ge(e["picked"], 1)
            a = [takes_any[:, tt * EXPERTS:(tt + 1) * EXPERTS] for tt in range(TT)]
            for c, terms in enumerate((((ones[:, 0:P], a[0]), (ones[:, 0:P], a[1])), ((strict[:, :], a[0]),),
                                       ((ones[:, 0:P], a[0]), (strict[:, :], a[1])))):
                for i, (lhs, rhs) in enumerate(terms):
                    ins = pe.matmul(ROUTE[:, CNT + c * EXPERTS:CNT + (c + 1) * EXPERTS], lhs, rhs, start=c == 0 and i == 0,
                                    stop=i == len(terms) - 1, skip_group_check=True)
            ins.then_inc(e["ranks"], 1)

        def rounds(eng):
            eng.wait_ge(e["plan"], 1)
            return eng.value_load(plan[0:1, 0:1], min_val=EXPERTS - 1, max_val=ITEMS - 1)

        def expert_gate_up_loads(sp, p, r, expert):
            for j in range(4):
                piece_loads(sp, p + j, r, gate_up_parts(p + j, experts[0][expert], experts[1][expert], j % 2, (j // 2) * CHUNK))

        def expert_down_loads(sp, p, r, expert):
            for j in range(2):
                piece_loads(sp, p + j, r, down_parts(p + j, experts[2][expert], j * 2 * P))

        def moe_sp(sp):
            expert_gate_up_loads(sp, MOE, 0, 0)
            expert_gate_up_loads(sp, BODY, 0, 1)
            expert_down_loads(sp, BODY + 4, 0, 0)
            n = rounds(sp)

            def expert_of(i):
                return sp.value_load(plan[0:1, bass.ds(i + 1, 1)], min_val=0, max_val=EXPERTS - 1)
            with sp.Fori(1, n) as i:
                expert_gate_up_loads(sp, BODY, i * 2, expert_of(i + 1))
                expert_down_loads(sp, BODY + 4, i * 2, expert_of(i))
            expert_down_loads(sp, BODY, n * 2, expert_of(n))

        def moe_pool(pool, step):
            pool.wait_ge(x_ready, X_COUNT[8] + 2)
            pool.iota(iota, pattern=[[1, SLOTS]], base=0, channel_multiplier=0, allow_small_or_imprecise_dtypes=True)
            step(pool.iota(own_slot, pattern=[[0, 1]], base=-SLOTS, channel_multiplier=1,
                           allow_small_or_imprecise_dtypes=True))
            step(pool.tensor_scalar(own_slot[SLOTS:, :], own_slot[SLOTS:, :], -float(SLOTS), None, ALU.add))
            pool.sem_inc(e["tables"], 1)
            pool.wait_ge(e["logits"], 1)
            pool.memset(y_high.bitcast(F32), 0.0)
            pool.memset(y_low.bitcast(F32), 0.0).then_inc(e["y_low"], 1)
            pool.memset(spread.bitcast(F32), 0.0).then_inc(e["spreads"], 1)

            def pick(i):
                if not isinstance(i, int) or i:
                    pool.wait_ge(e["shares"], i)
                pool.sem_inc(e["pool_passed"], 1)
                pool.tensor_scalar(from_slot, from_slot, -float(SLOTS), None, ALU.add).then_inc(e["pick_parts"], 1)
                pool.wait_ge(e["pick_parts"], i * 2 + 1)
                pool.sem_inc(e["pool_passed"], 1)
                for q in range(2 * TT):
                    ins = pool.tensor_scalar(pick_by_k[:, q * SLOTS:(q + 1) * SLOTS], iota, from_slot[:, q:q + 1], None,
                                             ALU.is_equal)
                ins.then_inc(e["pick_parts"], 1)
                pool.wait_ge(e["pick_parts"], i * 2 + 2)
                pool.tensor_tensor(picks, pick_by_k[:, 0:TT * SLOTS], pick_by_k[:, TT * SLOTS:], ALU.add).then_inc(e["picks"], 1)

            def spread_of(i):
                pool.tensor_scalar(own_slot, own_slot, float(SLOTS), None, ALU.add).then_inc(e["spread_parts"], 1)
                pool.wait_ge(e["spread_parts"], i * 3 + 1)
                pool.sem_inc(e["pool_passed"], 1)
                for k in range(2):
                    pool.tensor_scalar(spread_part[:, k * TOKENS:(k + 1) * TOKENS], slot_rows[:, k * TOKENS:(k + 1) * TOKENS],
                                       own_slot, None, ALU.is_equal).then_inc(e["spread_parts"], 1)
                pool.wait_ge(e["scattered"], i + 1)
                pool.wait_ge(e["spread_parts"], i * 3 + 3)
                pool.tensor_tensor(spread, spread_part[:, 0:TOKENS], spread_part[:, TOKENS:],
                                          ALU.add).then_inc(e["spreads"], 1)

            pool.wait_ge(e["slots"], 1)
            pick(0)
            pick(1)
            pool.wait_ge(e["slot_rows_sb"], 1)
            n = rounds(pool)
            with pool.Fori(0, n) as i:
                pick(i + 2)
                spread_of(i)
            spread_of(n)

        def moe_pe(pe):
            route_pe(pe)

            def turn_rows(i):
                pe.wait_ge(e["picks"], i + 1)
                for k in range(KD):
                    for tt in range(TT):
                        ins = pe.matmul(GU[0][:, k * SLOTS:(k + 1) * SLOTS], h[:, tt, k * P:(k + 1) * P],
                                        picks[:, tt * SLOTS:(tt + 1) * SLOTS], start=tt == 0, stop=tt == TT - 1,
                                        skip_group_check=True)
                ins.then_inc(e["x_turned"], 1)

            def shares():
                for q in range(2 * TT):
                    ins = pe.matmul(GU[1][0:SLOTS, 4 * SLOTS:4 * SLOTS + 1], pick_by_k[:, q * SLOTS:(q + 1) * SLOTS],
                                    share[:, q:q + 1], start=q == 0, stop=q == 2 * TT - 1, skip_group_check=True)
                ins.then_inc(e["shares"], 1)

            def both_parts(out, lhs, rhs_high, rhs_low, start, stop):
                pe.matmul(out, lhs, rhs_high, start=start, stop=False, skip_group_check=True)
                return pe.matmul(out, lhs, rhs_low, start=False, stop=stop, skip_group_check=True)

            def gate_up(j, p, r):
                q = p + j
                pe.wait_ge(split, q + 1 + scales_with(r, 3))
                for k in range(4):
                    kk = 4 * (j % 2) + k
                    ins = both_parts(GU[j // 2], XT[:, kk, :], four_k(high, q)[:, k, :], four_k(low, q)[:, k, :],
                                     start=kk == 0, stop=kk == KD - 1)
                ins.then_inc(used, 1)

            def turn_inner(i):
                pe.wait_ge(e["act"], i * 2 + 2)
                pe.sem_inc(e["pe_passed"], 1)
                for f in range(4):
                    ins = pe.transpose(GU[1][:, f * SLOTS:(f + 1) * SLOTS], act_tok[0:SLOTS, f // 2, (f % 2) * P:(f % 2 + 1) * P],
                                       ident[0:SLOTS, 0:SLOTS])
                ins.then_inc(e["a_turned"], 1)

            def down(p, r):
                for j in range(2):
                    q = p + j
                    pe.wait_ge(split, q + 1 + scales_with(r, 3))
                    for k in range(2):
                        f = 2 * j + k
                        for c in range(2):
                            cols = slice(c * BANK, (c + 1) * BANK)
                            ins = both_parts(ITEM_Y[:, cols], AT[:, f, :], two_k(high, q)[:, k, cols],
                                             two_k(low, q)[:, k, cols], start=f == 0, stop=f == 3)
                    ins.then_inc(used, 1)

            def scatter(i):
                pe.wait_ge(e["y_low"], i + 1)
                pe.wait_ge(e["spreads"], i + 1)
                for part in (y_high, y_low):
                    for tt in range(TT):
                        for c in range(2):
                            cols = slice(c * BANK, (c + 1) * BANK)
                            ins = pe.matmul(Y[tt][:, cols], spread[:, tt * P:(tt + 1) * P], part[:, cols], start=False,
                                            stop=False, skip_group_check=True)
                ins.then_inc(e["scattered"], 1)

            pe.wait_ge(e["slots"], 1)
            for q in range(2 * TT):
                ins = pe.matmul(SLOT_ROWS[:, q * P:(q + 1) * P], slot_of[:, q:q + 1].to_broadcast([P, P]), ident[:, :],
                                start=True, stop=True, skip_group_check=True)
            ins.then_inc(e["slot_rows"], 1)
            pe.wait_ge(x_ready, X_COUNT[8] + 2)
            clear_Y(pe)
            turn_rows(0)
            shares()
            pe.wait_ge(e["x_low"], 1)
            for j in range(2):
                gate_up(j, MOE, 0)
            pe.wait_ge(e["share_sb"], 1)
            for j in range(2, 4):
                gate_up(j, MOE, 0)
            n = rounds(pe)
            pe.wait_ge(e["gu_sum"], 1)
            turn_rows(1)
            with pe.Fori(0, n) as i:
                pe.wait_ge(e["x_low"], i + 2)
                gate_up(0, BODY, i * 2)
                pe.wait_ge(e["act"], i * 2 + 2)
                shares()
                turn_inner(i)
                gate_up(1, BODY, i * 2)
                scatter(i)
                pe.wait_ge(e["a_low"], i + 1)
                pe.wait_ge(e["share_sb"], i + 2)
                for j in range(2, 4):
                    gate_up(j, BODY, i * 2)
                pe.wait_ge(e["gu_sum"], i * 2 + 3)
                turn_rows(i + 2)
                down(BODY + 4, i * 2)
            turn_inner(n)
            scatter(n)
            pe.wait_ge(e["a_low"], n + 1)
            down(BODY, n * 2)
            scatter(n + 1)

        slots_x = GU[0].rearrange("p (k n) -> p k n", n=SLOTS)
        slots_a = GU[1][:, 0:4 * SLOTS].rearrange("p (k n) -> p k n", n=SLOTS)

        def moe_act(act):
            act.wait_ge(e["gexp_in"], 1)
            act.activation(group_exp, group_exp, ACT.Exp).then_inc(e["gexp"], 1)
            act.wait_ge(e["gexp_in"], 2)
            act.activation(gap_exp, gap, ACT.Exp).then_inc(e["gexp"], 1)

            def inner_high(i):
                act.wait_ge(e["a_turned"], i + 1)
                act.activation(AT[:, :, 0:SLOTS], slots_a, ACT.Copy).then_inc(e["a_high"], 1)

            def rows_high(i):
                act.wait_ge(e["x_turned"], i + 1)
                act.activation(XT[:, :, 0:SLOTS], slots_x, ACT.Copy).then_inc(e["x_high"], 1)

            def rest(chunk, used_value):
                act.wait_ge(used, used_value)
                act.activation(gu_rest[chunk][0:SLOTS, :], GU[chunk][SLOTS:P, :], ACT.Copy).then_inc(e["gu_rest"], 1)

            def silu(chunk, count):
                act.wait_ge(e["gu_sum"], count)
                act.activation(gate[0:SLOTS, chunk, :], gu_sum[chunk][0:SLOTS, 0:CHUNK], ACT.Silu).then_inc(e["silu"], 1)

            def result(used_value):
                act.wait_ge(used, used_value)
                act.activation(y_high, ITEM_Y, ACT.Copy).then_inc(e["y_high"], 1)

            round_piece(act, MOE + 2)
            act.wait_ge(e["slot_rows"], 1)
            act.activation(slot_rows, SLOT_ROWS, ACT.Copy).then_inc(e["slot_rows_sb"], 1)
            rows_high(0)
            round_piece(act, MOE + 3)
            rest(0, MOE + 2)
            round_piece(act, BODY)
            silu(0, 1)
            round_piece(act, BODY + 1)
            rest(1, MOE + 4)
            rows_high(1)
            silu(1, 2)
            n = rounds(act)
            with act.Fori(0, n) as i:
                r = i * 2
                round_piece(act, BODY + 2, r)
                inner_high(i)
                round_piece(act, BODY + 3, r)
                rest(0, i * 6 + (BODY + 2))
                round_piece(act, BODY + 4, r)
                silu(0, i * 2 + 3)
                round_piece(act, BODY + 5, r)
                rest(1, i * 6 + (BODY + 4))
                round_piece(act, BODY + 6, r)
                rows_high(i + 2)
                silu(1, i * 2 + 4)
                round_piece(act, BODY + 7, r)
                result(i * 6 + (BODY + 6))
            inner_high(n)
            result(n * 6 + (BODY + 2))

        def moe_dve(dve, step):
            route_dve(dve, step)

            def inner_low(i):
                dve.wait_ge(e["a_high"], i + 1)
                dve.tensor_tensor(AT[:, :, SLOTS:P], slots_a, AT[:, :, 0:SLOTS].bitcast(F32),
                                  ALU.subtract).then_inc(e["a_low"], 1)

            def rows_low(i):
                dve.wait_ge(e["x_high"], i + 1)
                dve.tensor_tensor(XT[:, :, SLOTS:P], slots_x, XT[:, :, 0:SLOTS].bitcast(F32),
                                  ALU.subtract).then_inc(e["x_low"], 1)

            def share_out(count):
                dve.wait_ge(e["shares"], count)
                dve.tensor_copy(share_slot[0:SLOTS, :], GU[1][0:SLOTS, 4 * SLOTS:4 * SLOTS + 1]).then_inc(e["share_sb"], 1)

            def add_rest(chunk, count):
                dve.wait_ge(e["gu_rest"], count)
                dve.tensor_tensor(gu_sum[chunk][0:SLOTS, :], GU[chunk][0:SLOTS, :], gu_rest[chunk][0:SLOTS, :],
                                  ALU.add).then_inc(e["gu_sum"], 1)

            def inner(chunk, count):
                dve.wait_ge(e["silu"], count)
                if isinstance(count, int) and count == 1:
                    dve.wait_ge(e["share_sb"], 1)
                dve.scalar_tensor_tensor(act_tok[0:SLOTS, chunk, :], gate[0:SLOTS, chunk, :], share_slot[0:SLOTS, :],
                                         gu_sum[chunk][0:SLOTS, CHUNK:2 * CHUNK], ALU.mult, ALU.mult).then_inc(e["act"], 1)

            def result(i):
                dve.wait_ge(e["y_high"], i + 1)
                dve.tensor_tensor(y_low, ITEM_Y, y_high.bitcast(F32), ALU.subtract).then_inc(e["y_low"], 1)

            split_piece(dve, MOE + 2)
            rows_low(0)
            share_out(1)
            split_piece(dve, MOE + 3)
            add_rest(0, 1)
            split_piece(dve, BODY)
            inner(0, 1)
            split_piece(dve, BODY + 1)
            add_rest(1, 2)
            rows_low(1)
            inner(1, 2)
            n = rounds(dve)
            with dve.Fori(0, n) as i:
                r = i * 2
                split_piece(dve, BODY + 2, r)
                inner_low(i)
                share_out(i + 2)
                split_piece(dve, BODY + 3, r)
                add_rest(0, i * 2 + 3)
                split_piece(dve, BODY + 4, r)
                inner(0, i * 2 + 3)
                split_piece(dve, BODY + 5, r)
                add_rest(1, i * 2 + 4)
                split_piece(dve, BODY + 6, r)
                rows_low(i + 2)
                inner(1, i * 2 + 4)
                split_piece(dve, BODY + 7, r)
                result(i)
            inner_low(n)
            result(n)
            dve.wait_ge(e["scattered"], n + 2)
            for tt in range(TT):
                dve.tensor_tensor(x[:, tt, :], Y[tt], x[:, tt, :], ALU.add).then_inc(final, 1)

        block = ctx.enter_context(nc.Block())

        @block.sync
        def _(sp):
            def x_load(tt):
                sp.dma_start(x[:, tt, :], t["x"][0, tt * P:(tt + 1) * P, :]).then_inc(x_loaded[tt], 16)

            x_load(0)
            ffn_loads(sp, 0, lambda: x_load(1))
            in_loads(sp, "gla_in")
            out_loads(sp, "gla_out")
            ffn_loads(sp, 1)
            ffn_loads(sp, 2)
            in_loads(sp, "sb_in")
            out_loads(sp, "sb_out")
            ffn_loads(sp, 3)
            in_loads(sp, "mix_in")
            out_loads(sp, "mix_out")
            moe_sp(sp)
            for tt in range(TT):
                sp.wait_ge(final, tt + 1)
                sp.dma_start(out[0, tt * P:(tt + 1) * P, :], x[:, tt, :]).then_inc(stored_out, 16)
            sp.wait_ge(stored_out, TT * 16)

        @block.gpsimd
        def _(pool):
            n_steps = [0]

            def step(ins):
                n_steps[0] += 1
                ins.then_inc(pool_step, 1)
                pool.wait_ge(pool_step, n_steps[0])

            def select(v, op, fill, base, pattern, by_partition):
                step(nc.gpsimd.affine_select(out=v, in_=v, compare_op=op, fill=fill, base=base, pattern=pattern,
                                             channel_multiplier=by_partition))

            pool.memset(eps[:, :], EPS).then_inc(eps_set, 1)
            pool.dma_start(gain[:, 0, :], gains[0].partition_broadcast(P)).then_inc(gain_loaded[0], 16)
            pool.memset(zero_r[:, :].bitcast(F32), 0.0)
            step(pool.memset(ident[:, :], 0.0))
            select(ident[:, :], ALU.not_equal, 1.0, 0, [[-1, P]], 1)
            pool.sem_inc(consts, 1)
            pool.dma_start(gain[:, 1, :], gains[1].partition_broadcast(P)).then_inc(gain_loaded[1], 16)
            pool.dma_start(wgk2[:, :], t["gla_w_gk2"][0]).then_inc(small_loaded, 16)
            pool.dma_start(bgk[:, :], t["gla_b_gk"][0].rearrange("(a p) -> p a", p=P),
                           allow_slow_non_contiguous=True).then_inc(small_loaded, 16)
            pool.dma_start(gla_gain[:, :], t["gla_o_norm"][0].partition_broadcast(P)).then_inc(small_loaded, 16)
            pool.dma_start(gkw[:, :, :], t["gla_w_in"][0][:, IN_CHUNKS * BANK:].rearrange("(k p) n -> p k n", p=P)
                           ).then_inc(small_loaded, 16)
            for dst, src in ((router[:, :, 0:GROUPS], t["w_router_group_2"]), (router[:, :, GROUPS:], t["w_router_expert_2"])):
                pool.dma_start(dst, src[0].rearrange("(k p) n -> p k n", p=P)).then_inc(small_loaded, 16)
            pool.memset(ones[:, :], 1.0)
            pool.memset(suffix[:, :], 1.0)
            pool.memset(strict[:, :], 1.0)
            pool.memset(levels[:, :, :], 0.0)
            step(pool.memset(causal[:, :], 0.0))
            pool.dma_start(conv_rows[0:CONV_W - 1, :], zero_r[0:CONV_W - 1, :].bitcast(F32)).then_inc(m["zeros"], 16)
            select(suffix[:, :], ALU.is_ge, 0.0, 0, [[-1, P]], 1)
            select(strict[:, :], ALU.is_gt, 0.0, 0, [[1, P]], -1)
            for c in (0, 2):
                select(causal[:, c * P:(c + 1) * P], ALU.is_ge, NEG, 0, [[-1, P]], 1)
            for j, B in enumerate(LEVELS):
                n = P // (2 * B)
                late = levels[:, j, :].rearrange("p (m n) -> p m n", n=2 * B)[:, :, B:2 * B]
                step(pool.memset(late, 1.0))
                select(late, ALU.is_ge, 0.0, 0, [[-2 * B, n], [0, B]], 1)
                select(late, ALU.is_ge, 0.0, B - 1, [[2 * B, n], [0, B]], -1)
            pool.memset(gscore, 0.0).then_inc(consts, 1)
            for k in range(2, 9):
                if k - 2 != 6:
                    pool.wait_ge(h_ready, 2 * H_ORDER.index(f"n{k - 2}") + 2)
                else:
                    pool.wait_ge(x_ready, 14)
                pool.dma_start(gain[:, k % 2, :], gains[k].partition_broadcast(P)).then_inc(gain_loaded[k % 2], 16)
                if k == 7:
                    mix_pool(pool, step)
            mix_conv_pool(pool, step)
            moe_pool(pool, step)

        @block.scalar
        def _(act):
            n_steps = [0]

            def step(ins):
                n_steps[0] += 1
                ins.then_inc(act_step, 1)
                act.wait_ge(act_step, n_steps[0])

            load_roots(act)
            for tt in range(TT):
                root(act, 0, tt)
                round_piece(act, tt)
                turn_act(act, 0, tt)
            ffn_act(act, 0)
            norm_act(act, 1)
            act.wait_ge(small_loaded, 96)
            act.activation(flat(router_high), flat(router), ACT.Copy)
            act.activation(flat(gkw_high), flat(gkw), ACT.Copy).then_inc(small_high, 1)
            gla_act(act, step)
            norm_act(act, 2)
            ffn_act(act, 1)
            norm_act(act, 3)
            ffn_act(act, 2)
            norm_act(act, 4)
            sb_act(act, step)
            norm_act(act, 5)
            ffn_act(act, 3)
            norm_act(act, 6)
            mix_act(act, step)
            norm_act(act, 8)
            moe_act(act)

        @block.vector
        def _(dve):
            n_steps = [0]

            def step(ins):
                n_steps[0] += 1
                ins.then_inc(dve_step, 1)
                dve.wait_ge(dve_step, n_steps[0])

            for tt in range(TT):
                scale_x(dve, step, 0, tt)
                split_piece(dve, tt)
                turn_dve(dve, 0, tt)
            ffn_dve(dve, 0)
            norm_dve(dve, step, 1, 0.5, FIRST_PIECE["gla_in"] - 1)
            dve.wait_ge(small_high, 1)
            dve.tensor_tensor(flat(router_low), flat(router), flat(router_high).bitcast(F32), ALU.subtract)
            dve.tensor_tensor(flat(gkw_low), flat(gkw), flat(gkw_high).bitcast(F32), ALU.subtract).then_inc(small_low, 1)
            gla_dve(dve, step)
            norm_dve(dve, step, 2, 1.0, FIRST_PIECE["ffn1"] - 1)
            ffn_dve(dve, 1)
            norm_dve(dve, step, 3, 0.5, FIRST_PIECE["ffn2"] - 1)
            ffn_dve(dve, 2)
            norm_dve(dve, step, 4, 0.5, FIRST_PIECE["sb_in"] - 1)
            sb_dve(dve, step)
            norm_dve(dve, step, 5, 1.0, FIRST_PIECE["ffn3"] - 1)
            ffn_dve(dve, 3)
            norm_6_7_dve(dve, step, FIRST_PIECE["mix_in"] - 1)
            mix_dve(dve, step)
            norm_dve(dve, step, 8, 1.0, FIRST_PIECE["experts"] - 1)
            moe_dve(dve, step)

        @block.tensor
        def _(pe):
            ffn_pe(pe, 0, 0, "n0")
            gla_pe(pe)
            ffn_pe(pe, 1, TURN_OF_NORM[2], "n2")
            ffn_pe(pe, 2, TURN_OF_NORM[3], "n3")
            sb_pe(pe)
            ffn_pe(pe, 3, TURN_OF_NORM[5], "n5")
            mix_pe(pe)
            moe_pe(pe)


_INS = ["x", "ffn1_norm", "ffn1_w_gate", "ffn1_w_up", "ffn1_w_down", "mix_norm", "ffn2_norm", "ffn2_w_gate",
        "ffn2_w_up", "ffn2_w_down", "gla_w_in", "gla_w_gk2", "gla_b_gk", "gla_o_norm", "gla_w_out", "sb_w_in",
        "sb_w_out", "final_norm", "attn_norm_g_2", "w_in_2", "conv_w_2", "conv_out_g_2", "q_norm_g_2", "k_norm_g_2",
        "lambda_q1_2", "lambda_k1_2", "lambda_q2_2", "lambda_k2_2", "attn_subln_g_2", "w_out_2", "ffn_norm_g_2",
        "w_router_group_2", "w_router_expert_2", "w_exp_gate_2", "w_exp_up_2", "w_exp_down_2"]


def arrays_of(inputs):
    return {f"in_{n}": np.ascontiguousarray(inputs[n]) for n in _INS}


def declare_and_build(nc, arrays):
    t = {n: nc.dram_tensor(f"in_{n}", arrays[f"in_{n}"].shape, F32, kind="ExternalInput").ap() for n in _INS}
    out = nc.dram_tensor("out", (1, TOKENS, D), F32, kind="ExternalOutput").ap()
    build(nc, t, out)


def kernel(**inputs):
    import concourse.bacc as bacc
    from concourse.bass_utils import run_bass_kernel_spmd

    nc = bacc.Bacc("TRN2", target_bir_lowering=False, num_devices=1)
    arrays = arrays_of(inputs)
    declare_and_build(nc, arrays)
    result = run_bass_kernel_spmd(nc, [arrays], core_ids=[0])
    return result.results[0]["out"]
```
